# Optimizing a Trainium2 kernel written in Bass

```python
import math
import jax, jax.numpy as jnp
from jax import lax
import numpy as np

D_MODEL = 1024
BATCH = 1
SEQ = 256
DEPTH = 2

N_MIXERS = 2
N_HEADS = 16
HEAD_DIM = 64
ATTN_WIDTH = N_HEADS * HEAD_DIM
FOX_BLOCK = 128
FOX_IN = 4 * ATTN_WIDTH + N_HEADS
NSA_GROUPS = 4
NSA_REP = N_HEADS // NSA_GROUPS
KV_WIDTH = NSA_GROUPS * HEAD_DIM
CMP_LEN = 32
CMP_STRIDE = 16
CMP_HIDDEN = 256
SEL_LEN = 64
N_SELECT = 8
SEL_QCHUNK = 32
WINDOW = 512
WIN_BLOCK = 128
N_BRANCH = 3
NSA_IN = 2 * ATTN_WIDTH + 6 * KV_WIDTH + N_BRANCH * N_HEADS
ROPE_THETA = 500000.0
ROPE_DIM = HEAD_DIM // 4
NORM_EPS = 1e-6
NEG = -1e30
FORCE = 1e6
N_FOX = (DEPTH + 1) // 2
N_NSA = DEPTH // 2


def rmsnorm(x, g):
    xf = x.astype(jnp.float32)
    y = xf * lax.rsqrt(jnp.mean(xf * xf, axis=-1, keepdims=True) + NORM_EPS)
    return (y * g.astype(jnp.float32)).astype(x.dtype)

def rope_partial(x, pos):
    half = ROPE_DIM // 2
    inv_freq = jnp.power(ROPE_THETA, -jnp.arange(half, dtype=jnp.float32) * (2.0 / ROPE_DIM))
    ang = pos.astype(jnp.float32)[:, None] * inv_freq[None, :]
    shape = (pos.shape[0],) + (1,) * (x.ndim - 3) + (half,)
    cos = jnp.cos(ang).reshape(shape)
    sin = jnp.sin(ang).reshape(shape)
    xr = x[..., :ROPE_DIM].astype(jnp.float32)
    x1, x2 = xr[..., :half], xr[..., half:]
    rot = jnp.concatenate([x1 * cos - x2 * sin, x1 * sin + x2 * cos], axis=-1).astype(x.dtype)
    return jnp.concatenate([rot, x[..., ROPE_DIM:]], axis=-1)

def fox_mixer(h, w_in, b_f, w_out):
    B, S, _ = h.shape
    W = ATTN_WIDTH
    proj = h @ w_in
    q, k, v, f, z = jnp.split(proj, [W, 2 * W, 3 * W, 3 * W + N_HEADS], axis=-1)
    q = q.reshape(B, S, N_HEADS, HEAD_DIM)
    k = k.reshape(B, S, N_HEADS, HEAD_DIM)
    v = v.reshape(B, S, N_HEADS, HEAD_DIM)
    log_f = jax.nn.log_sigmoid(f.astype(jnp.float32) + b_f.astype(jnp.float32))
    c = jnp.cumsum(log_f, axis=1).transpose(0, 2, 1)
    scale = HEAD_DIM ** -0.5
    outs = []
    for qb in range(S // FOX_BLOCK):
        s0, s1 = qb * FOX_BLOCK, (qb + 1) * FOX_BLOCK
        logits = jnp.einsum('bqhd,bkhd->bhqk', q[:, s0:s1], k[:, :s1]).astype(jnp.float32) * scale
        logits = logits + c[:, :, s0:s1, None] - c[:, :, None, :s1]
        tq = jnp.arange(s0, s1)
        tk = jnp.arange(s1)
        logits = jnp.where(tk[None, :] <= tq[:, None], logits, NEG)
        p = jax.nn.softmax(logits, axis=-1).astype(v.dtype)
        outs.append(jnp.einsum('bhqk,bkhd->bqhd', p, v[:, :s1]))
    o = jnp.concatenate(outs, axis=1).reshape(B, S, W)
    return (o * jax.nn.silu(z)) @ w_out

def compress_blocks(x, pe, w1, w2):
    B, S, G, D = x.shape
    n_chunk = S // CMP_STRIDE
    r = CMP_LEN // CMP_STRIDE
    n_cmp = n_chunk - r + 1
    ch = x.reshape(B, n_chunk, CMP_STRIDE, G, D)
    blk = jnp.concatenate([ch[:, j:j + n_cmp] for j in range(r)], axis=2)
    blk = blk + pe[None, None, :, None, :]
    blk = blk.transpose(0, 1, 3, 2, 4).reshape(B, n_cmp, G, CMP_LEN * D)
    return jax.nn.silu(blk @ w1) @ w2

def nsa_mixer(h, w_in, pe_k, w_ck1, w_ck2, pe_v, w_cv1, w_cv2, w_out):
    B, S, _ = h.shape
    G, R, D, W = NSA_GROUPS, NSA_REP, HEAD_DIM, ATTN_WIDTH
    proj = h @ w_in
    offs = [W + i * KV_WIDTH for i in range(1, 7)] + [W + 6 * KV_WIDTH + N_BRANCH * N_HEADS]
    q, kc_raw, vc_raw, ks_raw, vs_raw, kw_raw, vw_raw, gate_raw, z = jnp.split(proj, [W] + offs, axis=-1)
    pos = jnp.arange(S)
    q = rope_partial(q.reshape(B, S, G, R, D), pos)
    scale = D ** -0.5

    kc = compress_blocks(kc_raw.reshape(B, S, G, D), pe_k, w_ck1, w_ck2)
    vc = compress_blocks(vc_raw.reshape(B, S, G, D), pe_v, w_cv1, w_cv2)
    n_cmp = kc.shape[1]
    cmp_end = jnp.arange(n_cmp) * CMP_STRIDE + CMP_LEN - 1
    kc = rope_partial(kc, cmp_end)
    lg_c = jnp.einsum('bsgrd,bcgd->bgrsc', q, kc).astype(jnp.float32) * scale
    mask_c = cmp_end[None, :] <= pos[:, None]
    p_c = jax.nn.softmax(jnp.where(mask_c, lg_c, NEG), axis=-1)
    p_c = jnp.where(mask_c, p_c, 0.0)
    o_c = jnp.einsum('bgrsc,bcgd->bsgrd', p_c.astype(vc.dtype), vc)

    n_sel_blk = S // SEL_LEN
    n_sel = min(N_SELECT, n_sel_blk)
    ci = jnp.arange(n_cmp) * CMP_STRIDE
    sj = jnp.arange(n_sel_blk) * SEL_LEN
    overlap = ((ci[:, None] < sj[None, :] + SEL_LEN) & (ci[:, None] + CMP_LEN > sj[None, :])).astype(jnp.float32)
    imp = jnp.einsum('bgsc,cj->bgsj', p_c.sum(axis=2), overlap)
    cur = pos // SEL_LEN
    blk_ids = jnp.arange(n_sel_blk)
    forced = (blk_ids[None, :] == 0) | (blk_ids[None, :] == cur[:, None]) | (blk_ids[None, :] == cur[:, None] - 1)
    causal = blk_ids[None, :] <= cur[:, None]
    imp = jnp.where(forced, FORCE, jnp.where(causal, imp, -1.0))
    _, idx = lax.top_k(imp, n_sel)

    ks = rope_partial(ks_raw.reshape(B, S, G, D), pos)
    vs = vs_raw.reshape(B, S, G, D)
    k_blocks = ks.reshape(B, n_sel_blk, SEL_LEN, G, D).transpose(0, 3, 1, 2, 4)
    v_blocks = vs.reshape(B, n_sel_blk, SEL_LEN, G, D).transpose(0, 3, 1, 2, 4)
    n_qc = S // SEL_QCHUNK
    q_ch = q.reshape(B, n_qc, SEL_QCHUNK, G, R, D).transpose(1, 0, 2, 3, 4, 5)
    idx_ch = idx.transpose(0, 2, 1, 3).reshape(B, n_qc, SEL_QCHUNK, G, n_sel).transpose(1, 0, 2, 3, 4)
    pos_ch = pos.reshape(n_qc, SEL_QCHUNK)
    bi = jnp.arange(B)[:, None, None, None]
    gi = jnp.arange(G)[None, None, :, None]
    l_off = jnp.arange(SEL_LEN)

    def sel_chunk(args):
        qc, ic, tc = args
        kb = k_blocks[bi, gi, ic]
        vb = v_blocks[bi, gi, ic]
        lg = jnp.einsum('btgrd,btgnld->btgrnl', qc, kb).astype(jnp.float32) * scale
        kpos = ic[..., None] * SEL_LEN + l_off
        m = (kpos <= tc[None, :, None, None, None])[:, :, :, None]
        lg = jnp.where(m, lg, NEG)
        p = jax.nn.softmax(lg.reshape(B, SEL_QCHUNK, G, R, n_sel * SEL_LEN), axis=-1)
        p = p.reshape(B, SEL_QCHUNK, G, R, n_sel, SEL_LEN).astype(vb.dtype)
        return jnp.einsum('btgrnl,btgnld->btgrd', p, vb)

    o_s = lax.map(sel_chunk, (q_ch, idx_ch, pos_ch))
    o_s = o_s.transpose(1, 0, 2, 3, 4, 5).reshape(B, S, G, R, D)

    kw = rope_partial(kw_raw.reshape(B, S, G, D), pos)
    vw = vw_raw.reshape(B, S, G, D)
    n_qb = S // WIN_BLOCK
    n_wb = -(-WINDOW // WIN_BLOCK)
    pad = n_wb * WIN_BLOCK
    band = (n_wb + 1) * WIN_BLOCK
    kpad = jnp.pad(kw, ((0, 0), (pad, 0), (0, 0), (0, 0))).reshape(B, n_qb + n_wb, WIN_BLOCK, G, D)
    vpad = jnp.pad(vw, ((0, 0), (pad, 0), (0, 0), (0, 0))).reshape(B, n_qb + n_wb, WIN_BLOCK, G, D)
    k_band = jnp.concatenate([kpad[:, j:j + n_qb] for j in range(n_wb + 1)], axis=2)
    v_band = jnp.concatenate([vpad[:, j:j + n_qb] for j in range(n_wb + 1)], axis=2)
    qb = q.reshape(B, n_qb, WIN_BLOCK, G, R, D)
    lg_w = jnp.einsum('bnqgrd,bnkgd->bngrqk', qb, k_band).astype(jnp.float32) * scale
    tq = pos.reshape(n_qb, WIN_BLOCK)
    tk = jnp.arange(n_qb)[:, None] * WIN_BLOCK - pad + jnp.arange(band)[None, :]
    m_w = (tk[:, None, :] <= tq[:, :, None]) & (tk[:, None, :] > tq[:, :, None] - WINDOW) & (tk[:, None, :] >= 0)
    lg_w = jnp.where(m_w[None, :, None, None], lg_w, NEG)
    p_w = jax.nn.softmax(lg_w, axis=-1).astype(v_band.dtype)
    o_w = jnp.einsum('bngrqk,bnkgd->bnqgrd', p_w, v_band).reshape(B, S, G, R, D)

    g = jax.nn.sigmoid(gate_raw.astype(jnp.float32)).reshape(B, S, G, R, N_BRANCH).astype(o_c.dtype)
    o = g[..., 0:1] * o_c + g[..., 1:2] * o_s + g[..., 2:3] * o_w
    return (o.reshape(B, S, W) * jax.nn.silu(z)) @ w_out

def first_inputs(seed: int = 0) -> dict:
    key = jax.random.key(seed)
    ks = jax.random.split(key, 16)
    f32 = jnp.float32
    W = ATTN_WIDTH
    cdim = CMP_LEN * HEAD_DIM
    return {
        "x": jax.random.normal(ks[0], (BATCH, SEQ, D_MODEL), f32),
        "norm_g": 1.0 + 0.1 * jax.random.normal(ks[1], (DEPTH, D_MODEL), f32),
        "fox_w_in": jax.random.normal(ks[2], (N_FOX, D_MODEL, FOX_IN), f32) * D_MODEL ** -0.5,
        "fox_b_f": jax.random.uniform(ks[3], (N_FOX, N_HEADS), f32, 1.0, 6.0),
        "fox_w_out": jax.random.normal(ks[4], (N_FOX, W, D_MODEL), f32) * W ** -0.5,
        "nsa_w_in": jax.random.normal(ks[5], (N_NSA, D_MODEL, NSA_IN), f32) * D_MODEL ** -0.5,
        "nsa_pe_k": 0.1 * jax.random.normal(ks[6], (N_NSA, CMP_LEN, HEAD_DIM), f32),
        "nsa_w_ck1": jax.random.normal(ks[7], (N_NSA, cdim, CMP_HIDDEN), f32) * cdim ** -0.5,
        "nsa_w_ck2": jax.random.normal(ks[8], (N_NSA, CMP_HIDDEN, HEAD_DIM), f32) * CMP_HIDDEN ** -0.5,
        "nsa_pe_v": 0.1 * jax.random.normal(ks[9], (N_NSA, CMP_LEN, HEAD_DIM), f32),
        "nsa_w_cv1": jax.random.normal(ks[10], (N_NSA, cdim, CMP_HIDDEN), f32) * cdim ** -0.5,
        "nsa_w_cv2": jax.random.normal(ks[11], (N_NSA, CMP_HIDDEN, HEAD_DIM), f32) * CMP_HIDDEN ** -0.5,
        "nsa_w_out": jax.random.normal(ks[12], (N_NSA, W, D_MODEL), f32) * W ** -0.5,
        "final_g": 1.0 + 0.1 * jax.random.normal(ks[13], (D_MODEL,), f32),
    }

def first_block(x, norm_g, fox_w_in, fox_b_f, fox_w_out, nsa_w_in, nsa_pe_k, nsa_w_ck1, nsa_w_ck2,
              nsa_pe_v, nsa_w_cv1, nsa_w_cv2, nsa_w_out, final_g):
    for i in range(DEPTH):
        h = rmsnorm(x, norm_g[i])
        j = i // N_MIXERS
        if i % N_MIXERS == 0:
            y = fox_mixer(h, fox_w_in[j], fox_b_f[j], fox_w_out[j])
        else:
            y = nsa_mixer(h, nsa_w_in[j], nsa_pe_k[j], nsa_w_ck1[j], nsa_w_ck2[j],
                          nsa_pe_v[j], nsa_w_cv1[j], nsa_w_cv2[j], nsa_w_out[j])
        x = x + y
    return rmsnorm(x, final_g)


N_HGRN_LAYERS = (DEPTH + 1) // 2
N_MLA_LAYERS = DEPTH // 2
RMS_EPS = 1e-6

HGRN_EXPAND = 128
HGRN_HEADS = D_MODEL // HGRN_EXPAND
HGRN_VDIM = D_MODEL // HGRN_HEADS
HGRN_CHUNK = 64

MLA_HEADS = D_MODEL // 128
MLA_NOPE = 128
MLA_ROPE = 64
MLA_QK_HEAD = MLA_NOPE + MLA_ROPE
MLA_V_HEAD = 128
MLA_Q_LORA = D_MODEL // 4
MLA_KV_LORA = D_MODEL // 4
ROPE_THETA_2 = 10000.0
Q_BLOCK = 128

D_FF = 2816
FFN_CONV = 3


def _rmsnorm(x, gain):
    xf = x.astype(jnp.float32)
    y = xf * lax.rsqrt(jnp.mean(xf * xf, axis=-1, keepdims=True) + RMS_EPS)
    return (y * gain.astype(jnp.float32)).astype(x.dtype)

def _chunk_gated_recurrence(q, k, v, log_f):
    B, S, H, Dk = q.shape
    Dv = v.shape[-1]
    C = HGRN_CHUNK
    N = S // C

    def to_chunks(t):
        return t.astype(jnp.float32).reshape(B, N, C, H, t.shape[-1]).transpose(1, 0, 3, 2, 4)

    causal = jnp.tril(jnp.ones((C, C), dtype=bool))[:, :, None]

    def step(state, inp):
        qc, kc, vc, gc = inp
        G = jnp.cumsum(gc, axis=2)
        o_inter = jnp.einsum("bhtd,bhde->bhte", qc * jnp.exp(G), state)
        diff = G[:, :, :, None, :] - G[:, :, None, :, :]
        decay = jnp.where(causal, jnp.exp(jnp.where(causal, diff, 0.0)), 0.0)
        scores = jnp.einsum("bhtd,bhsd,bhtsd->bhts", qc, kc, decay)
        o_intra = jnp.einsum("bhts,bhse->bhte", scores, vc)
        G_last = G[:, :, -1:, :]
        new_state = state * jnp.exp(G_last[:, :, 0, :, None]) + jnp.einsum(
            "bhsd,bhse->bhde", kc * jnp.exp(G_last - G), vc)
        return new_state, o_inter + o_intra

    state0 = jnp.zeros((B, H, Dk, Dv), jnp.float32)
    _, o = lax.scan(step, state0, (to_chunks(q), to_chunks(k), to_chunks(v), to_chunks(log_f)))
    return o.transpose(1, 0, 3, 2, 4).reshape(B, S, H, Dv)

def _hgrn2_mixer(h, w_in, lower_bound, out_norm, w_out):
    B, S, _ = h.shape
    q, f, i, g = jnp.split(h @ w_in, 4, axis=-1)

    def heads(t):
        return t.reshape(B, S, HGRN_HEADS, -1)

    lb = lower_bound.astype(jnp.float32)
    forget = lb + (1.0 - lb) * jax.nn.sigmoid(f.astype(jnp.float32))
    key_in = 1.0 - forget
    log_f = jnp.log(forget)
    o = _chunk_gated_recurrence(heads(jax.nn.silu(q)), heads(key_in), heads(i), heads(log_f))
    o = _rmsnorm(o, out_norm) * jax.nn.silu(heads(g.astype(jnp.float32)))
    return o.reshape(B, S, D_MODEL).astype(h.dtype) @ w_out

def _rope_tail(x, cos, sin):
    x_nope, x1, x2 = jnp.split(x, [MLA_NOPE, MLA_NOPE + MLA_ROPE // 2], axis=-1)
    xf1 = x1.astype(jnp.float32)
    xf2 = x2.astype(jnp.float32)
    rot = jnp.concatenate([xf1 * cos - xf2 * sin, xf2 * cos + xf1 * sin], axis=-1).astype(x.dtype)
    return jnp.concatenate([x_nope, rot], axis=-1)

def _causal_block_attention(q, k, v):
    B, S, H, Dqk = q.shape
    nb = S // Q_BLOCK
    scale = Dqk ** -0.5
    q_blocks = q.reshape(B, nb, Q_BLOCK, H, Dqk).transpose(1, 0, 3, 2, 4)
    k_t = k.transpose(0, 2, 1, 3)
    v_t = v.transpose(0, 2, 1, 3)
    key_pos = jnp.arange(S)

    def attend(args):
        q_blk, blk = args
        s = jnp.einsum("bhqd,bhkd->bhqk", q_blk, k_t).astype(jnp.float32) * scale
        q_pos = blk * Q_BLOCK + jnp.arange(Q_BLOCK)
        s = jnp.where(key_pos[None, :] <= q_pos[:, None], s, -jnp.inf)
        p = jax.nn.softmax(s, axis=-1).astype(v_t.dtype)
        return jnp.einsum("bhqk,bhkv->bhqv", p, v_t)

    o = lax.map(attend, (q_blocks, jnp.arange(nb)))
    return o.transpose(1, 0, 3, 2, 4).reshape(B, S, H, -1)

def _mla_mixer(h, cos, sin, w_in, q_a_norm, w_q_up, kv_a_norm, w_kv_up, q_norm, k_norm, w_out):
    B, S, _ = h.shape
    c_q, c_kv, k_rope = jnp.split(h @ w_in, [MLA_Q_LORA, MLA_Q_LORA + MLA_KV_LORA], axis=-1)
    q = (_rmsnorm(c_q, q_a_norm) @ w_q_up).reshape(B, S, MLA_HEADS, MLA_QK_HEAD)
    kv = (_rmsnorm(c_kv, kv_a_norm) @ w_kv_up).reshape(B, S, MLA_HEADS, MLA_NOPE + MLA_V_HEAD)
    k_nope, v = jnp.split(kv, [MLA_NOPE], axis=-1)
    k = jnp.concatenate(
        [k_nope, jnp.broadcast_to(k_rope[:, :, None, :], (B, S, MLA_HEADS, MLA_ROPE))], axis=-1)
    q = _rope_tail(_rmsnorm(q, q_norm), cos, sin)
    k = _rope_tail(_rmsnorm(k, k_norm), cos, sin)
    o = _causal_block_attention(q, k, v)
    return o.reshape(B, S, MLA_HEADS * MLA_V_HEAD) @ w_out

def _conv_ffn(h, w_up, conv_w, conv_b, w_down):
    S = h.shape[1]
    u = h @ w_up
    u_pad = jnp.pad(u, ((0, 0), (FFN_CONV - 1, 0), (0, 0)))
    y = conv_b.astype(u.dtype)
    for j in range(FFN_CONV):
        y = y + u_pad[:, j:j + S, :] * conv_w[j]
    gate, up = jnp.split(y, 2, axis=-1)
    return (jax.nn.silu(gate) * up) @ w_down

def second_inputs(seed: int = 0) -> dict:
    key = jax.random.key(seed)
    ks = iter(jax.random.split(key, 32))

    def nrm(shape, scale):
        return jax.random.normal(next(ks), shape, jnp.float32) * scale

    def gain(shape):
        return 1.0 + 0.02 * jax.random.normal(next(ks), shape, jnp.float32)

    D = D_MODEL
    x = jax.random.normal(next(ks), (BATCH, SEQ, D), jnp.float32)
    offsets = jax.random.randint(next(ks), (BATCH, 1), 0, 4096, dtype=jnp.int32)
    positions = offsets + jnp.arange(SEQ, dtype=jnp.int32)[None, :]
    return {
        "x": x,
        "positions": positions,
        "norm_mix": gain((DEPTH, D)),
        "norm_ffn": gain((DEPTH, D)),
        "hgrn_w_in": nrm((N_HGRN_LAYERS, D, 4 * D), D ** -0.5),
        "hgrn_lower_bounds": nrm((N_HGRN_LAYERS, HGRN_HEADS * HGRN_EXPAND), 0.1),
        "hgrn_out_norm": gain((N_HGRN_LAYERS, HGRN_VDIM)),
        "hgrn_w_out": nrm((N_HGRN_LAYERS, D, D), D ** -0.5),
        "mla_w_in": nrm((N_MLA_LAYERS, D, MLA_Q_LORA + MLA_KV_LORA + MLA_ROPE), D ** -0.5),
        "mla_q_a_norm": gain((N_MLA_LAYERS, MLA_Q_LORA)),
        "mla_w_q_up": nrm((N_MLA_LAYERS, MLA_Q_LORA, MLA_HEADS * MLA_QK_HEAD), MLA_Q_LORA ** -0.5),
        "mla_kv_a_norm": gain((N_MLA_LAYERS, MLA_KV_LORA)),
        "mla_w_kv_up": nrm((N_MLA_LAYERS, MLA_KV_LORA, MLA_HEADS * (MLA_NOPE + MLA_V_HEAD)), MLA_KV_LORA ** -0.5),
        "mla_q_norm": gain((N_MLA_LAYERS, MLA_QK_HEAD)),
        "mla_k_norm": gain((N_MLA_LAYERS, MLA_QK_HEAD)),
        "mla_w_out": nrm((N_MLA_LAYERS, MLA_HEADS * MLA_V_HEAD, D), (MLA_HEADS * MLA_V_HEAD) ** -0.5),
        "ffn_w_up": nrm((DEPTH, D, 2 * D_FF), D ** -0.5),
        "ffn_conv_w": nrm((DEPTH, FFN_CONV, 2 * D_FF), FFN_CONV ** -0.5),
        "ffn_conv_b": nrm((DEPTH, 2 * D_FF), 0.01),
        "ffn_w_down": nrm((DEPTH, D_FF, D), D_FF ** -0.5),
    }

def second_block(x, positions, norm_mix, norm_ffn, hgrn_w_in, hgrn_lower_bounds, hgrn_out_norm, hgrn_w_out,
              mla_w_in, mla_q_a_norm, mla_w_q_up, mla_kv_a_norm, mla_w_kv_up, mla_q_norm, mla_k_norm,
              mla_w_out, ffn_w_up, ffn_conv_w, ffn_conv_b, ffn_w_down):
    lb_soft = jax.nn.softmax(hgrn_lower_bounds.astype(jnp.float32), axis=0)
    lower_bounds = jnp.cumsum(lb_soft, axis=0) - lb_soft[0:1]
    inv_freq = ROPE_THETA_2 ** (-jnp.arange(0, MLA_ROPE, 2, dtype=jnp.float32) / MLA_ROPE)
    ang = positions.astype(jnp.float32)[..., None] * inv_freq
    cos = jnp.cos(ang)[:, :, None, :]
    sin = jnp.sin(ang)[:, :, None, :]

    for layer in range(DEPTH):
        h = _rmsnorm(x, norm_mix[layer])
        j = layer // N_MIXERS
        if layer % N_MIXERS == 0:
            y = _hgrn2_mixer(h, hgrn_w_in[j], lower_bounds[j], hgrn_out_norm[j], hgrn_w_out[j])
        else:
            y = _mla_mixer(h, cos, sin, mla_w_in[j], mla_q_a_norm[j], mla_w_q_up[j], mla_kv_a_norm[j],
                           mla_w_kv_up[j], mla_q_norm[j], mla_k_norm[j], mla_w_out[j])
        x = x + y
        h = _rmsnorm(x, norm_ffn[layer])
        x = x + _conv_ffn(h, ffn_w_up[layer], ffn_conv_w[layer], ffn_conv_b[layer], ffn_w_down[layer])
    return x


def setup_inputs(seed=0):
    out = dict(first_inputs(seed))
    for name, value in second_inputs(seed + 1).items():
        if name != "x":
            out[name + "_2"] = value
    return out


def reference(
    x, norm_g, fox_w_in, fox_b_f, fox_w_out, nsa_w_in, nsa_pe_k, nsa_w_ck1, nsa_w_ck2, nsa_pe_v,
    nsa_w_cv1, nsa_w_cv2, nsa_w_out, final_g, positions_2, norm_mix_2, norm_ffn_2, hgrn_w_in_2,
    hgrn_lower_bounds_2, hgrn_out_norm_2, hgrn_w_out_2, mla_w_in_2, mla_q_a_norm_2,
    mla_w_q_up_2, mla_kv_a_norm_2, mla_w_kv_up_2, mla_q_norm_2, mla_k_norm_2, mla_w_out_2,
    ffn_w_up_2, ffn_conv_w_2, ffn_conv_b_2, ffn_w_down_2,
):
    x = first_block(
        x, norm_g, fox_w_in, fox_b_f, fox_w_out, nsa_w_in, nsa_pe_k, nsa_w_ck1, nsa_w_ck2,
        nsa_pe_v, nsa_w_cv1, nsa_w_cv2, nsa_w_out, final_g,
    )
    return second_block(
        x, positions_2, norm_mix_2, norm_ffn_2, hgrn_w_in_2, hgrn_lower_bounds_2,
        hgrn_out_norm_2, hgrn_w_out_2, mla_w_in_2, mla_q_a_norm_2, mla_w_q_up_2,
        mla_kv_a_norm_2, mla_w_kv_up_2, mla_q_norm_2, mla_k_norm_2, mla_w_out_2, ffn_w_up_2,
        ffn_conv_w_2, ffn_conv_b_2, ffn_w_down_2,
    )


_drawn_inputs = setup_inputs


def setup_inputs(seed=0):
    import zlib

    import numpy as np

    out = dict(_drawn_inputs(seed))
    spreads = {}
    factors = {'nsa_pe_k': 8.0,
     'norm_mix_2': 3.075,
     'norm_ffn_2': 2.983,
     'hgrn_out_norm_2': 4.329,
     'mla_q_a_norm_2': 8.0,
     'mla_kv_a_norm_2': 8.0,
     'mla_q_norm_2': 8.0,
     'mla_k_norm_2': 8.0,
     'ffn_conv_b_2': 5.933}
    for name, (base, spread) in spreads.items():
        noise = np.random.default_rng([zlib.crc32(name.encode()), seed]).standard_normal(out[name].shape)
        drawn = base * np.exp(spread * noise) if base else spread * noise
        out[name] = __import__('jax').numpy.asarray(drawn.astype(out[name].dtype))
    for name, factor in factors.items():
        out[name] = (out[name] * factor).astype(out[name].dtype)
    return out
```

```python
from contextlib import ExitStack

import numpy as np

import concourse.bass as bass
from concourse import mybir

F32 = mybir.dt.float32
F32R = mybir.dt.float32r
BF16 = mybir.dt.bfloat16
I32 = mybir.dt.int32
ALU = mybir.AluOpType
ACT = mybir.ActivationFunctionType
AX = mybir.AxisListType

P = 128
D = 1024
S = 256
TT = S // P
DC = D // P
EPS = 1e-6
BIG = 1e30
LEAST = 1e-37

FOX_H, HD = 16, 64
FOX_F = 3 * D
G, CMP, STRIDE, CLEN, HID = 4, 15, 16, 32, 256
NG = G * CMP
NSA_KC, NSA_VC, NSA_KS, NSA_VS, NSA_KW, NSA_VW, NSA_GATE = [D + 256 * i for i in range(7)]
NSA_Z = NSA_GATE + 3 * FOX_H
HG_H, LEVELS = 8, 7
ML_H, NOPE, ROPE, QK, LORA = 8, 128, 64, 192, 256
FF = 2816
FC = FF // P
UNITS_PER_LOOP = 4

NSLOT = 6
SLOT = 2048
AB = 3


def shape_constants():
    p = np.arange(P)
    f = np.float32
    cols, at = [], {}

    def put(name, a):
        at[name] = (sum(c.shape[1] for c in cols), a.shape[1])
        cols.append(np.asarray(a, f))

    put("ident", np.eye(P))
    put("tri", p[:, None] <= p[None, :])
    put("ones", np.ones((P, P)))
    put("zero", np.zeros((P, P)))
    put("mask", np.where(p[None, :] > p[:, None], f(BIG), f(0)))
    end = np.arange(CMP) * STRIDE + CLEN - 1
    for t in range(TT):
        put(f"cmask{t}", np.where(end[None, :] > (p + t * P)[:, None], f(BIG), f(0)))
        put(f"cvalid{t}", (end[0] <= p + t * P)[:, None])
    half = HD // 8
    rot = np.zeros((P, P))
    for b in (0, HD):
        for d in range(half):
            rot[b + d + half, b + d] = -1.0
            rot[b + d, b + d + half] = 1.0
    put("rot", rot)
    inv = np.power(f(500000.0), -np.arange(half, dtype=f) * f(2.0 / (2 * half)))
    for name, pos in (("tok", np.arange(S)), ("cmp", np.tile(end, G))):
        ang = pos.astype(f)[None, :] * inv[:, None]
        c, s = np.ones((P, len(pos)), f), np.zeros((P, len(pos)), f)
        for b in (0, half, HD, HD + half):
            c[b:b + half], s[b:b + half] = np.cos(ang), np.sin(ang)
        put("cos_" + name, c)
        put("sin_" + name, s)
    lev, msk = [], []
    for l in range(LEVELS):
        m = 1 << l
        mid = p // (2 * m) * (2 * m) + m - 1
        up = (p & m) > 0
        a = np.where(up[None, :], (p[:, None] > mid[None, :]) & (p[:, None] <= p[None, :]),
                     (p[:, None] > p[None, :]) & (p[:, None] <= mid[None, :]))
        lev.append(a)
        msk.append((~up)[:, None] & up[None, :] & (p[:, None] // (2 * m) == p[None, :] // (2 * m)))
    before = p[:, None] > p[None, :]
    upto = p[:, None] <= p[None, :]
    put("levels", np.concatenate(lev[:4] + [before] + lev[4:] + [upto], 1))
    put("lmask", np.concatenate(msk + [np.eye(P)], 1))
    rot2 = np.zeros((P, P))
    for d in range(ROPE // 2):
        rot2[d + ROPE // 2, d] = -1.0
        rot2[d, d + ROPE // 2] = 1.0
    put("rot2", rot2)
    inv2 = f(10000.0) ** (-np.arange(0, ROPE, 2, dtype=f) / f(ROPE))
    put("inv2", np.where(p < ROPE, inv2[p % (ROPE // 2)], 0)[:, None])
    return np.ascontiguousarray(np.concatenate(cols, 1)), at


def bcast(ap, axis, n):
    a = ap.unsqueeze(axis)
    shape = list(a.shape)
    shape[axis] = n
    return a.broadcast_to(shape)


class Chain:

    def __init__(self, eng, sem):
        self.eng, self.sem, self.n = eng, sem, 0

    def __call__(self, ins):
        self.n += 1
        ins.then_inc(self.sem, 1)
        self.eng.wait_ge(self.sem, self.n)


def build(nc, A, cst_dram, out, at):
    ctx = ExitStack()
    with ctx:
        def sb(name, shape, dt=F32):
            return ctx.enter_context(nc.sbuf_tensor(name, shape, dt))

        def sem(name):
            return ctx.enter_context(nc.semaphore(name))

        B = [ctx.enter_context(nc.psum_tensor(f"bank{i}", [P, 512], F32)) for i in range(8)]
        x = sb("x", [P, DC, S])
        h = sb("h", [P, DC, S])
        ring = sb("ring", [P, NSLOT, SLOT])
        ncst = cst_dram.shape[1]
        cst = sb("cst", [P, ncst])
        zeros_bf = sb("zeros_bf", [P, 512], BF16)
        eps = sb("eps", [P, 1])
        rstd = sb("rstd", [P, S])
        WORK = 30 * 1024 + 768
        SPLITS = 3

        class Memory:

            def __init__(self):
                self.ctx, self.times = ExitStack(), 0

            def open(self):
                self.times += 1
                self.work = self.ctx.enter_context(nc.sbuf_tensor(f"work{self.times}", [P, WORK], F32))

            def close(self):
                self.ctx.close()

        memory = Memory()

        def C(name, a=0, b=None):
            o, n = at[name]
            return cst[:, o + a:o + (n if b is None else b)]

        ident, ones = C("ident"), C("ones")

        class Area:

            def __init__(self):
                self.at = 0

            def __call__(self, *dims):
                n = int(np.prod(dims))
                a = memory.work[:, self.at:self.at + n]
                self.at += n
                assert self.at <= WORK, self.at
                if len(dims) == 1:
                    return a
                names = "abcd"[:len(dims)]
                return a.rearrange(f"p ({' '.join(names)}) -> p {' '.join(names)}",
                                   **dict(zip(names, dims)))

        prows, pcol = [], {}

        def rows(name, ap, n, width=P):
            pcol[name] = len(prows)
            prows.extend((ap, i, n, width) for i in range(n))

        def vec(ap, n):
            return ap.rearrange("(r q) -> r q", q=n)

        rows("norm_g", A["norm_g"].rearrange("l (r q) -> (l r) q", q=P), 2 * DC)
        rows("final_g", vec(A["final_g"], P), DC)
        rows("norm_mix", A["norm_mix_2"].rearrange("l (r q) -> (l r) q", q=P), 2 * DC)
        rows("norm_ffn", A["norm_ffn_2"].rearrange("l (r q) -> (l r) q", q=P), 2 * DC)
        rows("hgrn_norm", A["hgrn_out_norm_2"], 1)
        rows("q_a", vec(A["mla_q_a_norm_2"][0], P), LORA // P)
        rows("kv_a", vec(A["mla_kv_a_norm_2"][0], P), LORA // P)
        for name in ("q", "k"):
            rows(name + "_nope", A[f"mla_{name}_norm_2"][:, 0:NOPE], 1)
            rows(name + "_rope", A[f"mla_{name}_norm_2"][:, NOPE:QK], 1, ROPE)
        for n in "kv":
            rows("pe_" + n, A[f"nsa_pe_{n}"][0].rearrange("(i a) d -> i (a d)", a=2), CLEN // 2)
        n_small = len(prows)
        conv_col = []
        for l in range(2):
            w = A["ffn_conv_w_2"][l].rearrange("j (r q) -> (j r) q", q=P)
            conv_col.append(n_small + 8 * FC * l)
            rows(f"conv_w{l}", w, 6 * FC)
            rows(f"conv_b{l}", vec(A["ffn_conv_b_2"][l], P), 2 * FC)
        NPAR = len(prows)
        par = sb("par", [P, NPAR])
        ctx.callback(memory.close)
        memory.open()

        def pc(name, i=0, n=1):
            return par[:, pcol[name] + i:pcol[name] + i + n]

        tiles = []

        def wtiles(w, c0, width, step=256, kc=DC):
            a = w.rearrange("(c p) n -> p c n", p=P)
            first = len(tiles)
            for c in range(c0, c0 + width, step):
                tiles.append((a[:, :, c:c + step], kc, step))
            return first

        T = {}
        fw = A["fox_w_in"][0]
        T["fox_q"] = wtiles(fw, 0, D)
        T["fox_k"] = wtiles(fw, D, D)
        T["fox_v"] = wtiles(fw, 2 * D, D)
        T["fox_z"] = wtiles(fw, FOX_F + FOX_H, D)
        T["fox_out"] = wtiles(A["fox_w_out"][0], 0, D)
        nw = A["nsa_w_in"][0]
        T["nsa_in"] = wtiles(nw, D, 6 * 256)
        ck = []
        for n, name in enumerate(("nsa_w_ck1", "nsa_w_cv1")):
            a = A[name][0].rearrange("(i p) n -> p i n", p=P)
            ck.append(len(tiles))
            for b in range(2):
                tiles.append((a[:, 8 * b:8 * b + 8, :], 8, HID))
        T["nsa_q"] = wtiles(nw, 0, D)
        T["nsa_z"] = wtiles(nw, NSA_Z, D)
        T["nsa_out"] = wtiles(A["nsa_w_out"][0], 0, D)
        hw = A["hgrn_w_in_2"][0]
        T["hgrn_f"] = wtiles(hw, D, D)
        T["hgrn_q"] = wtiles(hw, 0, D)
        T["hgrn_i"] = wtiles(hw, 2 * D, D)
        T["hgrn_g"] = wtiles(hw, 3 * D, D)
        T["hgrn_out"] = wtiles(A["hgrn_w_out_2"][0], 0, D)

        def ffn_tiles(l):
            up = A["ffn_w_up_2"][l].rearrange("(c p) (e n) -> p e c n", p=P, e=2)
            down = A["ffn_w_down_2"][l].rearrange("(c p) n -> p c n", p=P)
            first = len(tiles)
            for j in range(2):
                tiles.append(("up", up, j))
            for g in range(10):
                tiles.append(("up", up, 2 * g + 2))
                tiles.append(("up", up, 2 * g + 3))
                tiles.append(("down", down, g))
            tiles.append(("down", down, 10))
            return first

        T["ffn0"] = ffn_tiles(0)
        mw = A["mla_w_in_2"][0]
        T["mla_in"] = wtiles(mw, 0, 2 * LORA)
        T["mla_q"] = wtiles(A["mla_w_q_up_2"][0], 0, ML_H * QK, step=4 * QK, kc=2)
        T["mla_kv"] = wtiles(A["mla_w_kv_up_2"][0], 0, ML_H * 256, step=1024, kc=2)
        T["mla_out"] = wtiles(A["mla_w_out_2"][0], 0, D)
        T["ffn1"] = ffn_tiles(1)
        NT = len(tiles)

        def slot(t, kc, n):
            return ring[:, t % NSLOT, 0:kc * n].rearrange("p (k n) -> p k n", k=kc)

        w_loaded = [sem(f"w_loaded{i}") for i in range(NSLOT)]
        tile_done = sem("tile_done")
        bank_free = [sem(f"bank_free{i}") for i in range(2)]

        def load(sp, t):
            if t >= NT:
                return
            if t >= NSLOT:
                sp.wait_ge(tile_done, t - NSLOT + 1)
            src = tiles[t]
            s = w_loaded[t % NSLOT]
            if src[0] == "up":
                sp.dma_start(up_slot(t), src[1][:, :, :, src[2] * P:(src[2] + 1) * P]).then_inc(s, 16)
            elif src[0] == "down":
                sp.dma_start(slot(t, 2, D), src[1][:, 2 * src[2]:2 * src[2] + 2, :]).then_inc(s, 16)
            else:
                sp.dma_start(slot(t, src[1], src[2]), src[0]).then_inc(s, 16)

        def up_slot(t):
            return ring[:, t % NSLOT, :].rearrange("p (e c n) -> p e c n", e=2, c=DC)

        def landed(eng, t, later=0):
            eng.wait_ge(w_loaded[t % NSLOT], later * 16 + 16 * (t // NSLOT + 1))

        turn = {"n": 0}
        bank_of = {}

        def plan_tile(t):
            bank_of[t] = turn["n"]
            turn["n"] += 1

        def pbank(t):
            return B[bank_of[t] % 2]

        def wait_bank(pe, t):
            u = bank_of[t]
            if u >= 2:
                pe.wait_ge(bank_free[u % 2], u // 2)

        def freed(t):
            return bank_free[bank_of[t] % 2]

        def evacuated(eng, t):
            eng.wait_ge(freed(t), bank_of[t] // 2 + 1)

        def by_feature(pe, t, act, kc=DC, chunks=2, ready=None):
            landed(pe, t)
            wait_bank(pe, t)
            w = slot(t, kc, tiles[t][2])
            for j in range(chunks):
                for c in range(kc):
                    if ready is not None and j == 0:
                        ready(c)
                    mm = nc.tensor.matmul(pbank(t)[:, j * S:(j + 1) * S], w[:, c, j * P:(j + 1) * P],
                                          act[:, c, :], start=(c == 0), stop=(c == kc - 1))
            mm.then_inc(tile_done, 1)

        def by_token(pe, t, act, ready=None):
            landed(pe, t)
            wait_bank(pe, t)
            w = slot(t, DC, 256)
            for tt in range(TT):
                for c in range(DC):
                    if ready is not None and tt == 0:
                        ready(c)
                    mm = nc.tensor.matmul(pbank(t)[:, tt * 256:(tt + 1) * 256], act[:, c, tt * P:(tt + 1) * P],
                                          w[:, c, :], start=(c == 0), stop=(c == DC - 1))
            mm.then_inc(tile_done, 1)

        def bank2(t):
            return pbank(t)[:, :].rearrange("p (a b) -> p a b", a=2)

        norms = {"n": 0, "split": 0}
        sq_act, sq_dve = sem("squares_act"), sem("squares_dve")
        n_summed, n_root, n_inv = sem("norm_summed"), sem("norm_root"), sem("norm_inverse")
        n_ready = sem("norm_ready")
        n_high, n_split = sem("norm_high_ready"), sem("norm_split")

        class Norm:

            def __init__(self, gain, dst=None, after=None, split=None, sq=None):
                self.split = split
                self.after = after
                self.n = norms["n"]
                norms["n"] += 1
                self.gain, self.dst = gain, h if dst is None else dst
                self.sq = memory.work[:, WORK - DC * S:WORK].rearrange("p (c t) -> p c t", c=DC) if sq is None else sq
                if split is not None:
                    self.s = DC * norms["split"]
                    norms["split"] += 1

            def act(self, act):
                if self.after:
                    self.after.wait(act, DC)
                for c in range(0, 4, 2):
                    nc.scalar.activation(self.sq[:, c:c + 2, :], x[:, c:c + 2, :], ACT.Square).then_inc(sq_act, 1)
                act.wait_ge(n_summed, self.n + 1)
                nc.scalar.activation(rstd[:, :], B[7][:, 0:S], ACT.Sqrt, scale=1.0 / D,
                                     bias=eps[:, 0:1]).then_inc(n_root, 1)

            def act_split(self, act):
                for c in range(DC):
                    self.wait(act, c + 1)
                    nc.scalar.activation(self.split[0][:, c, :], self.dst[:, c, :], ACT.Copy).then_inc(n_high, 1)

            def low(self, dve, c):
                dve.wait_ge(n_high, self.s + c + 1)
                nc.vector.tensor_tensor(self.split[1][:, c, :], self.dst[:, c, :],
                                        self.split[0][:, c, :].bitcast(F32), ALU.subtract).then_inc(n_split, 1)

            def dve(self, dve):
                if self.after:
                    self.after.wait(dve, DC)
                for c in range(4, DC, 2):
                    nc.vector.tensor_tensor(self.sq[:, c:c + 2, :], x[:, c:c + 2, :], x[:, c:c + 2, :],
                                            ALU.mult).then_inc(sq_dve, 1)
                dve.wait_ge(n_root, self.n + 1)
                nc.vector.reciprocal(rstd[:, :], rstd[:, :]).then_inc(n_inv, 1)
                dve.wait_ge(n_inv, self.n + 1)
                for c in range(DC):
                    nc.vector.scalar_tensor_tensor(out=self.dst[:, c, :], in0=x[:, c, :],
                                                   scalar=self.gain[:, c:c + 1], in1=rstd[:, :],
                                                   op0=ALU.mult, op1=ALU.mult).then_inc(n_ready, 1)
                    if self.split and c >= 2:
                        self.low(dve, c - 2)
                if self.split:
                    self.low(dve, DC - 2)
                    self.low(dve, DC - 1)

            def pe(self, pe):
                order = [0, 1, 4, 5, 2, 3, 6, 7]
                for n, c in enumerate(order):
                    if c < 4:
                        pe.wait_ge(sq_act, 2 * self.n + c // 2 + 1)
                    else:
                        pe.wait_ge(sq_dve, 2 * self.n + c // 2 - 1)
                    mm = nc.tensor.matmul(B[7][:, 0:S], ones, self.sq[:, c, :], start=(n == 0), stop=(n == DC - 1))
                mm.then_inc(n_summed, 1)

            def wait(self, eng, chunks):
                eng.wait_ge(n_ready, DC * self.n + chunks)

            def chunk(self, pe):
                if self.split:
                    return lambda c: pe.wait_ge(n_split, self.s + c + 1)
                return lambda c: self.wait(pe, c + 1)

        before = {"units": 0, "groups": 0}
        a_multiplied, a_biased, a_exped = sem("logits_ready"), sem("logits_biased"), sem("weights_exped")
        a_inv, a_scaled, a_turned = sem("sums_inverted"), sem("weights_scaled"), sem("weights_turned")
        a_copied, a_weighed, a_taken = sem("weights_copied"), sem("values_weighed"), sem("output_taken")

        class Attention:

            def __init__(self, area, units, groups, take):
                self.units, self.groups, self.take = units, groups, take
                self.u0, self.g0 = before["units"], before["groups"]
                before["units"] += len(units)
                before["groups"] += groups
                n = len(units)
                self.least, self.sum, self.rsum = area(n, 2), area(n, 2), area(n, 2)
                self.lb, self.pb, self.pt = [area(AB, 512) for _ in range(3)]
                self.last_unit = {}
                for u, unit in enumerate(units):
                    self.last_unit[unit["group"]] = u

            def view(self, buf, u):
                unit = self.units[u]
                if buf is None:
                    return B[2 + u % 2][:, 0:unit["nh"] * unit["w"]].rearrange("p (e k) -> p e k", e=unit["nh"])
                return buf[:, u % AB, 0:unit["nh"] * unit["w"]].rearrange("p (e k) -> p e k", e=unit["nh"])

            def pview(self, u):
                unit = self.units[u]
                if unit.get("pb") is not None:
                    return unit["pb"]
                return self.view(self.pb, u)

            def logits(self, pe, u):
                unit = self.units[u]
                if u >= 2:
                    pe.wait_ge(a_biased, self.u0 + u - 1)
                n = len(unit["qk"])
                o = self.view(None, u)
                for i, (q, k) in enumerate(unit["qk"]):
                    mm = nc.tensor.matmul(o, q, k, start=(i == 0), stop=(i == n - 1))
                mm.then_inc(a_multiplied, 1)

            def bias(self, dve, u):
                unit = self.units[u]
                dve.wait_ge(a_multiplied, self.u0 + u + 1)
                if u >= AB:
                    dve.wait_ge(a_exped, self.u0 + u - AB + 1)
                ps, lb = self.view(None, u), self.view(self.lb, u)
                for e in range(unit["nh"]):
                    i = nc.vector.tensor_tensor_reduce(out=lb[:, e, :], in0=ps[:, e, :], in1=unit["bias"][e],
                                                       scale=1.0, scalar=3e38, op0=ALU.add, op1=ALU.min,
                                                       accum_out=self.least[:, u, e:e + 1])
                i.then_inc(a_biased, 1)

            def exp(self, act, u):
                unit = self.units[u]
                act.wait_ge(a_biased, self.u0 + u + 1)
                if u >= AB:
                    act.wait_ge(a_turned, self.u0 + u - AB + 1)
                lb, pb = self.view(self.lb, u), self.pview(u)
                for e in range(unit["nh"]):
                    i = nc.scalar.activation(pb[:, e, 0:unit["w"]], lb[:, e, :], ACT.Exp, scale=-1.0,
                                             bias=self.least[:, u, e:e + 1],
                                             accum_out=self.sum[:, u, e:e + 1])
                i.then_inc(a_exped, 1)

            def scale(self, dve, u):
                unit = self.units[u]
                dve.wait_ge(a_exped, self.u0 + u + 1)
                nh = unit["nh"]
                nc.vector.reciprocal(self.rsum[:, u, 0:nh], self.sum[:, u, 0:nh]).then_inc(a_inv, 1)
                dve.wait_ge(a_inv, self.u0 + u + 1)
                pb = self.pview(u)
                for e in range(nh):
                    w = pb[:, e, 0:unit["w"]]
                    if unit.get("gate") is None:
                        i = nc.vector.tensor_scalar(w, w, self.rsum[:, u, e:e + 1], None, ALU.mult)
                    else:
                        i = nc.vector.tensor_scalar(w, w, self.rsum[:, u, e:e + 1], unit["gate"][e],
                                                    ALU.mult, ALU.mult)
                i.then_inc(a_scaled, 1)

            def turn(self, pe, u):
                unit = self.units[u]
                pe.wait_ge(a_scaled, self.u0 + u + 1)
                if u >= 2:
                    pe.wait_ge(a_copied, self.u0 + u - 1)
                pb = self.pview(u)
                for i in range(unit["nh"] * unit["nkt"]):
                    e, kt = i // unit["nkt"], i % unit["nkt"]
                    mm = nc.tensor.transpose(B[4 + u % 2][:, i * P:(i + 1) * P],
                                             pb[:, e, kt * P:(kt + 1) * P], ident)
                mm.then_inc(a_turned, 1)

            def copy(self, act, u):
                unit = self.units[u]
                act.wait_ge(a_turned, self.u0 + u + 1)
                if u >= AB:
                    act.wait_ge(a_weighed, self.u0 + u - AB + 1)
                n = unit["nh"] * unit["nkt"] * P
                nc.scalar.activation(self.pt[:, u % AB, 0:n], B[4 + u % 2][:, 0:n], ACT.Copy).then_inc(a_copied, 1)

            def weigh(self, pe, u):
                unit = self.units[u]
                pe.wait_ge(a_copied, self.u0 + u + 1)
                g = unit["group"]
                if unit["first"] and g >= 2:
                    pe.wait_ge(a_taken, self.g0 + g - 1)
                o = B[6 + g % 2]
                rows_e = P // unit["nh"]
                c0 = unit["qt"] * P
                for e in range(unit["nh"]):
                    for kt in range(unit["nkt"]):
                        i = e * unit["nkt"] + kt
                        mm = nc.tensor.matmul(o[e * rows_e:(e + 1) * rows_e, c0:c0 + P], unit["v"](e, kt),
                                              self.pt[:, u % AB, i * P:(i + 1) * P],
                                              start=(unit["open"] and kt == 0),
                                              stop=(unit["close"] and kt == unit["nkt"] - 1))
                mm.then_inc(a_weighed, 1)

            def out(self, dve, g):
                dve.wait_ge(a_weighed, self.u0 + self.last_unit[g] + 1)
                self.take(g, B[6 + g % 2][:, 0:S]).then_inc(a_taken, 1)

            def chunk(self, pe):
                return lambda c: pe.wait_ge(a_taken, self.g0 + c + 1)

            def pe(self, pe):
                n = len(self.units)
                for u in range(n + 3):
                    if u < n:
                        self.logits(pe, u)
                    if 2 <= u <= n + 1:
                        self.turn(pe, u - 2)
                    if u >= 3:
                        self.weigh(pe, u - 3)

            def act(self, act):
                n = len(self.units)
                for u in range(n + 2):
                    if u < n:
                        self.exp(act, u)
                    if u >= 2:
                        self.copy(act, u - 2)

            def dve(self, dve):
                n = len(self.units)
                ends = {u: g for g, u in self.last_unit.items()}
                for u in range(n + 4):
                    if u < n:
                        self.bias(dve, u)
                    if 1 <= u <= n:
                        self.scale(dve, u - 1)
                    if u - 4 in ends:
                        self.out(dve, ends[u - 4])

        def project_out(t0, src):
            for t in range(t0, t0 + 4):
                plan_tile(t)

            def pe(pe, ready=None):
                for t in range(t0, t0 + 4):
                    by_feature(pe, t, src, ready=ready if t == t0 else None)

            def dve(dve):
                for i, t in enumerate(range(t0, t0 + 4)):
                    dve.wait_ge(tile_done, t + 1)
                    xs = x[:, 2 * i:2 * i + 2, :]
                    nc.vector.tensor_tensor(xs, bank2(t), xs, ALU.add).then_inc(freed(t), 1)
            return pe, dve

        tapped, convolved, gated = sem("ffn_tapped"), sem("ffn_convolved"), sem("ffn_gated")
        hidden, conv_step = sem("ffn_hidden_ready"), sem("ffn_conv_step")
        product, high = sem("ffn_hidden_product"), sem("ffn_hidden_high")
        rounded, low_up, low_down = sem("weights_rounded"), sem("pair_weights_low"), sem("down_weights_low")

        def ffn(l, gain, t0, sp_from, sp_to):
            mem = ExitStack()

            def buf(name, *dims, dt=F32):
                return mem.enter_context(nc.sbuf_tensor(f"ffn{l}_{name}", [P, *dims], dt))

            memory.close()
            h_hi, h_lo = buf("h_high", DC, S, dt=F32R), buf("h_low", DC, S, dt=F32R)
            w_hi, w_lo = buf("w_high", SPLITS, SLOT, dt=F32R), buf("w_low", SPLITS, SLOT, dt=F32R)
            act_hi, act_lo = buf("hidden_high", FC, S, dt=F32R), buf("hidden_low", FC, S, dt=F32R)
            y, sg, hid32 = buf("conv", 2, 2, S), buf("gate", 2, S), buf("hidden", 2, S)
            nrm = Norm(gain, split=(h_hi, h_lo), sq=buf("squares", DC, S))
            NTILE = 33
            r0 = NTILE * l
            p0 = l * FC
            u0 = turn["n"]
            turn["n"] += FC
            cw, cb = pcol[f"conv_w{l}"], pcol[f"conv_b{l}"]
            NLOOP = 5

            def column(base, e, j, later):
                c = base + e * FC + j
                return par[:, c:c + 1] if isinstance(later, int) else par[:, bass.ds(later * 4 + c, 1)]

            def pair_tile(j):
                return t0 + (j if j < 2 else 2 + (j - 2) // 2 * 3 + (j - 2) % 2)

            def split_views(off, up):
                both = [r[:, off % SPLITS, :] for r in (w_hi, w_lo)]
                if up:
                    return [b.rearrange("p (e c n) -> p e c n", e=2, c=DC) for b in both]
                return [b.rearrange("p (k n) -> p k n", k=2) for b in both]

            def product3(o, w, a, start, stop, **kw):
                (wh, wl), (ah, al) = w, a
                nc.tensor.matmul(o, wh, ah, start=start, stop=False, **kw)
                nc.tensor.matmul(o, wh, al, start=False, stop=False, **kw)
                return nc.tensor.matmul(o, wl, ah, start=False, stop=stop, **kw)

            def pair(pe, j, later=0, ready=None):
                t, u = pair_tile(j), u0 + j
                pe.wait_ge(low_up, p0 + later * 4 + j + 1)
                if u >= 2:
                    pe.wait_ge(bank_free[u % 2], later * 2 + u // 2)
                w = split_views(t - t0, True)
                for e in range(2):
                    for c in range(DC):
                        if ready and e == 0:
                            ready(c)
                        mm = product3(B[u % 2][:, e * S:(e + 1) * S], [v[:, e, c, :] for v in w],
                                      [v[:, c, :] for v in (h_hi, h_lo)], c == 0, c == DC - 1)
                mm.then_inc(tile_done, 1)

            def step_down(pe, g, later=0, last=False):
                off = 4 + 3 * g if g < 10 else 32
                pe.wait_ge(low_down, p0 // 2 + later * 2 + g + 1)
                pe.wait_ge(hidden, p0 + later * 4 + 2 * g + 2)
                w = split_views(off, False)
                for k in range(2):
                    c = 2 * g + k
                    a = [v[:, c, :] if isinstance(later, int) else v[:, bass.ds(later * 4 + c, 1), :]
                         for v in (act_hi, act_lo)]
                    for o in range(DC):
                        mm = product3(B[4 + o // 2][:, (o % 2) * S:(o % 2 + 1) * S],
                                      [v[:, k, o * P:(o + 1) * P] for v in w], a, False, last and k == 1,
                                      skip_group_check=True)
                mm.then_inc(tile_done, 1)

            def round_tile(act, off, later=0):
                if off >= NTILE:
                    return
                landed(act, t0 + off, later)
                if not (isinstance(later, int) and off < SPLITS):
                    act.wait_ge(tile_done, later * 6 + t0 + off - SPLITS + 1)
                nc.scalar.activation(w_hi[:, off % SPLITS, :], ring[:, (t0 + off) % NSLOT, :],
                                     ACT.Copy).then_inc(rounded, 1)

            def low_tile(eng, ops, off, signal, later=0):
                eng.wait_ge(rounded, r0 + later * 6 + off + 1)
                ops.tensor_tensor(w_lo[:, off % SPLITS, :], ring[:, (t0 + off) % NSLOT, :],
                                  w_hi[:, off % SPLITS, :].bitcast(F32), ALU.subtract).then_inc(signal, 1)

            def tap(act, j, later=0):
                t, u = pair_tile(j), u0 + j
                act.wait_ge(tile_done, later * 6 + t + 1)
                if not (isinstance(later, int) and j < 2):
                    act.wait_ge(hidden, p0 + later * 4 + j - 1)
                for e in range(2):
                    i = nc.scalar.activation(y[:, j % 2, e, :], B[u % 2][:, e * S:(e + 1) * S], ACT.Identity,
                                             scale=column(cw + 4 * FC, e, j, later),
                                             bias=column(cb, e, j, later))
                i.then_inc(tapped, 1)

            def gate(act, j, later=0):
                act.wait_ge(convolved, p0 + later * 4 + j + 1)
                nc.scalar.activation(sg[:, j % 2, :], y[:, j % 2, 0, :], ACT.Silu).then_inc(gated, 1)

            def convolve(dve, j, later=0):
                u = u0 + j
                dve.wait_ge(tapped, p0 + later * 4 + j + 1)
                for back in (1, 2):
                    for e in range(2):
                        dst = y[:, j % 2, e, back:S]
                        i = nc.vector.scalar_tensor_tensor(
                            out=dst, in0=B[u % 2][:, e * S:(e + 1) * S - back],
                            scalar=column(cw + (2 - back) * 2 * FC, e, j, later), in1=dst,
                            op0=ALU.mult, op1=ALU.add)
                        if back == 1:
                            i.then_inc(conv_step, 1)
                        elif e == 0:
                            i.then_inc(convolved, 1)
                        else:
                            i.then_inc(bank_free[u % 2], 1)
                    if back == 1:
                        dve.wait_ge(conv_step, 2 * p0 + later * 8 + 2 * j + 2)

            def multiply(dve, j, later=0):
                u = u0 + j
                dve.wait_ge(gated, p0 + later * 4 + j + 1)
                dve.wait_ge(bank_free[u % 2], later * 2 + u // 2 + 1)
                ah, al = [v[:, j, :] if isinstance(later, int) else v[:, bass.ds(later * 4 + j, 1), :].squeeze(1)
                          for v in (act_hi, act_lo)]
                a = hid32[:, j % 2, :]
                nc.vector.tensor_tensor(a, sg[:, j % 2, :], y[:, j % 2, 1, :], ALU.mult).then_inc(product, 1)
                dve.wait_ge(product, p0 + later * 4 + j + 1)
                nc.vector.tensor_copy(ah, a).then_inc(high, 1)
                dve.wait_ge(high, p0 + later * 4 + j + 1)
                nc.vector.tensor_tensor(al, a, ah.bitcast(F32), ALU.subtract).then_inc(hidden, 1)
                dve.wait_ge(hidden, p0 + later * 4 + j + 1)

            def load_ffn(sp, off, later=0):
                t = t0 + off
                sp.wait_ge(tile_done, later * 6 + t - NSLOT + 1)
                kind, src, n = tiles[t]
                s = w_loaded[t % NSLOT]
                if kind == "up":
                    sp.dma_start(up_slot(t), src[:, :, :, bass.ds(later * (4 * P) + n * P, P)]).then_inc(s, 16)
                else:
                    sp.dma_start(slot(t, 2, D), src[:, bass.ds(later * 4 + 2 * n, 2), :]).then_inc(s, 16)

            with nc.Block() as block:
                @block.sync
                def _(sp):
                    for t in range(sp_from, t0 + NSLOT):
                        load(sp, t)
                    with sp.Fori(0, 4) as i:
                        for off in range(NSLOT, 2 * NSLOT):
                            load_ffn(sp, off, i)
                    for t in range(t0 + 30, sp_to):
                        load(sp, t)

                @block.tensor
                def _(pe):
                    nrm.pe(pe)
                    for b in range(4, 8):
                        if b == 7:
                            pe.wait_ge(n_root, nrm.n + 1)
                        nc.tensor.matmul(B[b][:, :], zeros_bf[:, 0:P], zeros_bf[:, :], start=True, stop=False,
                                         skip_group_check=True)
                    pair(pe, 0, ready=nrm.chunk(pe))
                    pair(pe, 1)
                    with pe.Fori(0, NLOOP) as i:
                        for g in range(2):
                            pair(pe, 2 * g + 2, i)
                            pair(pe, 2 * g + 3, i)
                            step_down(pe, g, i)
                    step_down(pe, 10, last=True)

                @block.gpsimd
                def _(pool):
                    for j in range(4):
                        low_tile(pool, nc.gpsimd, pair_tile(j) - t0, low_up)
                    with pool.Fori(0, 4) as i:
                        for r in range(4):
                            low_tile(pool, nc.gpsimd, pair_tile(4 + r) - t0, low_up, i)
                    for j in (FC - 2, FC - 1):
                        low_tile(pool, nc.gpsimd, pair_tile(j) - t0, low_up)

                @block.scalar
                def _(act):
                    nrm.act(act)
                    for off in range(SPLITS):
                        round_tile(act, off)
                    nrm.act_split(act)
                    tap(act, 0)
                    round_tile(act, 3)
                    tap(act, 1)
                    round_tile(act, 4)
                    gate(act, 0)

                    def two_pairs(r, off, later=0):
                        tap(act, r, later)
                        round_tile(act, off, later)
                        gate(act, r - 1, later)
                        tap(act, r + 1, later)
                        round_tile(act, off + 1, later)
                        gate(act, r, later)
                        round_tile(act, off + 2, later)

                    with act.Fori(0, NLOOP - 1) as i:
                        for g in range(2):
                            two_pairs(2 + 2 * g, 5 + 3 * g, i)
                    for g in range(2):
                        two_pairs(18 + 2 * g, 29 + 3 * g)
                    gate(act, FC - 1)

                @block.vector
                def _(dve):
                    nrm.dve(dve)
                    convolve(dve, 0)
                    convolve(dve, 1)
                    low_tile(dve, nc.vector, 4, low_down)
                    multiply(dve, 0)

                    def two_pairs(r, off, later=0):
                        for k in range(2):
                            convolve(dve, r + k, later)
                            multiply(dve, r + k - 1, later)
                        if off < NTILE:
                            low_tile(dve, nc.vector, off, low_down, later)

                    with dve.Fori(0, NLOOP - 1) as i:
                        for g in range(2):
                            two_pairs(2 + 2 * g, 7 + 3 * g, i)
                    two_pairs(18, 31)
                    two_pairs(20, 32)
                    multiply(dve, FC - 1)
                    dve.wait_ge(tile_done, t0 + 33)
                    for o in range(4):
                        xs = x[:, 2 * o:2 * o + 2, :]
                        nc.vector.tensor_tensor(xs, B[4 + o][:, :].rearrange("p (a b) -> p a b", a=2), xs, ALU.add)
            mem.close()
            memory.open()

        area = Area()
        x_tok = area(TT, D)
        prow = [area(P) for _ in range(6)]
        groups = [(0, n_small)] + [(n_small + 88 * i, 88) for i in range(4)]
        loaded_c, loaded_c2 = sem("constants_loaded"), sem("late_constants_loaded")
        loaded_x, loaded_p = sem("x_loaded"), sem("params_loaded")
        cleared, x_turned, x_placed = sem("cleared"), sem("x_turned"), sem("x_placed")
        p_turned = sem("params_turned")
        n_pdma = []
        with nc.Block() as block:
            @block.sync
            def _(sp):
                sp.dma_start(x_tok, A["x"][0].rearrange("(t p) d -> p t d", p=P)).then_inc(loaded_x, 16)
                sp.dma_start(cst[:, 0:640], cst_dram[:, 0:640]).then_inc(loaded_c, 16)
                for t in range(NSLOT):
                    load(sp, t)
                sp.dma_start(cst[:, 640:], cst_dram[:, 640:]).then_inc(loaded_c2, 16)

            @block.gpsimd
            def _(pool):
                nc.gpsimd.memset(prow[0], 0.0).then_inc(cleared, 1)
                nc.gpsimd.memset(zeros_bf[:, :], 0.0)
                nc.gpsimd.memset(eps[:, :], EPS).then_inc(cleared, 1)

            @block.scalar
            def _(act):
                act.wait_ge(cleared, 1)
                n = 0
                for g, (r0, count) in enumerate(groups):
                    r = r0
                    while r < r0 + count:
                        ap, i, total, width = prows[r]
                        m = min(total - i, r0 + count - r)
                        act.dma_start(prow[g][r - r0:r - r0 + m, 0:width], ap[i:i + m, :]).then_inc(loaded_p, 16)
                        r += m
                        n += 1
                n_pdma.append(n)

            @block.tensor
            def _(pe):
                pe.wait_ge(loaded_x, 16)
                pe.wait_ge(loaded_c, 16)
                for c in range(DC):
                    for tt in range(TT):
                        mm = nc.tensor.transpose(B[c // 2][:, (c % 2) * S + tt * P:(c % 2) * S + (tt + 1) * P],
                                                 x_tok[:, tt, c * P:(c + 1) * P], ident)
                    if c % 2:
                        mm.then_inc(x_turned, 1)
                pe.wait_ge(loaded_p, 16 * n_pdma[0])
                for g, (r0, count) in enumerate(groups):
                    mm = nc.tensor.transpose(B[4][:, r0:r0 + count], prow[g][0:count, :],
                                             ident[0:count, 0:count])
                mm.then_inc(p_turned, 1)

            @block.vector
            def _(dve):
                for i in range(4):
                    dve.wait_ge(x_turned, i + 1)
                    nc.vector.tensor_copy(x[:, 2 * i:2 * i + 2, :],
                                          B[i][:, :].rearrange("p (a b) -> p a b", a=2)).then_inc(x_placed, 1)
                dve.wait_ge(p_turned, 1)
                for g, (r0, count) in enumerate(groups):
                    nc.vector.tensor_copy(par[:, r0:r0 + count], B[4][:, r0:r0 + count])

        area = Area()
        w_f = area(DC, FOX_H)
        b_f = area(FOX_H)
        f_raw, f_abs, f_exp, f_log = [area(TT * FOX_H) for _ in range(4)]
        logf = area(TT, FOX_H)
        c_q = area(TT, FOX_H)
        qT, zT, oz = area(DC, S), area(DC, S), area(DC, S)
        kz = area(FOX_H, S)
        v = area(TT, D)
        cm0, cm1 = area(FOX_H, P), area(FOX_H, S)
        nrm = Norm(pc("norm_g", 0, DC))
        fl, fps = sem("fox_f_loaded"), sem("fox_f_product")
        f_steps, f_steps_a = sem("fox_f_steps"), sem("fox_f_act")
        logf_ready, cq_ps, cq_ready = sem("logf_ready"), sem("c_q_product"), sem("c_q_ready")
        ck_ps, ck_used = sem("c_k_product"), sem("c_k_used")
        kz_clear = sem("fox_keys_clear")
        fq, fk, fv, fz = T["fox_q"], T["fox_k"], T["fox_v"], T["fox_z"]
        for t in range(fq, fz + 4):
            plan_tile(t)

        def masks(qt):
            o, n = at["zero"]
            return cst[:, o:o + S] if qt else C("mask")

        units = []
        for c in range(DC):
            for qt in range(TT):
                w = (qt + 1) * P
                cm = (cm0, cm1)[qt]
                units.append(dict(
                    group=c, qt=qt, nh=2, w=w, nkt=qt + 1, first=(qt == 0), open=True, close=True,
                    qk=[(qT[:, c, qt * P:(qt + 1) * P], kz[:, 2 * c:2 * c + 2, 0:w])],
                    bias=[cm[:, 2 * c + e, :] for e in range(2)],
                    v=lambda e, kt, c=c: v[:, kt, (2 * c + e) * HD:(2 * c + e + 1) * HD]))
        att = Attention(area, units, DC,
                        lambda g, ps: nc.vector.tensor_tensor(oz[:, g, :], ps, zT[:, g, :], ALU.mult))
        out_pe, out_dve = project_out(T["fox_out"], oz)

        with nc.Block() as block:
            @block.sync
            def _(sp):
                sp.dma_start(w_f, fw.rearrange("(c p) n -> p c n", p=P)[:, :, FOX_F:FOX_F + FOX_H]).then_inc(fl, 16)
                sp.dma_start(b_f, A["fox_b_f"].broadcast_to([P, FOX_H])).then_inc(fl, 16)
                for t in range(NSLOT, T["fox_out"] + 4 + NSLOT):
                    load(sp, t)

            @block.gpsimd
            def _(pool):
                k4 = kz.rearrange("p (c e) t -> p c e t", e=2)
                nc.gpsimd.memset(k4[0:HD, :, 1, :], 0.0)
                nc.gpsimd.memset(k4[HD:P, :, 0, :], 0.0).then_inc(kz_clear, 1)

            @block.tensor
            def _(pe):
                nrm.pe(pe)
                pe.wait_ge(fl, 32)
                for tt in range(TT):
                    for c in range(DC):
                        if tt == 0:
                            nrm.wait(pe, c + 1)
                        mm = nc.tensor.matmul(B[6][:, tt * FOX_H:(tt + 1) * FOX_H], h[:, c, tt * P:(tt + 1) * P],
                                              w_f[:, c, :], start=(c == 0), stop=(c == DC - 1))
                mm.then_inc(fps, 1)
                for t in range(fq, fq + 4):
                    by_feature(pe, t, h)
                pe.wait_ge(logf_ready, 1)
                nc.tensor.matmul(B[6][:, 0:FOX_H], C("tri"), logf[:, 0, :], start=True, stop=True)
                nc.tensor.matmul(B[6][:, FOX_H:2 * FOX_H], ones, logf[:, 0, :], start=True, stop=False)
                nc.tensor.matmul(B[6][:, FOX_H:2 * FOX_H], C("tri"), logf[:, 1, :], start=False,
                                 stop=True).then_inc(cq_ps, 1)
                tri_ones = cst[:, at["tri"][0]:at["tri"][0] + S]
                for n in range(FOX_H):
                    if n >= 2:
                        pe.wait_ge(ck_used, n - 1)
                    o = B[4 + n % 2]
                    nc.tensor.matmul(o[:, 0:S], logf[:, 0, n:n + 1].broadcast_to([P, P]), tri_ones,
                                     start=True, stop=False)
                    nc.tensor.matmul(o[:, P:S], logf[:, 1, n:n + 1].broadcast_to([P, P]), C("tri"),
                                     start=False, stop=True).then_inc(ck_ps, 1)
                    if n % 4 == 3:
                        by_feature(pe, fk + n // 4, h)
                for t in range(fv, fv + 4):
                    by_token(pe, t, h)
                for t in range(fz, fz + 4):
                    by_feature(pe, t, h)
                evacuated(pe, fz + 3)
                att.pe(pe)
                out_pe(pe, att.chunk(pe))

            @block.scalar
            def _(act):
                nrm.act(act)
                act.wait_ge(f_steps, 2)
                nc.scalar.activation(f_exp, f_abs, ACT.Exp).then_inc(f_steps_a, 1)
                act.wait_ge(f_steps_a, 1)
                nc.scalar.activation(f_log, f_exp, ACT.Ln, bias=ones[:, 0:1]).then_inc(f_steps_a, 1)
                for i in range(4):
                    act.wait_ge(tile_done, fq + i + 1)
                    nc.scalar.activation(qT[:, 2 * i:2 * i + 2, :], bank2(fq + i), ACT.Copy,
                                         scale=-(HD ** -0.5)).then_inc(freed(fq + i), 1)
                act.wait_ge(kz_clear, 1)
                for i in range(4):
                    act.wait_ge(tile_done, fk + i + 1)
                    k4 = kz[:, 4 * i:4 * i + 4, :].rearrange("p (c e) t -> p c e t", e=2)
                    b = bank2(fk + i)
                    nc.scalar.activation(k4[0:HD, :, 0, :], b[0:HD], ACT.Copy)
                    nc.scalar.activation(k4[HD:P, :, 1, :], b[HD:P], ACT.Copy).then_inc(freed(fk + i), 1)
                for i in range(4):
                    act.wait_ge(tile_done, fv + i + 1)
                    nc.scalar.activation(v[:, :, i * 256:(i + 1) * 256], bank2(fv + i), ACT.Copy)\
                        .then_inc(freed(fv + i), 1)
                for i in range(4):
                    act.wait_ge(tile_done, fz + i + 1)
                    a = nc.scalar.activation(zT[:, 2 * i:2 * i + 2, :], bank2(fz + i), ACT.Silu)
                    a.then_inc(freed(fz + i), 1)
                att.act(act)

            @block.vector
            def _(dve):
                nrm.dve(dve)
                dve.wait_ge(fps, 1)
                step = Chain(dve, f_steps)
                fr = f_raw.rearrange("p (t n) -> p t n", t=TT)
                step(nc.vector.tensor_tensor(fr, B[6][:, 0:TT * FOX_H].rearrange("p (t n) -> p t n", t=TT),
                                             bcast(b_f, 1, TT), ALU.add))
                step(nc.vector.scalar_tensor_tensor(out=f_abs, in0=f_raw, scalar=-1.0, in1=f_raw, op0=ALU.mult,
                                                    op1=ALU.min))
                dve.wait_ge(f_steps_a, 2)
                nc.vector.scalar_tensor_tensor(out=logf.rearrange("p t n -> p (t n)"), in0=f_raw, scalar=0.0,
                                               in1=f_log, op0=ALU.min, op1=ALU.subtract).then_inc(logf_ready, 1)
                dve.wait_ge(cq_ps, 1)
                nc.vector.tensor_copy(c_q.rearrange("p t n -> p (t n)"), B[6][:, 0:TT * FOX_H]).then_inc(cq_ready, 1)
                dve.wait_ge(cq_ready, 1)
                for n in range(FOX_H):
                    dve.wait_ge(ck_ps, n + 1)
                    o = B[4 + n % 2]
                    nc.vector.scalar_tensor_tensor(out=cm0[:, n, :], in0=o[:, 0:P], scalar=c_q[:, 0, n:n + 1],
                                                   in1=masks(0), op0=ALU.subtract, op1=ALU.add)
                    nc.vector.scalar_tensor_tensor(out=cm1[:, n, :], in0=o[:, 0:S], scalar=c_q[:, 1, n:n + 1],
                                                   in1=masks(1), op0=ALU.subtract, op1=ALU.add).then_inc(ck_used, 1)
                dve.wait_ge(ck_used, FOX_H)
                evacuated(dve, fz + 3)
                att.dve(dve)
                out_dve(dve)

        area = Area()
        raw_c = area(2, 2, S)
        xs2 = area(2, 2, 2, S)
        xb = [area(CLEN // 2, NG) for _ in range(2)]
        raw_k = [area(2, S) for _ in range(2)]
        roped_k = [area(2, S) for _ in range(2)]
        t_cos, t_sin = area(2, 2 * S), area(2, 2 * S)
        kz2 = [area(2, 2, 2, S) for _ in range(2)]
        v2 = [area(TT, 256) for _ in range(2)]
        raw_q, qT = area(DC, S), area(DC, S)
        zT, oz = area(DC, S), area(DC, S)
        w_gate = area(DC, 3 * FOX_H)
        gate, gatec = area(TT, 3 * FOX_H), area(TT, 3 * FOX_H)
        w2k, w2v = area(2, 2, HD), area(2, HD)
        hid = [area(2, NG) for _ in range(2)]
        raw_kc, cos_kc, sin_kc = area(NG), area(NG), area(NG)
        kzc = area(G, 2, CMP)
        vcm = area(G, HD)
        pbc = [area(2, P) for _ in range(2)]
        nrm2 = Norm(pc("norm_g", DC, DC))
        t_in, t_q, t_z = T["nsa_in"], T["nsa_q"], T["nsa_z"]
        for t in list(range(t_in, t_in + 6)) + list(range(t_q, t_z + 4)):
            plan_tile(t)
        small2, moved_x = sem("nsa_small_loaded"), sem("nsa_blocks_moved")
        moved_k = [sem("nsa_sel_keys_moved"), sem("nsa_win_keys_moved")]
        clear2, pool_step = sem("nsa_cleared"), sem("nsa_clear_step")
        rotated, roped, rope_step = sem("nsa_rotated"), sem("nsa_roped"), sem("nsa_rope_step")
        gate_ps, gate_in, gate_out = sem("gate_product"), sem("gate_sigmoid"), sem("gate_masked")
        blocked, hid_ps, hid_in = sem("blocks_ready"), sem("hidden_product"), sem("hidden_ready")
        cmp_ps, cmp_raw, cmp_rot = sem("cmp_product"), sem("cmp_raw"), sem("cmp_rotated")
        cmp_k, cmp_step = sem("cmp_keys_ready"), sem("cmp_step")
        ropes = [(raw_k[0], roped_k[0]), (raw_k[1], roped_k[1])] + \
            [(raw_q[:, 2 * i:2 * i + 2, :], qT[:, 2 * i:2 * i + 2, :]) for i in range(4)]
        raw_tile = [t_in + 2, t_in + 4] + [t_q + i for i in range(4)]

        units = []
        for c in range(DC):
            g = c // 2
            for qt in range(TT):
                w = (qt + 1) * P
                q = qT[:, c, qt * P:(qt + 1) * P]
                for br in (1, 2):
                    kz_b, v_b = kz2[br - 1], v2[br - 1]
                    units.append(dict(
                        group=c, qt=qt, nh=2, w=w, nkt=qt + 1, first=(qt == 0 and br == 1), open=(br == 1),
                        close=False, qk=[(q, kz_b[:, g // 2, g % 2, :, 0:w])], bias=[masks(qt)] * 2,
                        gate=[gate[:, qt, 3 * (2 * c + e) + br:3 * (2 * c + e) + br + 1] for e in range(2)],
                        v=lambda e, kt, g=g, v_b=v_b: v_b[:, kt, g * HD:(g + 1) * HD]))
                units.append(dict(
                    group=c, qt=qt, nh=2, w=CMP, nkt=1, first=False, open=False, close=True,
                    qk=[(q, kzc[:, g, :, :])], bias=[C(f"cmask{qt}")] * 2,
                    gate=[gatec[:, qt, 3 * (2 * c + e):3 * (2 * c + e) + 1] for e in range(2)],
                    v=lambda e, kt, g=g: vcm[:, g, :], pb=pbc[(2 * c + qt) % 2]))
        att2 = Attention(area, units, DC,
                         lambda g, ps, oz=oz, zT=zT: nc.vector.tensor_tensor(oz[:, g, :], ps, zT[:, g, :], ALU.mult))
        out2_pe, out2_dve = project_out(T["nsa_out"], oz)

        with nc.Block() as block:
            @block.sync
            def _(sp):
                sp.dma_start(w_gate, nw.rearrange("(c p) n -> p c n", p=P)[:, :, NSA_GATE:NSA_Z]).then_inc(small2, 16)
                for e in range(2):
                    sp.dma_start(w2k[:, :, e, :], A["nsa_w_ck2"][0].rearrange("(c p) n -> p c n", p=P))\
                        .then_inc(small2, 16)
                sp.dma_start(w2v, A["nsa_w_cv2"][0].rearrange("(c p) n -> p c n", p=P)).then_inc(small2, 16)
                for t in range(T["fox_out"] + 4 + NSLOT, T["nsa_out"] + 4 + NSLOT):
                    load(sp, t)

            @block.gpsimd
            def _(pool):
                step = Chain(pool, pool_step)
                for kz_b in kz2:
                    step(nc.gpsimd.memset(kz_b[0:HD, :, :, 1, :], 0.0))
                    step(nc.gpsimd.memset(kz_b[HD:P, :, :, 0, :], 0.0))
                step(nc.gpsimd.memset(kzc[0:HD, :, 1, :], 0.0))
                step(nc.gpsimd.memset(kzc[HD:P, :, 0, :], 0.0))
                for b in pbc:
                    step(nc.gpsimd.memset(b, 0.0))
                nc.gpsimd.memset(vcm, 0.0).then_inc(clear2, 1)
                evacuated(pool, t_in)
                evacuated(pool, t_in + 1)
                for par_g in range(2):
                    src = raw_c[par_g * HD:(par_g + 1) * HD]
                    for n in range(2):
                        pool.dma_start(xs2[0:HD, n, :, par_g, :], src[:, n]).then_inc(moved_x, 16)
                        pool.dma_start(xs2[HD:P, n, :, par_g, 0:S - 1], src[:, n, :, 1:S]).then_inc(moved_x, 16)
                for b in range(2):
                    pool.wait_ge(roped, b + 1)
                    for par_g in range(2):
                        for e in range(2):
                            pool.dma_start(kz2[b][e * HD:(e + 1) * HD, :, par_g, e, :],
                                           roped_k[b][par_g * HD:(par_g + 1) * HD]).then_inc(moved_k[b], 16)

            @block.tensor
            def _(pe):
                def rotate(r):
                    evacuated(pe, raw_tile[r])
                    if r >= 2:
                        pe.wait_ge(roped, r - 1)
                    nc.tensor.matmul(B[4 + r % 2][:, :], C("rot"), ropes[r][0], start=True,
                                     stop=True).then_inc(rotated, 1)

                def hidden(n):
                    pe.wait_ge(blocked, n + 1)
                    t0 = ck[n]
                    landed(pe, t0)
                    landed(pe, t0 + 1)
                    for j in range(2):
                        for i in range(CLEN // 2):
                            mm = nc.tensor.matmul(B[2 + n][:, j * NG:(j + 1) * NG],
                                                  slot(t0 + i // 8, 8, HID)[:, i % 8, j * P:(j + 1) * P],
                                                  xb[n][:, i, :], start=(i == 0), stop=(i == CLEN // 2 - 1))
                            if j == 1 and i % 8 == 7:
                                mm.then_inc(tile_done, 1)

                nrm2.pe(pe)
                by_feature(pe, t_in, h, ready=nrm2.chunk(pe))
                by_feature(pe, t_in + 1, h)
                by_feature(pe, t_in + 2, h)
                by_token(pe, t_in + 3, h)
                rotate(0)
                by_feature(pe, t_in + 4, h)
                by_token(pe, t_in + 5, h)
                rotate(1)
                pe.wait_ge(small2, 64)
                for tt in range(TT):
                    for c in range(DC):
                        mm = nc.tensor.matmul(B[6][:, tt * 48:(tt + 1) * 48], h[:, c, tt * P:(tt + 1) * P],
                                              w_gate[:, c, :], start=(c == 0), stop=(c == DC - 1))
                mm.then_inc(gate_ps, 1)
                hidden(0)
                hidden(1)
                by_feature(pe, t_q, h)
                pe.wait_ge(hid_in, 2)
                pe.wait_ge(gate_in, 1)
                for j in range(2):
                    nc.tensor.matmul(B[6][:, 0:NG], w2k[:, j].rearrange("p e d -> p (e d)"), hid[0][:, j, :],
                                     start=(j == 0), stop=(j == 1))
                for g in range(G):
                    for j in range(2):
                        mm = nc.tensor.matmul(B[7][0:CMP, g * HD:(g + 1) * HD], hid[1][:, j, g * CMP:(g + 1) * CMP],
                                              w2v[:, j, :], start=(j == 0), stop=(j == 1))
                mm.then_inc(cmp_ps, 1)
                by_feature(pe, t_q + 1, h)
                rotate(2)
                pe.wait_ge(cmp_raw, 1)
                nc.tensor.matmul(B[2][:, 0:NG], C("rot"), raw_kc, start=True, stop=True).then_inc(cmp_rot, 1)
                by_feature(pe, t_q + 2, h)
                rotate(3)
                by_feature(pe, t_q + 3, h)
                rotate(4)
                by_feature(pe, t_z, h)
                rotate(5)
                for t in range(t_z + 1, t_z + 4):
                    by_feature(pe, t, h)
                pe.wait_ge(roped, 6)
                pe.wait_ge(cmp_k, 1)
                for b in range(2):
                    pe.wait_ge(moved_k[b], 64)
                evacuated(pe, t_z + 3)
                att2.pe(pe)
                out2_pe(pe, att2.chunk(pe))

            @block.scalar
            def _(act):
                def evac(t, dst, func=ACT.Copy, scale=1.0):
                    act.wait_ge(tile_done, t + 1)
                    nc.scalar.activation(dst, bank2(t), func, scale=scale).then_inc(freed(t), 1)

                nrm2.act(act)
                evac(t_in, raw_c[:, 0])
                evac(t_in + 1, raw_c[:, 1])
                evac(t_in + 2, raw_k[0])
                evac(t_in + 3, v2[0])
                evac(t_in + 4, raw_k[1])
                evac(t_in + 5, v2[1])
                act.wait_ge(gate_ps, 1)
                nc.scalar.activation(gate, B[6][:, 0:96].rearrange("p (t n) -> p t n", t=TT),
                                     ACT.Sigmoid).then_inc(gate_in, 1)
                for n in range(2):
                    act.wait_ge(tile_done, ck[n] + 2)
                    nc.scalar.activation(hid[n], B[2 + n][:, 0:2 * NG].rearrange("p (j c) -> p j c", j=2),
                                         ACT.Silu).then_inc(hid_in, 1)
                evac(t_q, raw_q[:, 0:2, :], scale=-(HD ** -0.5))
                act.wait_ge(cmp_ps, 1)
                nc.scalar.activation(raw_kc, B[6][:, 0:NG], ACT.Copy).then_inc(cmp_raw, 1)
                act.wait_ge(clear2, 1)
                nc.scalar.activation(vcm[0:CMP], B[7][0:CMP, 0:G * HD].rearrange("p (g d) -> p g d", g=G),
                                     ACT.Copy)
                for i in range(1, 4):
                    evac(t_q + i, raw_q[:, 2 * i:2 * i + 2, :], scale=-(HD ** -0.5))
                for i in range(4):
                    evac(t_z + i, zT[:, 2 * i:2 * i + 2, :], ACT.Silu)
                att2.act(act)

            @block.vector
            def _(dve):
                step = Chain(dve, rope_step)

                def rope(r):
                    src, dst = ropes[r]
                    tc = t_cos[:, r % 2].rearrange("p (a b) -> p a b", a=2)
                    ts = t_sin[:, r % 2].rearrange("p (a b) -> p a b", a=2)
                    dve.wait_ge(rotated, r + 1)
                    nc.vector.tensor_tensor(tc, src, bcast(C("cos_tok"), 1, 2), ALU.mult)
                    step(nc.vector.tensor_tensor(ts, B[4 + r % 2][:, :].rearrange("p (a b) -> p a b", a=2),
                                                 bcast(C("sin_tok"), 1, 2), ALU.mult))
                    nc.vector.tensor_tensor(dst, tc, ts, ALU.add).then_inc(roped, 1)

                nrm2.dve(dve)
                rope(0)
                dve.wait_ge(moved_x, 128)
                for n in range(2):
                    src = xs2[:, n].rearrange("p a b (c i k) -> p i (a b) c k", c=16, k=2)
                    for half in range(2):
                        i8 = slice(8 * half, 8 * half + 8)
                        pe_n = pc("pe_" + "kv"[n], 8 * half, 8)
                        i = nc.vector.tensor_tensor(
                            xb[n][:, i8, :].rearrange("p i (g c) -> p i g c", g=G),
                            src[:, :, :, half:half + CMP, 0],
                            pe_n.unsqueeze(2).unsqueeze(3).broadcast_to([P, 8, G, CMP]), ALU.add)
                    i.then_inc(blocked, 1)
                rope(1)
                dve.wait_ge(gate_in, 1)
                for tt in range(TT):
                    i = nc.vector.tensor_scalar(gatec[:, tt, :], gate[:, tt, :], C(f"cvalid{tt}"), None, ALU.mult)
                i.then_inc(gate_out, 1)
                rope(2)
                dve.wait_ge(cmp_rot, 1)
                nc.vector.tensor_tensor(cos_kc, raw_kc, C("cos_cmp"), ALU.mult)
                nc.vector.tensor_tensor(sin_kc, B[2][:, 0:NG], C("sin_cmp"), ALU.mult).then_inc(cmp_step, 1)
                dve.wait_ge(cmp_step, 1)
                dve.wait_ge(clear2, 1)
                for e in range(2):
                    r0 = slice(e * HD, (e + 1) * HD)
                    i = nc.vector.tensor_tensor(kzc[r0, :, e, :], cos_kc[r0].rearrange("p (g c) -> p g c", g=G),
                                                sin_kc[r0].rearrange("p (g c) -> p g c", g=G), ALU.add)
                i.then_inc(cmp_k, 1)
                rope(3)
                rope(4)
                rope(5)
                dve.wait_ge(gate_out, 1)
                evacuated(dve, t_z + 3)
                att2.dve(dve)
                out2_dve(dve)

        area = Area()
        fg, keyt, lf = area(TT, D), area(TT, D), area(TT, D)
        b_row, e_row, lb_row, om_row = [area(D) for _ in range(4)]
        qT, gT, keyT, v, oh = area(DC, S), area(DC, S), area(DC, S), area(TT, D), area(DC, S)
        decay = area(2, 8, P)
        qd, kd = area(3, 8, P), area(3, 8, P)
        sm = area(8, P)
        sc, scx = area(2, TT, P), area(2, P)
        sq8, rs8 = fg.rearrange("p t n -> p (t n)"), keyt.rearrange("p t n -> p (t n)")
        nrm_f = Norm(pc("final_g", 0, DC), dst=x)
        nrm3 = Norm(pc("norm_mix", 0, DC), after=nrm_f)
        t_f, t_q3, t_i, t_g = T["hgrn_f"], T["hgrn_q"], T["hgrn_i"], T["hgrn_g"]
        for t in range(t_f, t_g + 4):
            plan_tile(t)
        lb_in, lb_step, lb_exp = sem("bounds_loaded"), sem("bounds_step"), sem("bounds_exp")
        forget, clamped, logged = sem("forget_step"), sem("forget_clamped"), sem("log_forget")
        key_turned, key_placed = sem("key_turned"), sem("key_placed")
        summed, decayed = sem("exponents_summed"), sem("decays_ready")
        q_dec, k_dec = sem("q_decayed"), sem("k_decayed")
        scored, masked, scores_in = sem("hgrn_scored"), sem("hgrn_masked"), sem("hgrn_scores_ready")
        cross_in, o_ps, o_in = sem("cross_scores_ready"), sem("hgrn_output_product"), sem("hgrn_output_ready")
        sq_in, sq_ps, sq_root = sem("hgrn_squares"), sem("hgrn_squares_summed"), sem("hgrn_roots")
        o_step, o_ready = sem("hgrn_norm_step"), sem("hgrn_gated")
        lev0 = at["levels"][0]
        out3_pe, out3_dve = project_out(T["hgrn_out"], oh)
        NU = 2 * HG_H

        def lslot(l, tt):
            return l if l < 4 or tt else l + 1

        with nc.Block() as block:
            @block.sync
            def _(sp):
                sp.dma_start(b_row, A["hgrn_lower_bounds_2"].broadcast_to([P, D])).then_inc(lb_in, 16)
                for t in range(T["nsa_out"] + 4 + NSLOT, T["hgrn_out"] + 4 + NSLOT):
                    load(sp, t)

            @block.gpsimd
            def _(pool):
                for w in range(NU):
                    hh, tt = w // 2, w % 2
                    pool.wait_ge(decayed, w + 1)
                    if w == 0:
                        pool.wait_ge(key_placed, 4)
                    if w >= 3:
                        pool.wait_ge(scored, w - 1)
                    nc.gpsimd.tensor_tensor(kd[:, w % 3], decay[:, w % 2],
                                            bcast(keyT[:, hh, tt * P:(tt + 1) * P], 1, 8), ALU.mult)\
                        .then_inc(k_dec, 1)

            @block.tensor
            def _(pe):
                nrm_f.pe(pe)
                nrm3.pe(pe)
                for i in range(4):
                    by_token(pe, t_f + i, h, ready=nrm3.chunk(pe) if i == 0 else None)
                for i in range(4):
                    by_feature(pe, t_q3 + i, h)
                pe.wait_ge(forget, 3)
                for c in range(DC):
                    for tt in range(TT):
                        mm = nc.tensor.transpose(B[2 + c // 2][:, (c % 2) * S + tt * P:(c % 2) * S + (tt + 1) * P],
                                                 keyt[:, tt, c * P:(c + 1) * P], ident)
                    if c % 2:
                        mm.then_inc(key_turned, 1)
                for i in range(4):
                    by_token(pe, t_i + i, h)
                for i in range(4):
                    by_feature(pe, t_g + i, h)
                pe.wait_ge(logged, 1)
                pe.wait_ge(key_placed, 4)
                evacuated(pe, t_g + 2)
                evacuated(pe, t_g + 3)

                def exponents(w):
                    hh, tt = w // 2, w % 2
                    if w >= 2:
                        pe.wait_ge(decayed, w - 1)
                    for b in range(2):
                        c0 = lev0 + b * (512 + P * tt)
                        mm = nc.tensor.matmul(B[2 * (w % 2) + b][:, :], lf[:, tt, hh * P:(hh + 1) * P],
                                              cst[:, c0:c0 + 512], start=True, stop=True)
                    mm.then_inc(summed, 1)

                def scores(w):
                    hh, tt = w // 2, w % 2
                    pe.wait_ge(q_dec, w + 1)
                    pe.wait_ge(k_dec, w + 1)
                    if w >= 1:
                        pe.wait_ge(masked, w)
                    for l in range(LEVELS):
                        s_ = lslot(l, tt)
                        nc.tensor.matmul(B[4 + l // 4][:, (l % 4) * P:(l % 4 + 1) * P], kd[:, w % 3, s_, :],
                                         qd[:, w % 3, s_, :], start=True, stop=True)
                    tk = slice(tt * P, (tt + 1) * P)
                    mm = nc.tensor.matmul(B[5][:, 3 * P:4 * P], keyT[:, hh, tk], qT[:, hh, tk], start=True, stop=True)
                    if tt:
                        if hh:
                            pe.wait_ge(cross_in, hh)
                        mm = nc.tensor.matmul(B[6][:, 0:P], kd[:, (w - 1) % 3, 4, :], qd[:, w % 3, 7, :],
                                              start=True, stop=True)
                    mm.then_inc(scored, 1)

                def outputs(hh):
                    pe.wait_ge(scores_in, 2 * hh + 2)
                    pe.wait_ge(cross_in, hh + 1)
                    if hh:
                        pe.wait_ge(o_in, hh)
                    vh = [v[:, tt, hh * P:(hh + 1) * P] for tt in range(TT)]
                    nc.tensor.matmul(B[7][:, 0:P], vh[0], sc[:, hh % 2, 0, :], start=True, stop=True)
                    nc.tensor.matmul(B[7][:, P:S], vh[0], scx[:, hh % 2, :], start=True, stop=False)
                    nc.tensor.matmul(B[7][:, P:S], vh[1], sc[:, hh % 2, 1, :], start=False, stop=True)\
                        .then_inc(o_ps, 1)

                for w in range(NU + 2):
                    if w < NU:
                        exponents(w)
                    if 1 <= w <= NU:
                        scores(w - 1)
                    if w >= 3 and w % 2:
                        outputs((w - 3) // 2)
                for i in range(4):
                    pe.wait_ge(sq_in, i + 1)
                    nc.tensor.matmul(B[2 + i][:, :], ones, sq8[:, i * 512:(i + 1) * 512], start=True,
                                     stop=True).then_inc(sq_ps, 1)
                out3_pe(pe, lambda c: pe.wait_ge(o_ready, c // 2 + 1))

            @block.scalar
            def _(act):
                nrm_f.act(act)
                nrm3.act(act)
                act.wait_ge(lb_step, 1)
                nc.scalar.activation(e_row, e_row, ACT.Exp).then_inc(lb_exp, 1)
                for i in range(4):
                    act.wait_ge(tile_done, t_f + i + 1)
                    nc.scalar.activation(fg[:, :, i * 256:(i + 1) * 256], bank2(t_f + i), ACT.Sigmoid)\
                        .then_inc(freed(t_f + i), 1)
                for i in range(4):
                    act.wait_ge(tile_done, t_q3 + i + 1)
                    nc.scalar.activation(qT[:, 2 * i:2 * i + 2, :], bank2(t_q3 + i), ACT.Silu)\
                        .then_inc(freed(t_q3 + i), 1)
                act.wait_ge(clamped, 1)
                nc.scalar.activation(lf, lf, ACT.Ln).then_inc(logged, 1)
                for i in range(4):
                    act.wait_ge(tile_done, t_i + i + 1)
                    nc.scalar.activation(v[:, :, i * 256:(i + 1) * 256], bank2(t_i + i), ACT.Copy)\
                        .then_inc(freed(t_i + i), 1)
                for i in range(4):
                    act.wait_ge(tile_done, t_g + i + 1)
                    nc.scalar.activation(gT[:, 2 * i:2 * i + 2, :], bank2(t_g + i), ACT.Silu)\
                        .then_inc(freed(t_g + i), 1)
                for w in range(NU + 3):
                    if w < NU:
                        act.wait_ge(summed, w + 1)
                        if w >= 2:
                            act.wait_ge(q_dec, w - 1)
                            act.wait_ge(k_dec, w - 1)
                        for b in range(2):
                            i = nc.scalar.activation(decay[:, w % 2, 4 * b:4 * b + 4, :],
                                                     B[2 * (w % 2) + b][:, :].rearrange("p (l t) -> p l t", l=4),
                                                     ACT.Exp)
                        i.then_inc(decayed, 1)
                    if w >= 2 and w % 2 == 0 and w <= NU:
                        hh = w // 2 - 1
                        act.wait_ge(scored, 2 * hh + 2)
                        if hh >= 2:
                            act.wait_ge(o_ps, hh - 1)
                        nc.scalar.activation(scx[:, hh % 2, :], B[6][:, 0:P], ACT.Copy).then_inc(cross_in, 1)
                    if w >= 4 and w % 2 == 0:
                        hh = (w - 4) // 2
                        act.wait_ge(o_ps, hh + 1)
                        nc.scalar.activation(oh[:, hh, :], B[7][:, 0:S], ACT.Copy).then_inc(o_in, 1)
                for i in range(4):
                    act.wait_ge(o_in, 2 * i + 2)
                    nc.scalar.activation(sq8[:, i * 512:(i + 1) * 512].rearrange("p (a b) -> p a b", a=2),
                                         oh[:, 2 * i:2 * i + 2, :], ACT.Square).then_inc(sq_in, 1)
                for i in range(4):
                    act.wait_ge(sq_ps, i + 1)
                    nc.scalar.activation(rs8[:, i * 512:(i + 1) * 512], B[2 + i][:, :], ACT.Sqrt,
                                         scale=1.0 / P, bias=eps[:, 0:1]).then_inc(sq_root, 1)

            @block.vector
            def _(dve):
                nrm_f.dve(dve)
                nrm3.dve(dve)
                dve.wait_ge(lb_in, 16)
                nc.vector.tensor_tensor(e_row, b_row, b_row, ALU.subtract).then_inc(lb_step, 1)
                dve.wait_ge(lb_exp, 1)
                nc.vector.reciprocal(om_row, e_row).then_inc(lb_step, 1)
                dve.wait_ge(lb_step, 2)
                nc.vector.tensor_tensor(b_row, e_row, om_row, ALU.mult).then_inc(lb_step, 1)
                dve.wait_ge(lb_step, 3)
                nc.vector.tensor_tensor(lb_row, b_row, b_row, ALU.subtract).then_inc(lb_step, 1)
                dve.wait_ge(lb_step, 4)
                nc.vector.tensor_scalar(om_row, lb_row, -1.0, 1.0, ALU.mult, ALU.add).then_inc(lb_step, 1)
                dve.wait_ge(lb_step, 5)
                evacuated(dve, t_f + 2)
                evacuated(dve, t_f + 3)
                nc.vector.tensor_tensor(fg, fg, bcast(om_row, 1, TT), ALU.mult).then_inc(forget, 1)
                dve.wait_ge(forget, 1)
                nc.vector.tensor_tensor(fg, fg, bcast(lb_row, 1, TT), ALU.add).then_inc(forget, 1)
                dve.wait_ge(forget, 2)
                nc.vector.tensor_scalar(keyt, fg, -1.0, 1.0, ALU.mult, ALU.add).then_inc(forget, 1)
                nc.vector.tensor_scalar(lf, fg, LEAST, None, ALU.max).then_inc(clamped, 1)
                for i in range(4):
                    dve.wait_ge(key_turned, i + 1)
                    nc.vector.tensor_copy(keyT[:, 2 * i:2 * i + 2, :],
                                          B[2 + i][:, :].rearrange("p (a b) -> p a b", a=2)).then_inc(key_placed, 1)

                def decayed_queries(w):
                    hh, tt = w // 2, w % 2
                    dve.wait_ge(decayed, w + 1)
                    if w == 0:
                        evacuated(dve, t_q3 + 3)
                    if w >= 3:
                        dve.wait_ge(scored, w - 1)
                    nc.vector.tensor_tensor(qd[:, w % 3], decay[:, w % 2],
                                            bcast(qT[:, hh, tt * P:(tt + 1) * P], 1, 8), ALU.mult).then_inc(q_dec, 1)

                def mask_scores(w):
                    hh, tt = w // 2, w % 2
                    dve.wait_ge(scored, w + 1)
                    if w >= 1:
                        dve.wait_ge(scores_in, w)
                    if hh >= 2:
                        dve.wait_ge(o_ps, hh - 1)
                    for b in range(2):
                        i = nc.vector.tensor_tensor(sm[:, 4 * b:4 * b + 4, :],
                                                    B[4 + b][:, :].rearrange("p (l t) -> p l t", l=4),
                                                    C("lmask", 512 * b, 512 * b + 512).rearrange("p (l t) -> p l t", l=4),
                                                    ALU.mult)
                    i.then_inc(masked, 1)
                    dve.wait_ge(masked, w + 1)
                    nc.vector.tensor_reduce(sc[:, hh % 2, tt, :], sm.rearrange("p l t -> p t l"), AX.X,
                                            ALU.add).then_inc(scores_in, 1)

                for w in range(NU + 1):
                    if w < NU:
                        decayed_queries(w)
                    if w >= 1:
                        mask_scores(w - 1)
                step = Chain(dve, o_step)
                for i in range(4):
                    r = rs8[:, i * 512:(i + 1) * 512]
                    o2 = oh[:, 2 * i:2 * i + 2, :]
                    dve.wait_ge(sq_root, i + 1)
                    step(nc.vector.reciprocal(r, r))
                    step(nc.vector.scalar_tensor_tensor(out=o2, in0=o2, scalar=pc("hgrn_norm"),
                                                        in1=r.rearrange("p (a b) -> p a b", a=2),
                                                        op0=ALU.mult, op1=ALU.mult))
                    nc.vector.tensor_tensor(o2, o2, gT[:, 2 * i:2 * i + 2, :], ALU.mult).then_inc(o_ready, 1)
                out3_dve(dve)

        ffn(0, pc("norm_ffn", 0, DC), T["ffn0"], T["ffn0"] + NSLOT, T["ffn0"] + 33 + NSLOT)

        area = Area()
        pos_i = area(S).bitcast(I32)
        ang, turns, sin_h = area(S), area(S), area(S)
        cosT, sinT = area(S), area(S)
        w_r = area(DC, ROPE)
        cq, ckv = area(2, S), area(2, S)
        lsq = [area(2, S) for _ in range(2)]
        lrs = area(2, S)
        gq = area(2)
        kr, krg, kr_sq, kr_t, kr_base = [area(S) for _ in range(5)]
        qn, qr, kn, krh = [area(ML_H, S) for _ in range(4)]
        v, oT = area(TT, D), area(ML_H, S)
        sqn, sqr, rs2, tcos, tsin = [area(2, 2, S) for _ in range(5)]
        nrm5 = Norm(pc("norm_mix", DC, DC))
        t_mi, t_mq, t_mkv = T["mla_in"], T["mla_q"], T["mla_kv"]
        for t in (t_mi, t_mi + 1):
            plan_tile(t)
        use0 = turn["n"]
        uses = [(kind, p) for p in range(4) for kind in ("qn", "qr")]
        for n in range(2):
            uses += [("kn", 4 + 2 * n), ("kn", 5 + 2 * n), ("v", 2 * n), ("v", 2 * n + 1)]
        use_no = {k: use0 + n for n, k in enumerate(uses)}
        turn["n"] += len(uses)
        small5, pos_in, kr_clear = sem("mla_small_loaded"), sem("positions_loaded"), sem("mla_cleared")
        ang_step, sins, cos_ready = sem("angle_step"), sem("sines_ready"), sem("cosines_ready")
        lora_ps, lora_sum = sem("rope_key_product"), sem("lora_summed")
        lora_root, lora_step, lora_ready = sem("lora_root"), sem("lora_step"), sem("lora_ready")
        kr_in, krg_in, kr_rot, kr_ready = sem("rope_key_raw"), sem("rope_key_gained"), sem("rope_key_rotated"), sem("rope_key_ready")
        up_done, sum5 = sem("mla_up_product"), sem("mla_squares_summed")
        root5, step5, gained = sem("mla_root"), sem("mla_step"), sem("mla_gained")
        rot5, ready5 = sem("mla_rotated"), sem("mla_pair_ready")

        units = []
        for hh in range(ML_H):
            for qt in range(TT):
                w = (qt + 1) * P
                tk = slice(qt * P, (qt + 1) * P)
                units.append(dict(
                    group=hh, qt=qt, nh=1, w=w, nkt=qt + 1, first=(qt == 0), open=True, close=True,
                    qk=[(qn[:, hh, tk], kn[:, hh:hh + 1, 0:w]), (qr[:, hh, tk], krh[:, hh:hh + 1, 0:w])],
                    bias=[masks(qt)], v=lambda e, kt, hh=hh, v=v: v[:, kt, hh * P:(hh + 1) * P]))
        att5 = Attention(area, units, ML_H,
                         lambda g, ps, oT=oT: nc.vector.tensor_copy(oT[:, g, :], ps))
        out5_pe, out5_dve = project_out(T["mla_out"], oT)
        TWO_PI = (6.28125, 0.0019340515136718750, float(np.float32(2 * np.pi - 6.28125 - 0.0019340515136718750)))
        ROUND = 1.5 * 2 ** 23

        with nc.Block() as block:
            @block.sync
            def _(sp):
                sp.dma_start(pos_i, A["positions_2"].broadcast_to([P, S])).then_inc(pos_in, 16)
                sp.dma_start(w_r, mw.rearrange("(c p) n -> p c n", p=P)[:, :, 2 * LORA:]).then_inc(small5, 16)
                for t in range(T["ffn0"] + 33 + NSLOT, T["mla_out"] + 4 + NSLOT):
                    load(sp, t)

            @block.gpsimd
            def _(pool):
                nc.gpsimd.memset(kr[ROPE:P], 0.0)
                nc.gpsimd.memset(qr[ROPE:P], 0.0)
                nc.gpsimd.memset(sqr[ROPE:P], 0.0).then_inc(kr_clear, 1)

            @block.tensor
            def _(pe):
                def use_bank(k):
                    u = use_no[k]
                    pe.wait_ge(bank_free[u % 2], u // 2)
                    return B[u % 2]

                def up(p):
                    t = (t_mq if p < 4 else t_mkv) + (p % 4) // 2
                    width = QK if p < 4 else 256
                    if p % 2 == 0:
                        landed(pe, t)
                    w = slot(t, 2, 4 * width)
                    act, parts = (cq, (("qn", 0, NOPE), ("qr", NOPE, ROPE))) if p < 4 else (ckv, (("kn", 0, NOPE),))
                    for kind, c0, m in parts:
                        b = use_bank((kind, p))
                        for e in range(2):
                            c = (2 * (p % 2) + e) * width + c0
                            for k in range(2):
                                mm = nc.tensor.matmul(b[0:m, e * S:(e + 1) * S], w[:, k, c:c + m], act[:, k, :],
                                                      start=(k == 0), stop=(k == 1))
                        if kind == "qr" and p % 2:
                            mm.then_inc(tile_done, 1)
                        else:
                            mm.then_inc(up_done, 1)

                def up_values(n):
                    t = t_mkv + n
                    w = slot(t, 2, 1024).rearrange("p k (e n) -> p k e n", e=4)
                    for tt in range(TT):
                        b = use_bank(("v", 2 * n + tt))
                        for k in range(2):
                            mm = nc.tensor.matmul(b[:, :], ckv[:, k, tt * P:(tt + 1) * P], w[:, k, :, NOPE:],
                                                  start=(k == 0), stop=(k == 1))
                        mm.then_inc(tile_done if tt else up_done, 1)

                def sums(p):
                    u = use_no[("qr" if p < 4 else "kn", p)]
                    pe.wait_ge(bank_free[u % 2], u // 2 + 1)
                    if p >= 2:
                        pe.wait_ge(root5, p - 1)
                    b = B[2 + p % 2]
                    nc.tensor.matmul(b[:, :], ones, sqn[:, p % 2], start=True, stop=False)
                    r = sqr[:, p % 2] if p < 4 else bcast(kr_sq, 1, 2)
                    nc.tensor.matmul(b[:, :], ones, r, start=False, stop=True).then_inc(sum5, 1)

                def rotate(p):
                    pe.wait_ge(gained, p + 1)
                    if p >= 2:
                        pe.wait_ge(ready5, p - 1)
                    nc.tensor.matmul(B[4 + p % 2][:, :], C("rot2"), qr[:, 2 * p:2 * p + 2, :], start=True,
                                     stop=True).then_inc(rot5, 1)

                nrm5.pe(pe)
                by_feature(pe, t_mi, h, ready=nrm5.chunk(pe))
                by_feature(pe, t_mi + 1, h)
                pe.wait_ge(small5, 16)
                for c in range(DC):
                    mm = nc.tensor.matmul(B[6][0:ROPE, 0:S], w_r[:, c, :], h[:, c, :], start=(c == 0), stop=(c == DC - 1))
                mm.then_inc(lora_ps, 1)
                for n in range(2):
                    evacuated(pe, t_mi + n)
                    for k in range(2):
                        mm = nc.tensor.matmul(B[4 + n][:, 0:S], ones, lsq[n][:, k, :], start=(k == 0), stop=(k == 1))
                    mm.then_inc(lora_sum, 1)
                pe.wait_ge(krg_in, 1)
                nc.tensor.matmul(B[7][:, 0:S], C("rot2"), krg, start=True, stop=True).then_inc(kr_rot, 1)
                pe.wait_ge(lora_ready, 2)
                for p in range(10):
                    if p < 8:
                        up(p)
                    if 1 <= p <= 8:
                        sums(p - 1)
                    if 2 <= p < 6:
                        rotate(p - 2)
                    if p in (5, 7):
                        up_values((p - 5) // 2)
                pe.wait_ge(ready5, 8)
                for k in (("v", 2), ("v", 3)):
                    pe.wait_ge(bank_free[use_no[k] % 2], use_no[k] // 2 + 1)
                att5.pe(pe)
                out5_pe(pe, att5.chunk(pe))

            def product_done(eng, k):
                last = {("qr", 1): t_mq, ("qr", 3): t_mq + 1, ("v", 1): t_mkv, ("v", 3): t_mkv + 1}
                if k in last:
                    eng.wait_ge(tile_done, last[k] + 1)
                else:
                    eng.wait_ge(up_done, sum(1 for q in uses[:uses.index(k) + 1] if q not in last))

            @block.scalar
            def _(act):
                act.wait_ge(ang_step, 7)
                nc.scalar.activation(sinT, ang, ACT.Sin)
                nc.scalar.activation(sin_h, ang, ACT.Sin, scale=0.5).then_inc(sins, 1)
                nrm5.act(act)
                for n, dst in enumerate((cq, ckv)):
                    act.wait_ge(tile_done, t_mi + n + 1)
                    nc.scalar.activation(dst, bank2(t_mi + n), ACT.Copy)
                    nc.scalar.activation(lsq[n], bank2(t_mi + n), ACT.Square).then_inc(freed(t_mi + n), 1)
                act.wait_ge(lora_ps, 1)
                act.wait_ge(kr_clear, 1)
                nc.scalar.activation(kr[0:ROPE], B[6][0:ROPE, 0:S], ACT.Copy).then_inc(kr_in, 1)
                act.wait_ge(kr_in, 1)
                nc.scalar.activation(kr_sq, kr, ACT.Square).then_inc(kr_in, 1)
                for n in range(2):
                    act.wait_ge(lora_sum, n + 1)
                    nc.scalar.activation(lrs[:, n, :], B[4 + n][:, 0:S], ACT.Sqrt, scale=1.0 / LORA,
                                         bias=eps[:, 0:1]).then_inc(lora_root, 1)

                def evac(p):
                    if p >= 2:
                        act.wait_ge(sum5, p - 1)
                    parts = (("qn", qn, P, sqn), ("qr", qr, ROPE, sqr)) if p < 4 else (("kn", kn, P, sqn),)
                    for kind, dst, m, sq in parts:
                        product_done(act, (kind, p))
                        u = use_no[(kind, p)]
                        b = B[u % 2][0:m, :].rearrange("p (a b) -> p a b", a=2)
                        pp = 2 * (p % 4)
                        nc.scalar.activation(dst[0:m, pp:pp + 2, :], b, ACT.Copy)
                        i = nc.scalar.activation(sq[0:m, p % 2], b, ACT.Square)
                        i.then_inc(bank_free[u % 2], 1)

                def root(p):
                    act.wait_ge(sum5, p + 1)
                    if p >= 2:
                        act.wait_ge(ready5, p - 1)
                    nc.scalar.activation(rs2[:, p % 2], B[2 + p % 2][:, :].rearrange("p (a b) -> p a b", a=2),
                                         ACT.Sqrt, scale=1.0 / QK, bias=eps[:, 0:1]).then_inc(root5, 1)

                for p in range(9):
                    if p < 8:
                        evac(p)
                    if p >= 1:
                        root(p - 1)
                    if p in (5, 7):
                        n = (p - 5) // 2
                        for tt in range(TT):
                            k = ("v", 2 * n + tt)
                            product_done(act, k)
                            nc.scalar.activation(v[:, tt, n * 512:(n + 1) * 512], B[use_no[k] % 2][:, :],
                                                 ACT.Copy).then_inc(bank_free[use_no[k] % 2], 1)
                att5.act(act)

            @block.vector
            def _(dve):
                step = Chain(dve, ang_step)
                dve.wait_ge(pos_in, 16)
                step(nc.vector.tensor_copy(ang, pos_i))
                step(nc.vector.tensor_scalar(ang, ang, C("inv2"), None, ALU.mult))
                step(nc.vector.tensor_scalar(turns, ang, 1 / (2 * np.pi), ROUND, ALU.mult, ALU.add))
                step(nc.vector.tensor_scalar(turns, turns, ROUND, None, ALU.subtract))
                for part in TWO_PI:
                    step(nc.vector.scalar_tensor_tensor(out=ang, in0=turns, scalar=-part, in1=ang,
                                                        op0=ALU.mult, op1=ALU.add))
                dve.wait_ge(sins, 1)
                nc.vector.tensor_tensor(cosT, sin_h, sin_h, ALU.mult).then_inc(cos_ready, 1)
                dve.wait_ge(cos_ready, 1)
                nc.vector.tensor_scalar(cosT, cosT, -2.0, 1.0, ALU.mult, ALU.add).then_inc(cos_ready, 1)
                nrm5.dve(dve)
                nc.vector.tensor_scalar(gq, par[:, pcol["q_nope"]:pcol["q_nope"] + 2], -(QK ** -0.5), None, ALU.mult)
                dve.wait_ge(kr_in, 2)
                nc.vector.tensor_scalar(krg, kr, pc("k_rope"), None, ALU.mult).then_inc(krg_in, 1)
                lstep = Chain(dve, lora_step)
                for n, (c, g) in enumerate(((cq, "q_a"), (ckv, "kv_a"))):
                    dve.wait_ge(lora_root, n + 1)
                    lstep(nc.vector.reciprocal(lrs[:, n, :], lrs[:, n, :]))
                    for k in range(2):
                        i = nc.vector.scalar_tensor_tensor(out=c[:, k, :], in0=c[:, k, :], scalar=pc(g, k),
                                                           in1=lrs[:, n, :], op0=ALU.mult, op1=ALU.mult)
                    i.then_inc(lora_ready, 1)
                dve.wait_ge(kr_rot, 1)
                dve.wait_ge(cos_ready, 2)
                nc.vector.tensor_tensor(kr_t, B[7][:, 0:S], sinT, ALU.mult)
                lstep(nc.vector.tensor_tensor(kr_base, krg, cosT, ALU.mult))
                lstep(nc.vector.tensor_tensor(kr_base, kr_base, kr_t, ALU.add))
                step = Chain(dve, step5)

                def gain(p):
                    dve.wait_ge(root5, p + 1)
                    r = rs2[:, p % 2]
                    step(nc.vector.reciprocal(r, r))
                    pp = 2 * (p % 4)
                    src, g = (qn, gq[:, 0:1]) if p < 4 else (kn, pc("k_nope"))
                    o = src[:, pp:pp + 2, :]
                    i = nc.vector.scalar_tensor_tensor(out=o, in0=o, scalar=g, in1=r, op0=ALU.mult, op1=ALU.mult)
                    if p < 4:
                        o = qr[:, pp:pp + 2, :]
                        nc.vector.scalar_tensor_tensor(out=o, in0=o, scalar=gq[:, 1:2], in1=r, op0=ALU.mult,
                                                       op1=ALU.mult).then_inc(gained, 1)
                    else:
                        nc.vector.tensor_tensor(krh[:, pp:pp + 2, :], bcast(kr_base, 1, 2), r,
                                                ALU.mult).then_inc(ready5, 1)

                def rope(p):
                    dve.wait_ge(rot5, p + 1)
                    o = qr[:, 2 * p:2 * p + 2, :]
                    nc.vector.tensor_tensor(tcos[:, p % 2], o, bcast(cosT, 1, 2), ALU.mult)
                    step(nc.vector.tensor_tensor(tsin[:, p % 2], B[4 + p % 2][:, :].rearrange("p (a b) -> p a b", a=2),
                                                 bcast(sinT, 1, 2), ALU.mult))
                    nc.vector.tensor_tensor(o, tcos[:, p % 2], tsin[:, p % 2], ALU.add).then_inc(ready5, 1)

                for p in range(9):
                    if p < 8:
                        gain(p)
                    if 1 <= p <= 4:
                        rope(p - 1)
                att5.dve(dve)
                out5_dve(dve)

        ffn(1, pc("norm_ffn", DC, DC), T["ffn1"], T["ffn1"] + NSLOT, NT)

        area = Area()
        res = area(TT, D)
        res_turned, res_in, stored = sem("result_turned"), sem("result_placed"), sem("result_stored")
        with nc.Block() as block:
            @block.tensor
            def _(pe):
                for i in range(4):
                    tt, half = i // 2, i % 2
                    for c in range(4):
                        mm = nc.tensor.transpose(B[i][:, c * P:(c + 1) * P],
                                                 x[:, 4 * half + c, tt * P:(tt + 1) * P], ident)
                    mm.then_inc(res_turned, 1)

            @block.vector
            def _(dve):
                for i in range(4):
                    dve.wait_ge(res_turned, i + 1)
                    nc.vector.tensor_copy(res[:, i // 2, (i % 2) * 512:(i % 2 + 1) * 512], B[i][:, :])\
                        .then_inc(res_in, 1)

            @block.sync
            def _(sp):
                for tt in range(TT):
                    sp.wait_ge(res_in, 2 * tt + 2)
                    sp.dma_start(out[0, tt * P:(tt + 1) * P, :], res[:, tt, :]).then_inc(stored, 16)
                sp.wait_ge(stored, 32)


_OUTS = [((1, 256, 1024), 'float32')]
_INS = ['x', 'norm_g', 'fox_w_in', 'fox_b_f', 'fox_w_out', 'nsa_w_in', 'nsa_pe_k', 'nsa_w_ck1', 'nsa_w_ck2',
        'nsa_pe_v', 'nsa_w_cv1', 'nsa_w_cv2', 'nsa_w_out', 'final_g', 'positions_2', 'norm_mix_2', 'norm_ffn_2',
        'hgrn_w_in_2', 'hgrn_lower_bounds_2', 'hgrn_out_norm_2', 'hgrn_w_out_2', 'mla_w_in_2', 'mla_q_a_norm_2',
        'mla_w_q_up_2', 'mla_kv_a_norm_2', 'mla_w_kv_up_2', 'mla_q_norm_2', 'mla_k_norm_2', 'mla_w_out_2',
        'ffn_w_up_2', 'ffn_conv_w_2', 'ffn_conv_b_2', 'ffn_w_down_2']


def kernel(**inputs):
    import numpy as _np
    import concourse.bacc as _bacc
    from concourse import mybir as _mybir
    from concourse.bass_utils import run_bass_kernel_spmd as _run

    nc = _bacc.Bacc("TRN2", target_bir_lowering=False, num_devices=1)
    arrays, args = {}, {}
    consts, at = shape_constants()
    for name, a in [(n, inputs[n]) for n in _INS] + [("consts", consts)]:
        a = _np.ascontiguousarray(a)
        arrays[f"in_{name}_dram"] = a
        args[name] = nc.dram_tensor(f"in_{name}_dram", a.shape, _mybir.dt.from_np(a.dtype), kind="ExternalInput").ap()
    outs = []
    for i, (shape, dtype) in enumerate(_OUTS):
        dt = _mybir.dt.from_np(_np.dtype(dtype))
        outs.append(nc.dram_tensor(f"out_{i}_dram", shape, dt, kind="ExternalOutput").ap())
    build(nc, args, args["consts"], outs[0], at)
    r = _run(nc, [arrays], core_ids=[0])
    return r.results[0]["out_0_dram"]
```

```python
from contextlib import ExitStack

import numpy as np

import concourse.bass as bass
from concourse import mybir

F32 = mybir.dt.float32
F32R = mybir.dt.float32r
BF16 = mybir.dt.bfloat16
I32 = mybir.dt.int32
ALU = mybir.AluOpType
ACT = mybir.ActivationFunctionType
AX = mybir.AxisListType

P = 128
D = 1024
S = 256
TT = S // P
DC = D // P
EPS = 1e-6
BIG = 1e30
LEAST = 1e-37

FOX_H, HD = 16, 64
FOX_F = 3 * D
G, CMP, STRIDE, CLEN, HID = 4, 15, 16, 32, 256
NG = G * CMP
NSA_KC, NSA_VC, NSA_KS, NSA_VS, NSA_KW, NSA_VW, NSA_GATE = [D + 256 * i for i in range(7)]
NSA_Z = NSA_GATE + 3 * FOX_H
HG_H, LEVELS = 8, 7
ML_H, NOPE, ROPE, QK, LORA = 8, 128, 64, 192, 256
FF = 2816
FC = FF // P
UNITS_PER_LOOP = 4

NSLOT = 3
SLOT = 2048
AB = 3


def shape_constants():
    p = np.arange(P)
    f = np.float32
    cols, at = [], {}

    def put(name, a):
        at[name] = (sum(c.shape[1] for c in cols), a.shape[1])
        cols.append(np.asarray(a, f))

    put("ident", np.eye(P))
    put("tri", p[:, None] <= p[None, :])
    put("ones", np.ones((P, P)))
    put("zero", np.zeros((P, P)))
    put("mask", np.where(p[None, :] > p[:, None], f(BIG), f(0)))
    end = np.arange(CMP) * STRIDE + CLEN - 1
    for t in range(TT):
        put(f"cmask{t}", np.where(end[None, :] > (p + t * P)[:, None], f(BIG), f(0)))
        put(f"cvalid{t}", (end[0] <= p + t * P)[:, None])
    half = HD // 8
    rot = np.zeros((P, P))
    for b in (0, HD):
        for d in range(half):
            rot[b + d + half, b + d] = -1.0
            rot[b + d, b + d + half] = 1.0
    put("rot", rot)
    inv = np.power(f(500000.0), -np.arange(half, dtype=f) * f(2.0 / (2 * half)))
    for name, pos in (("tok", np.arange(S)), ("cmp", np.tile(end, G))):
        ang = pos.astype(f)[None, :] * inv[:, None]
        c, s = np.ones((P, len(pos)), f), np.zeros((P, len(pos)), f)
        for b in (0, half, HD, HD + half):
            c[b:b + half], s[b:b + half] = np.cos(ang), np.sin(ang)
        put("cos_" + name, c)
        put("sin_" + name, s)
    lev, msk = [], []
    for l in range(LEVELS):
        m = 1 << l
        mid = p // (2 * m) * (2 * m) + m - 1
        up = (p & m) > 0
        a = np.where(up[None, :], (p[:, None] > mid[None, :]) & (p[:, None] <= p[None, :]),
                     (p[:, None] > p[None, :]) & (p[:, None] <= mid[None, :]))
        lev.append(a)
        msk.append((~up)[:, None] & up[None, :] & (p[:, None] // (2 * m) == p[None, :] // (2 * m)))
    before = p[:, None] > p[None, :]
    upto = p[:, None] <= p[None, :]
    rot2 = np.zeros((P, P))
    for d in range(ROPE // 2):
        rot2[d + ROPE // 2, d] = -1.0
        rot2[d, d + ROPE // 2] = 1.0
    put("rot2", rot2)
    inv2 = f(10000.0) ** (-np.arange(0, ROPE, 2, dtype=f) / f(ROPE))
    put("inv2", np.where(p < ROPE, inv2[p % (ROPE // 2)], 0)[:, None])
    put("levels", np.concatenate(lev[:4] + [before] + lev[4:] + [upto], 1))
    put("lmask", np.concatenate(msk + [np.eye(P)], 1))
    return np.ascontiguousarray(np.concatenate(cols, 1)), at


def bcast(ap, axis, n):
    a = ap.unsqueeze(axis)
    shape = list(a.shape)
    shape[axis] = n
    return a.broadcast_to(shape)


class Chain:

    def __init__(self, eng, sem):
        self.eng, self.sem, self.n = eng, sem, 0

    def __call__(self, ins):
        self.n += 1
        ins.then_inc(self.sem, 1)
        self.eng.wait_ge(self.sem, self.n)


def build(nc, A, cst_dram, out, at):
    ctx = ExitStack()
    with ctx:
        def sb(name, shape, dt=F32):
            return ctx.enter_context(nc.sbuf_tensor(name, shape, dt))

        def sem(name):
            return ctx.enter_context(nc.semaphore(name))

        B = [ctx.enter_context(nc.psum_tensor(f"bank{i}", [P, 512], F32)) for i in range(8)]
        x = sb("x", [P, DC, S])
        h = sb("h", [P, DC, S])
        h_hi, h_lo = sb("h_high", [P, DC, S], F32R), sb("h_low", [P, DC, S], F32R)
        w_hi, w_lo = sb("w_high", [P, NSLOT, SLOT], F32R), sb("w_low", [P, NSLOT, SLOT], F32R)
        ring = sb("ring", [P, NSLOT, SLOT])
        ncst = at["levels"][0]
        cst = sb("cst", [P, ncst])
        zeros_bf = sb("zeros_bf", [P, 512], BF16)
        eps = sb("eps", [P, 1])
        rstd = sb("rstd", [P, S])
        WORK = 23 * 1024 + 448
        class Memory:

            def __init__(self):
                self.ctx, self.times = ExitStack(), 0

            def open(self, less=0):
                self.ctx.close()
                self.times += 1
                self.work = self.ctx.enter_context(nc.sbuf_tensor(f"work{self.times}", [P, WORK - less], F32))

            def float32r(self, name, *dims):
                return self.ctx.enter_context(nc.sbuf_tensor(name, [P, *dims], F32R))

            def close(self):
                self.ctx.close()

        memory = Memory()

        def C(name, a=0, b=None):
            o, n = at[name]
            return cst[:, o + a:o + (n if b is None else b)]

        ident, ones = C("ident"), C("ones")

        class Area:

            def __init__(self):
                self.at = 0

            def same(self, n):
                other = Area()
                other.at = self.at - n
                return other

            def __call__(self, *dims):
                n = int(np.prod(dims))
                a = memory.work[:, self.at:self.at + n]
                self.at += n
                assert self.at <= WORK, self.at
                if len(dims) == 1:
                    return a
                names = "abcd"[:len(dims)]
                return a.rearrange(f"p ({' '.join(names)}) -> p {' '.join(names)}",
                                   **dict(zip(names, dims)))

        prows, pcol = [], {}

        def rows(name, ap, n, width=P):
            pcol[name] = len(prows)
            prows.extend((ap, i, n, width) for i in range(n))

        def vec(ap, n):
            return ap.rearrange("(r q) -> r q", q=n)

        rows("norm_g", A["norm_g"].rearrange("l (r q) -> (l r) q", q=P), 2 * DC)
        rows("final_g", vec(A["final_g"], P), DC)
        rows("norm_mix", A["norm_mix_2"].rearrange("l (r q) -> (l r) q", q=P), 2 * DC)
        rows("norm_ffn", A["norm_ffn_2"].rearrange("l (r q) -> (l r) q", q=P), 2 * DC)
        rows("hgrn_norm", A["hgrn_out_norm_2"], 1)
        rows("q_a", vec(A["mla_q_a_norm_2"][0], P), LORA // P)
        rows("kv_a", vec(A["mla_kv_a_norm_2"][0], P), LORA // P)
        for name in ("q", "k"):
            rows(name + "_nope", A[f"mla_{name}_norm_2"][:, 0:NOPE], 1)
            rows(name + "_rope", A[f"mla_{name}_norm_2"][:, NOPE:QK], 1, ROPE)
        for n in "kv":
            rows("pe_" + n, A[f"nsa_pe_{n}"][0].rearrange("(i a) d -> i (a d)", a=2), CLEN // 2)
        n_small = len(prows)
        conv_col = []
        for l in range(2):
            w = A["ffn_conv_w_2"][l].rearrange("j (r q) -> (j r) q", q=P)
            conv_col.append(n_small + 8 * FC * l)
            rows(f"conv_w{l}", w, 6 * FC)
            rows(f"conv_b{l}", vec(A["ffn_conv_b_2"][l], P), 2 * FC)
        NPAR = len(prows)
        par = sb("par", [P, NPAR])
        ctx.callback(memory.close)
        memory.open()

        def pc(name, i=0, n=1):
            return par[:, pcol[name] + i:pcol[name] + i + n]

        tiles = []

        def wtiles(w, c0, width, step=256, kc=DC):
            a = w.rearrange("(c p) n -> p c n", p=P)
            first = len(tiles)
            for c in range(c0, c0 + width, step):
                tiles.append((a[:, :, c:c + step], kc, step))
            return first

        T = {}
        fw = A["fox_w_in"][0]
        T["fox_q"] = wtiles(fw, 0, D)
        T["fox_k"] = wtiles(fw, D, D)
        T["fox_v"] = wtiles(fw, 2 * D, D)
        T["fox_z"] = wtiles(fw, FOX_F + FOX_H, D)
        T["fox_out"] = wtiles(A["fox_w_out"][0], 0, D)
        nw = A["nsa_w_in"][0]
        T["nsa_in"] = wtiles(nw, D, 6 * 256)
        ck = []
        for n, name in enumerate(("nsa_w_ck1", "nsa_w_cv1")):
            a = A[name][0].rearrange("(i p) n -> p i n", p=P)
            ck.append(len(tiles))
            for b in range(2):
                tiles.append((a[:, 8 * b:8 * b + 8, :], 8, HID))
        T["nsa_q"] = wtiles(nw, 0, D)
        T["nsa_z"] = wtiles(nw, NSA_Z, D)
        T["nsa_out"] = wtiles(A["nsa_w_out"][0], 0, D)
        hw = A["hgrn_w_in_2"][0]
        T["hgrn_f"] = wtiles(hw, D, D)
        T["hgrn_q"] = wtiles(hw, 0, D)
        T["hgrn_i"] = wtiles(hw, 2 * D, D)
        T["hgrn_g"] = wtiles(hw, 3 * D, D)
        T["hgrn_out"] = wtiles(A["hgrn_w_out_2"][0], 0, D)

        def ffn_tiles(l):
            up = A["ffn_w_up_2"][l].rearrange("(c p) (e n) -> p e c n", p=P, e=2)
            down = A["ffn_w_down_2"][l].rearrange("(c p) n -> p c n", p=P)
            first = len(tiles)
            for j in range(2):
                tiles.append(("up", up, j))
            for g in range(10):
                tiles.append(("up", up, 2 * g + 2))
                tiles.append(("up", up, 2 * g + 3))
                tiles.append(("down", down, g))
            tiles.append(("down", down, 10))
            return first

        T["ffn0"] = ffn_tiles(0)
        mw = A["mla_w_in_2"][0]
        T["mla_in"] = wtiles(mw, 0, 2 * LORA)
        T["mla_q"] = wtiles(A["mla_w_q_up_2"][0], 0, ML_H * QK, step=4 * QK, kc=2)
        T["mla_kv"] = wtiles(A["mla_w_kv_up_2"][0], 0, ML_H * 256, step=1024, kc=2)
        T["mla_out"] = wtiles(A["mla_w_out_2"][0], 0, D)
        T["ffn1"] = ffn_tiles(1)
        NT = len(tiles)

        def slot(t, kc, n):
            return ring[:, t % NSLOT, 0:kc * n].rearrange("p (k n) -> p k n", k=kc)

        w_loaded = [sem(f"w_loaded{i}") for i in range(NSLOT)]
        high_in = [sem(f"w_high_ready{i}") for i in range(NSLOT)]
        low_in = [sem(f"w_low_ready{i}") for i in range(NSLOT)]
        tile_done = sem("tile_done")
        bank_free = [sem(f"bank_free{i}") for i in range(2)]

        def load(sp, t):
            if t >= NT:
                return
            if t >= NSLOT:
                sp.wait_ge(low_in[t % NSLOT], t // NSLOT)
            src = tiles[t]
            s = w_loaded[t % NSLOT]
            if src[0] == "up":
                sp.dma_start(up_slot(t), src[1][:, :, :, src[2] * P:(src[2] + 1) * P]).then_inc(s, 16)
            elif src[0] == "down":
                sp.dma_start(slot(t, 2, D), src[1][:, 2 * src[2]:2 * src[2] + 2, :]).then_inc(s, 16)
            else:
                sp.dma_start(slot(t, src[1], src[2]), src[0]).then_inc(s, 16)

        def up_slot(t):
            return ring[:, t % NSLOT, :].rearrange("p (e c n) -> p e c n", e=2, c=DC)

        def landed(eng, t, later=0):
            eng.wait_ge(w_loaded[t % NSLOT], later * 32 + 16 * (t // NSLOT + 1))

        def high(act, t, later=0, ops=None):
            if t >= NT:
                return
            landed(act, t, later)
            if t >= NSLOT:
                act.wait_ge(tile_done, later * 6 + t - NSLOT + 1)
            dst, src = w_hi[:, t % NSLOT, :], ring[:, t % NSLOT, :]
            if ops is None:
                i = nc.scalar.activation(dst, src, ACT.Copy)
            else:
                i = ops.tensor_copy(dst, src)
            i.then_inc(high_in[t % NSLOT], 1)

        def low(eng, ops, t, later=0):
            if t >= NT:
                return
            eng.wait_ge(high_in[t % NSLOT], later * 2 + t // NSLOT + 1)
            ops.tensor_tensor(w_lo[:, t % NSLOT, :], ring[:, t % NSLOT, :], w_hi[:, t % NSLOT, :].bitcast(F32),
                              ALU.subtract).then_inc(low_in[t % NSLOT], 1)

        def in_parts(eng, t, later=0):
            eng.wait_ge(low_in[t % NSLOT], later * 2 + t // NSLOT + 1)

        def parts(t, pattern, **dims):
            n = int(np.prod(list(dims.values())))
            return [r[:, t % NSLOT, 0:n].rearrange(pattern, **dims) for r in (w_hi, w_lo)]

        def product3(o, a, b, start, stop, **kw):
            (ah, al), (bh, bl) = a, b
            nc.tensor.matmul(o, ah, bh, start=start, stop=False, **kw)
            nc.tensor.matmul(o, ah, bl, start=False, stop=False, **kw)
            return nc.tensor.matmul(o, al, bh, start=False, stop=stop, **kw)

        high_step, act_split = sem("high_step"), sem("activations_split")
        steps_taken = {"n": 0}

        def split_chunk(pool, c, src, wait):
            wait()
            steps_taken["n"] += 1
            nc.gpsimd.tensor_copy(h_hi[:, c, :], src[:, c, :]).then_inc(high_step, 1)
            pool.wait_ge(high_step, steps_taken["n"])
            nc.gpsimd.tensor_tensor(h_lo[:, c, :], src[:, c, :], h_hi[:, c, :].bitcast(F32),
                                    ALU.subtract).then_inc(act_split, 1)

        hsp = (h_hi, h_lo)

        turn = {"n": 0}
        bank_of = {}

        def plan_tile(t):
            bank_of[t] = turn["n"]
            turn["n"] += 1

        def pbank(t):
            return B[bank_of[t] % 2]

        def wait_bank(pe, t):
            u = bank_of[t]
            if u >= 2:
                pe.wait_ge(bank_free[u % 2], u // 2)

        def freed(t):
            return bank_free[bank_of[t] % 2]

        def evacuated(eng, t):
            eng.wait_ge(freed(t), bank_of[t] // 2 + 1)

        def by_feature(pe, t, act, ready=None):
            in_parts(pe, t)
            wait_bank(pe, t)
            w = parts(t, "p (c n) -> p c n", c=DC, n=256)
            for j in range(2):
                for c in range(DC):
                    if ready is not None and j == 0:
                        ready(c)
                    mm = product3(pbank(t)[:, j * S:(j + 1) * S], [v[:, c, j * P:(j + 1) * P] for v in w],
                                  [v[:, c, :] for v in act], c == 0, c == DC - 1)
            mm.then_inc(tile_done, 1)

        def by_token(pe, t, act, ready=None):
            in_parts(pe, t)
            wait_bank(pe, t)
            w = parts(t, "p (c n) -> p c n", c=DC, n=256)
            for tt in range(TT):
                for c in range(DC):
                    if ready is not None and tt == 0:
                        ready(c)
                    mm = product3(pbank(t)[:, tt * 256:(tt + 1) * 256], [v[:, c, tt * P:(tt + 1) * P] for v in act],
                                  [v[:, c, :] for v in w], c == 0, c == DC - 1)
            mm.then_inc(tile_done, 1)

        def bank2(t):
            return pbank(t)[:, :].rearrange("p (a b) -> p a b", a=2)

        norms = {"n": 0, "split": 0}
        sq_act, sq_dve = sem("squares_act"), sem("squares_dve")
        n_summed, n_root, n_inv = sem("norm_summed"), sem("norm_root"), sem("norm_inverse")
        n_ready = sem("norm_ready")
        n_high, n_split = sem("norm_high_ready"), sem("norm_split")

        class Norm:

            def __init__(self, gain, dst=None, after=None, split=None, sq=None):
                self.split = split
                self.after = after
                self.n = norms["n"]
                norms["n"] += 1
                self.gain, self.dst = gain, h if dst is None else dst
                self.sq = sq
                if split is not None:
                    self.s = DC * norms["split"]
                    norms["split"] += 1

            def act(self, act, meanwhile=None):
                if self.after:
                    self.after.wait(act, DC)
                for c in range(0, 4, 2):
                    nc.scalar.activation(self.sq[:, c:c + 2, :], x[:, c:c + 2, :], ACT.Square).then_inc(sq_act, 1)
                if meanwhile is not None:
                    high(act, meanwhile)
                act.wait_ge(n_summed, self.n + 1)
                nc.scalar.activation(rstd[:, :], B[7][:, 0:S], ACT.Sqrt, scale=1.0 / D,
                                     bias=eps[:, 0:1]).then_inc(n_root, 1)

            def act_split(self, act):
                for c in range(DC):
                    self.wait(act, c + 1)
                    nc.scalar.activation(self.split[0][:, c, :], self.dst[:, c, :], ACT.Copy).then_inc(n_high, 1)

            def low(self, dve, c):
                dve.wait_ge(n_high, self.s + c + 1)
                nc.vector.tensor_tensor(self.split[1][:, c, :], self.dst[:, c, :],
                                        self.split[0][:, c, :].bitcast(F32), ALU.subtract).then_inc(n_split, 1)

            def dve(self, dve, meanwhile=None):
                if self.after:
                    self.after.wait(dve, DC)
                for c in range(4, DC, 2):
                    nc.vector.tensor_tensor(self.sq[:, c:c + 2, :], x[:, c:c + 2, :], x[:, c:c + 2, :],
                                            ALU.mult).then_inc(sq_dve, 1)
                if meanwhile is not None:
                    high(dve, meanwhile, ops=nc.vector)
                dve.wait_ge(n_root, self.n + 1)
                nc.vector.reciprocal(rstd[:, :], rstd[:, :]).then_inc(n_inv, 1)
                dve.wait_ge(n_inv, self.n + 1)
                for c in range(DC):
                    nc.vector.scalar_tensor_tensor(out=self.dst[:, c, :], in0=x[:, c, :],
                                                   scalar=self.gain[:, c:c + 1], in1=rstd[:, :],
                                                   op0=ALU.mult, op1=ALU.mult).then_inc(n_ready, 1)
                    if self.split and c >= 2:
                        self.low(dve, c - 2)
                if self.split:
                    self.low(dve, DC - 2)
                    self.low(dve, DC - 1)

            def pe(self, pe):
                order = [0, 1, 4, 5, 2, 3, 6, 7]
                for n, c in enumerate(order):
                    if c < 4:
                        pe.wait_ge(sq_act, 2 * self.n + c // 2 + 1)
                    else:
                        pe.wait_ge(sq_dve, 2 * self.n + c // 2 - 1)
                    mm = nc.tensor.matmul(B[7][:, 0:S], ones, self.sq[:, c, :], start=(n == 0), stop=(n == DC - 1))
                mm.then_inc(n_summed, 1)

            def wait(self, eng, chunks):
                eng.wait_ge(n_ready, DC * self.n + chunks)

            def chunk(self, pe):
                if self.split:
                    return lambda c: pe.wait_ge(n_split, self.s + c + 1)
                return lambda c: self.wait(pe, c + 1)

        before = {"units": 0, "groups": 0}
        a_multiplied, a_biased, a_exped = sem("logits_ready"), sem("logits_biased"), sem("weights_exped")
        a_inv, a_scaled, a_turned = sem("sums_inverted"), sem("weights_scaled"), sem("weights_turned")
        a_copied, a_weighed, a_taken = sem("weights_copied"), sem("values_weighed"), sem("output_taken")

        class Attention:

            def __init__(self, area, units, groups, take):
                self.units, self.groups, self.take = units, groups, take
                self.u0, self.g0 = before["units"], before["groups"]
                before["units"] += len(units)
                before["groups"] += groups
                n = len(units)
                self.least, self.sum, self.rsum = area(n, 2), area(n, 2), area(n, 2)
                self.lb, self.pb, self.pt = [area(AB, 512) for _ in range(3)]
                self.last_unit = {}
                for u, unit in enumerate(units):
                    self.last_unit[unit["group"]] = u

            def view(self, buf, u):
                unit = self.units[u]
                if buf is None:
                    return B[2 + u % 2][:, 0:unit["nh"] * unit["w"]].rearrange("p (e k) -> p e k", e=unit["nh"])
                return buf[:, u % AB, 0:unit["nh"] * unit["w"]].rearrange("p (e k) -> p e k", e=unit["nh"])

            def pview(self, u):
                unit = self.units[u]
                if unit.get("pb") is not None:
                    return unit["pb"]
                return self.view(self.pb, u)

            def logits(self, pe, u):
                unit = self.units[u]
                if u >= 2:
                    pe.wait_ge(a_biased, self.u0 + u - 1)
                n = len(unit["qk"])
                o = self.view(None, u)
                for i, (q, k) in enumerate(unit["qk"]):
                    mm = nc.tensor.matmul(o, q, k, start=(i == 0), stop=(i == n - 1))
                mm.then_inc(a_multiplied, 1)

            def bias(self, dve, u):
                unit = self.units[u]
                dve.wait_ge(a_multiplied, self.u0 + u + 1)
                if u >= AB:
                    dve.wait_ge(a_exped, self.u0 + u - AB + 1)
                ps, lb = self.view(None, u), self.view(self.lb, u)
                for e in range(unit["nh"]):
                    i = nc.vector.tensor_tensor_reduce(out=lb[:, e, :], in0=ps[:, e, :], in1=unit["bias"][e],
                                                       scale=1.0, scalar=3e38, op0=ALU.add, op1=ALU.min,
                                                       accum_out=self.least[:, u, e:e + 1])
                i.then_inc(a_biased, 1)

            def exp(self, act, u):
                unit = self.units[u]
                act.wait_ge(a_biased, self.u0 + u + 1)
                if u >= AB:
                    act.wait_ge(a_turned, self.u0 + u - AB + 1)
                lb, pb = self.view(self.lb, u), self.pview(u)
                for e in range(unit["nh"]):
                    i = nc.scalar.activation(pb[:, e, 0:unit["w"]], lb[:, e, :], ACT.Exp, scale=-1.0,
                                             bias=self.least[:, u, e:e + 1],
                                             accum_out=self.sum[:, u, e:e + 1])
                i.then_inc(a_exped, 1)

            def scale(self, dve, u):
                unit = self.units[u]
                dve.wait_ge(a_exped, self.u0 + u + 1)
                nh = unit["nh"]
                nc.vector.reciprocal(self.rsum[:, u, 0:nh], self.sum[:, u, 0:nh]).then_inc(a_inv, 1)
                dve.wait_ge(a_inv, self.u0 + u + 1)
                pb = self.pview(u)
                for e in range(nh):
                    w = pb[:, e, 0:unit["w"]]
                    if unit.get("gate") is None:
                        i = nc.vector.tensor_scalar(w, w, self.rsum[:, u, e:e + 1], None, ALU.mult)
                    else:
                        i = nc.vector.tensor_scalar(w, w, self.rsum[:, u, e:e + 1], unit["gate"][e],
                                                    ALU.mult, ALU.mult)
                i.then_inc(a_scaled, 1)

            def turn(self, pe, u):
                unit = self.units[u]
                pe.wait_ge(a_scaled, self.u0 + u + 1)
                if u >= 2:
                    pe.wait_ge(a_copied, self.u0 + u - 1)
                pb = self.pview(u)
                for i in range(unit["nh"] * unit["nkt"]):
                    e, kt = i // unit["nkt"], i % unit["nkt"]
                    mm = nc.tensor.transpose(B[4 + u % 2][:, i * P:(i + 1) * P],
                                             pb[:, e, kt * P:(kt + 1) * P], ident)
                mm.then_inc(a_turned, 1)

            def copy(self, act, u):
                unit = self.units[u]
                act.wait_ge(a_turned, self.u0 + u + 1)
                if u >= AB:
                    act.wait_ge(a_weighed, self.u0 + u - AB + 1)
                n = unit["nh"] * unit["nkt"] * P
                nc.scalar.activation(self.pt[:, u % AB, 0:n], B[4 + u % 2][:, 0:n], ACT.Copy).then_inc(a_copied, 1)

            def weigh(self, pe, u):
                unit = self.units[u]
                pe.wait_ge(a_copied, self.u0 + u + 1)
                g = unit["group"]
                if unit["first"] and g >= 2:
                    pe.wait_ge(a_taken, self.g0 + g - 1)
                o = B[6 + g % 2]
                rows_e = P // unit["nh"]
                c0 = unit["qt"] * P
                for e in range(unit["nh"]):
                    for kt in range(unit["nkt"]):
                        i = e * unit["nkt"] + kt
                        mm = nc.tensor.matmul(o[e * rows_e:(e + 1) * rows_e, c0:c0 + P], unit["v"](e, kt),
                                              self.pt[:, u % AB, i * P:(i + 1) * P],
                                              start=(unit["open"] and kt == 0),
                                              stop=(unit["close"] and kt == unit["nkt"] - 1))
                mm.then_inc(a_weighed, 1)

            def out(self, dve, g):
                dve.wait_ge(a_weighed, self.u0 + self.last_unit[g] + 1)
                self.take(g, B[6 + g % 2][:, 0:S]).then_inc(a_taken, 1)

            def chunk(self, pe):
                return lambda c: pe.wait_ge(a_taken, self.g0 + c + 1)

            def split(self, pool, src):
                for c in range(DC):
                    split_chunk(pool, c, src, lambda: pool.wait_ge(a_taken, self.g0 + c + 1))

            def pe(self, pe):
                n = len(self.units)
                for u in range(n + 3):
                    if u < n:
                        self.logits(pe, u)
                    if 2 <= u <= n + 1:
                        self.turn(pe, u - 2)
                    if u >= 3:
                        self.weigh(pe, u - 3)

            def act(self, act):
                n = len(self.units)
                for u in range(n + 2):
                    if u < n:
                        self.exp(act, u)
                    if u >= 2:
                        self.copy(act, u - 2)

            def dve(self, dve):
                n = len(self.units)
                ends = {u: g for g, u in self.last_unit.items()}
                for u in range(n + 4):
                    if u < n:
                        self.bias(dve, u)
                    if 1 <= u <= n:
                        self.scale(dve, u - 1)
                    if u - 4 in ends:
                        self.out(dve, ends[u - 4])

        projected = {"n": 0}

        def project_out(t0):
            for t in range(t0, t0 + 4):
                plan_tile(t)
            n0 = projected["n"]
            projected["n"] += DC

            def pe(pe):
                for t in range(t0, t0 + 4):
                    by_feature(pe, t, hsp, ready=(lambda c: pe.wait_ge(act_split, n0 + c + 1)) if t == t0 else None)

            def dve(dve):
                for i, t in enumerate(range(t0, t0 + 4)):
                    dve.wait_ge(tile_done, t + 1)
                    xs = x[:, 2 * i:2 * i + 2, :]
                    nc.vector.tensor_tensor(xs, bank2(t), xs, ALU.add).then_inc(freed(t), 1)
            return pe, dve

        tapped, convolved, gated = sem("ffn_tapped"), sem("ffn_convolved"), sem("ffn_gated")
        hidden, conv_step = sem("ffn_hidden_ready"), sem("ffn_conv_step")
        product, hidden_high = sem("ffn_hidden_product"), sem("ffn_hidden_high")

        def ffn(l, gain, t0, sp_from, sp_to):
            mem = ExitStack()

            def buf(name, *dims, dt=F32):
                return mem.enter_context(nc.sbuf_tensor(f"ffn{l}_{name}", [P, *dims], dt))

            memory.close()
            act_hi, act_lo = buf("hidden_high", FC, S, dt=F32R), buf("hidden_low", FC, S, dt=F32R)
            y, sg, hid32 = buf("conv", 2, 2, S), buf("gate", 2, S), buf("hidden", 2, S)
            nrm = Norm(gain, split=(h_hi, h_lo), sq=buf("squares", DC, S))
            NTILE = 33
            p0 = l * FC
            u0 = turn["n"]
            turn["n"] += FC
            cw, cb = pcol[f"conv_w{l}"], pcol[f"conv_b{l}"]
            NLOOP = 5

            def column(base, e, j, later):
                c = base + e * FC + j
                return par[:, c:c + 1] if isinstance(later, int) else par[:, bass.ds(later * 4 + c, 1)]

            def pair_tile(j):
                return t0 + (j if j < 2 else 2 + (j - 2) // 2 * 3 + (j - 2) % 2)

            def pair(pe, j, later=0, ready=None):
                t, u = pair_tile(j), u0 + j
                in_parts(pe, t, later)
                if u >= 2:
                    pe.wait_ge(bank_free[u % 2], later * 2 + u // 2)
                w = parts(t, "p (e c n) -> p e c n", e=2, c=DC, n=P)
                for e in range(2):
                    for c in range(DC):
                        if ready and e == 0:
                            ready(c)
                        mm = product3(B[u % 2][:, e * S:(e + 1) * S], [v[:, e, c, :] for v in w],
                                      [v[:, c, :] for v in (h_hi, h_lo)], c == 0, c == DC - 1)
                mm.then_inc(tile_done, 1)

            def step_down(pe, g, later=0, last=False):
                t = t0 + 4 + 3 * g if g < 10 else t0 + 32
                in_parts(pe, t, later)
                pe.wait_ge(hidden, p0 + later * 4 + 2 * g + 2)
                w = parts(t, "p (k n) -> p k n", k=2, n=D)
                for k in range(2):
                    c = 2 * g + k
                    a = [v[:, c, :] if isinstance(later, int) else v[:, bass.ds(later * 4 + c, 1), :]
                         for v in (act_hi, act_lo)]
                    for o in range(DC):
                        mm = product3(B[4 + o // 2][:, (o % 2) * S:(o % 2 + 1) * S],
                                      [v[:, k, o * P:(o + 1) * P] for v in w], a, False, last and k == 1,
                                      skip_group_check=True)
                mm.then_inc(tile_done, 1)

            def tap(act, j, later=0):
                t, u = pair_tile(j), u0 + j
                act.wait_ge(tile_done, later * 6 + t + 1)
                if not (isinstance(later, int) and j < 2):
                    act.wait_ge(hidden, p0 + later * 4 + j - 1)
                for e in range(2):
                    i = nc.scalar.activation(y[:, j % 2, e, :], B[u % 2][:, e * S:(e + 1) * S], ACT.Identity,
                                             scale=column(cw + 4 * FC, e, j, later),
                                             bias=column(cb, e, j, later))
                i.then_inc(tapped, 1)

            def gate(act, j, later=0):
                act.wait_ge(convolved, p0 + later * 4 + j + 1)
                nc.scalar.activation(sg[:, j % 2, :], y[:, j % 2, 0, :], ACT.Silu).then_inc(gated, 1)

            def convolve(dve, j, later=0):
                u = u0 + j
                dve.wait_ge(tapped, p0 + later * 4 + j + 1)
                for back in (1, 2):
                    for e in range(2):
                        dst = y[:, j % 2, e, back:S]
                        i = nc.vector.scalar_tensor_tensor(
                            out=dst, in0=B[u % 2][:, e * S:(e + 1) * S - back],
                            scalar=column(cw + (2 - back) * 2 * FC, e, j, later), in1=dst,
                            op0=ALU.mult, op1=ALU.add)
                        if back == 1:
                            i.then_inc(conv_step, 1)
                        elif e == 0:
                            i.then_inc(convolved, 1)
                        else:
                            i.then_inc(bank_free[u % 2], 1)
                    if back == 1:
                        dve.wait_ge(conv_step, 2 * p0 + later * 8 + 2 * j + 2)

            def multiply(dve, j, later=0):
                u = u0 + j
                dve.wait_ge(gated, p0 + later * 4 + j + 1)
                dve.wait_ge(bank_free[u % 2], later * 2 + u // 2 + 1)
                ah, al = [v[:, j, :] if isinstance(later, int) else v[:, bass.ds(later * 4 + j, 1), :].squeeze(1)
                          for v in (act_hi, act_lo)]
                a = hid32[:, j % 2, :]
                nc.vector.tensor_tensor(a, sg[:, j % 2, :], y[:, j % 2, 1, :], ALU.mult).then_inc(product, 1)
                dve.wait_ge(product, p0 + later * 4 + j + 1)
                nc.vector.tensor_copy(ah, a).then_inc(hidden_high, 1)
                dve.wait_ge(hidden_high, p0 + later * 4 + j + 1)
                nc.vector.tensor_tensor(al, a, ah.bitcast(F32), ALU.subtract).then_inc(hidden, 1)
                dve.wait_ge(hidden, p0 + later * 4 + j + 1)

            def load_ffn(sp, off, later=0):
                t = t0 + off
                sp.wait_ge(low_in[t % NSLOT], later * 2 + t // NSLOT)
                kind, src, n = tiles[t]
                s = w_loaded[t % NSLOT]
                if kind == "up":
                    sp.dma_start(up_slot(t), src[:, :, :, bass.ds(later * (4 * P) + n * P, P)]).then_inc(s, 16)
                else:
                    sp.dma_start(slot(t, 2, D), src[:, bass.ds(later * 4 + 2 * n, 2), :]).then_inc(s, 16)

            with nc.Block() as block:
                @block.sync
                def _(sp):
                    for t in range(sp_from, t0 + 5):
                        load(sp, t)
                    with sp.Fori(0, 4) as i:
                        for off in range(5, 11):
                            load_ffn(sp, off, i)
                    for t in range(t0 + 29, sp_to):
                        load(sp, t)

                @block.tensor
                def _(pe):
                    nrm.pe(pe)
                    for b in range(4, 8):
                        if b == 7:
                            pe.wait_ge(n_root, nrm.n + 1)
                        nc.tensor.matmul(B[b][:, :], zeros_bf[:, 0:P], zeros_bf[:, :], start=True, stop=False,
                                         skip_group_check=True)
                    pair(pe, 0, ready=nrm.chunk(pe))
                    pair(pe, 1)
                    with pe.Fori(0, NLOOP) as i:
                        for g in range(2):
                            pair(pe, 2 * g + 2, i)
                            pair(pe, 2 * g + 3, i)
                            step_down(pe, g, i)
                    step_down(pe, 10, last=True)

                @block.gpsimd
                def _(pool):
                    for j in range(4):
                        low(pool, nc.gpsimd, pair_tile(j))
                    with pool.Fori(0, 4) as i:
                        for r in range(4):
                            low(pool, nc.gpsimd, pair_tile(4 + r), i)
                    for j in (FC - 2, FC - 1):
                        low(pool, nc.gpsimd, pair_tile(j))

                @block.scalar
                def _(act):
                    nrm.act(act, meanwhile=t0)
                    nrm.act_split(act)
                    high(act, t0 + 2)
                    tap(act, 0)
                    high(act, t0 + 3)
                    tap(act, 1)
                    high(act, t0 + 4)
                    gate(act, 0)

                    def high_ahead(act, off, later):
                        if off < NTILE:
                            high(act, t0 + off, later)

                    def two_pairs(r, off, later=0):
                        tap(act, r, later)
                        high_ahead(act, off, later)
                        gate(act, r - 1, later)
                        tap(act, r + 1, later)
                        high_ahead(act, off + 1, later)
                        gate(act, r, later)
                        high_ahead(act, off + 2, later)

                    with act.Fori(0, NLOOP - 1) as i:
                        for g in range(2):
                            two_pairs(2 + 2 * g, 5 + 3 * g, i)
                    for g in range(2):
                        two_pairs(18 + 2 * g, 29 + 3 * g)
                    gate(act, FC - 1)

                @block.vector
                def _(dve):
                    nrm.dve(dve, meanwhile=t0 + 1)
                    convolve(dve, 0)
                    convolve(dve, 1)
                    low(dve, nc.vector, t0 + 4)
                    multiply(dve, 0)

                    def two_pairs(r, off, later=0):
                        for k in range(2):
                            convolve(dve, r + k, later)
                            multiply(dve, r + k - 1, later)
                        if off < NTILE:
                            low(dve, nc.vector, t0 + off, later)

                    with dve.Fori(0, NLOOP - 1) as i:
                        for g in range(2):
                            two_pairs(2 + 2 * g, 7 + 3 * g, i)
                    two_pairs(18, 31)
                    two_pairs(20, 32)
                    multiply(dve, FC - 1)
                    dve.wait_ge(tile_done, t0 + 33)
                    for o in range(4):
                        xs = x[:, 2 * o:2 * o + 2, :]
                        nc.vector.tensor_tensor(xs, B[4 + o][:, :].rearrange("p (a b) -> p a b", a=2), xs, ALU.add)
            mem.close()

        area = Area()
        x_tok = area(TT, D)
        prow = [area(P) for _ in range(6)]
        groups = [(0, n_small)] + [(n_small + 88 * i, 88) for i in range(4)]
        loaded_c, loaded_c2 = sem("constants_loaded"), sem("late_constants_loaded")
        loaded_x, loaded_p = sem("x_loaded"), sem("params_loaded")
        cleared, x_turned, x_placed = sem("cleared"), sem("x_turned"), sem("x_placed")
        p_turned = sem("params_turned")
        n_pdma = []
        with nc.Block() as block:
            @block.sync
            def _(sp):
                sp.dma_start(x_tok, A["x"][0].rearrange("(t p) d -> p t d", p=P)).then_inc(loaded_x, 16)
                sp.dma_start(cst[:, 0:640], cst_dram[:, 0:640]).then_inc(loaded_c, 16)
                for t in range(NSLOT):
                    load(sp, t)
                sp.dma_start(cst[:, 640:], cst_dram[:, 640:ncst]).then_inc(loaded_c2, 16)

            @block.gpsimd
            def _(pool):
                nc.gpsimd.memset(prow[0], 0.0).then_inc(cleared, 1)
                nc.gpsimd.memset(zeros_bf[:, :], 0.0)
                nc.gpsimd.memset(eps[:, :], EPS).then_inc(cleared, 1)

            @block.scalar
            def _(act):
                act.wait_ge(cleared, 1)
                n = 0
                for g, (r0, count) in enumerate(groups):
                    r = r0
                    while r < r0 + count:
                        ap, i, total, width = prows[r]
                        m = min(total - i, r0 + count - r)
                        act.dma_start(prow[g][r - r0:r - r0 + m, 0:width], ap[i:i + m, :]).then_inc(loaded_p, 16)
                        r += m
                        n += 1
                n_pdma.append(n)

            @block.tensor
            def _(pe):
                pe.wait_ge(loaded_x, 16)
                pe.wait_ge(loaded_c, 16)
                for c in range(DC):
                    for tt in range(TT):
                        mm = nc.tensor.transpose(B[c // 2][:, (c % 2) * S + tt * P:(c % 2) * S + (tt + 1) * P],
                                                 x_tok[:, tt, c * P:(c + 1) * P], ident)
                    if c % 2:
                        mm.then_inc(x_turned, 1)
                pe.wait_ge(loaded_p, 16 * n_pdma[0])
                for g, (r0, count) in enumerate(groups):
                    mm = nc.tensor.transpose(B[4][:, r0:r0 + count], prow[g][0:count, :],
                                             ident[0:count, 0:count])
                mm.then_inc(p_turned, 1)

            @block.vector
            def _(dve):
                for i in range(4):
                    dve.wait_ge(x_turned, i + 1)
                    nc.vector.tensor_copy(x[:, 2 * i:2 * i + 2, :],
                                          B[i][:, :].rearrange("p (a b) -> p a b", a=2)).then_inc(x_placed, 1)
                dve.wait_ge(p_turned, 1)
                for g, (r0, count) in enumerate(groups):
                    nc.vector.tensor_copy(par[:, r0:r0 + count], B[4][:, r0:r0 + count])

        memory.open()
        area = Area()
        w_f = area(DC, FOX_H)
        b_f = area(FOX_H)
        f_raw, f_abs, f_exp, f_log = [area(TT * FOX_H) for _ in range(4)]
        logf = area(TT, FOX_H)
        c_q = area(TT, FOX_H)
        qT = area(DC, S)
        zT = h
        kz = area(FOX_H, S)
        v = area(TT, D)
        cm0, cm1 = area(FOX_H, P), area(FOX_H, S)
        nrm = Norm(pc("norm_g", 0, DC), split=hsp, sq=qT)
        fl, fps = sem("fox_f_loaded"), sem("fox_f_product")
        f_steps, f_steps_a = sem("fox_f_steps"), sem("fox_f_act")
        logf_ready, cq_ps, cq_ready = sem("logf_ready"), sem("c_q_product"), sem("c_q_ready")
        ck_ps, ck_used = sem("c_k_product"), sem("c_k_used")
        kz_clear = sem("fox_keys_clear")
        fq, fk, fv, fz = T["fox_q"], T["fox_k"], T["fox_v"], T["fox_z"]
        for t in range(fq, fz + 4):
            plan_tile(t)

        def masks(qt):
            o, n = at["zero"]
            return cst[:, o:o + S] if qt else C("mask")

        units = []
        for c in range(DC):
            for qt in range(TT):
                w = (qt + 1) * P
                cm = (cm0, cm1)[qt]
                units.append(dict(
                    group=c, qt=qt, nh=2, w=w, nkt=qt + 1, first=(qt == 0), open=True, close=True,
                    qk=[(qT[:, c, qt * P:(qt + 1) * P], kz[:, 2 * c:2 * c + 2, 0:w])],
                    bias=[cm[:, 2 * c + e, :] for e in range(2)],
                    v=lambda e, kt, c=c: v[:, kt, (2 * c + e) * HD:(2 * c + e + 1) * HD]))
        att = Attention(area, units, DC,
                        lambda g, ps: nc.vector.tensor_tensor(zT[:, g, :], ps, zT[:, g, :], ALU.mult))
        out_pe, out_dve = project_out(T["fox_out"])

        with nc.Block() as block:
            @block.sync
            def _(sp):
                sp.dma_start(w_f, fw.rearrange("(c p) n -> p c n", p=P)[:, :, FOX_F:FOX_F + FOX_H]).then_inc(fl, 16)
                sp.dma_start(b_f, A["fox_b_f"].broadcast_to([P, FOX_H])).then_inc(fl, 16)
                for t in range(NSLOT, T["fox_out"] + 4 + NSLOT):
                    load(sp, t)

            @block.gpsimd
            def _(pool):
                low(pool, nc.gpsimd, fq)
                low(pool, nc.gpsimd, fq + 1)
                nc.gpsimd.memset(kz, 0.0).then_inc(kz_clear, 1)
                for t in range(fq + 2, T["fox_out"] + 3):
                    low(pool, nc.gpsimd, t)
                att.split(pool, zT)
                low(pool, nc.gpsimd, T["fox_out"] + 3)

            @block.tensor
            def _(pe):
                nrm.pe(pe)
                pe.wait_ge(fl, 32)
                for tt in range(TT):
                    for c in range(DC):
                        if tt == 0:
                            nrm.wait(pe, c + 1)
                        mm = nc.tensor.matmul(B[6][:, tt * FOX_H:(tt + 1) * FOX_H], h[:, c, tt * P:(tt + 1) * P],
                                              w_f[:, c, :], start=(c == 0), stop=(c == DC - 1))
                mm.then_inc(fps, 1)
                for t in range(fq, fq + 4):
                    by_feature(pe, t, hsp, ready=nrm.chunk(pe) if t == fq else None)
                pe.wait_ge(logf_ready, 1)
                nc.tensor.matmul(B[6][:, 0:FOX_H], C("tri"), logf[:, 0, :], start=True, stop=True)
                nc.tensor.matmul(B[6][:, FOX_H:2 * FOX_H], ones, logf[:, 0, :], start=True, stop=False)
                nc.tensor.matmul(B[6][:, FOX_H:2 * FOX_H], C("tri"), logf[:, 1, :], start=False,
                                 stop=True).then_inc(cq_ps, 1)
                tri_ones = cst[:, at["tri"][0]:at["tri"][0] + S]
                for n in range(FOX_H):
                    if n >= 2:
                        pe.wait_ge(ck_used, n - 1)
                    o = B[4 + n % 2]
                    nc.tensor.matmul(o[:, 0:S], logf[:, 0, n:n + 1].broadcast_to([P, P]), tri_ones,
                                     start=True, stop=False)
                    nc.tensor.matmul(o[:, P:S], logf[:, 1, n:n + 1].broadcast_to([P, P]), C("tri"),
                                     start=False, stop=True).then_inc(ck_ps, 1)
                    if n % 4 == 3:
                        by_feature(pe, fk + n // 4, hsp)
                for t in range(fv, fv + 4):
                    by_token(pe, t, hsp)
                for t in range(fz, fz + 4):
                    by_feature(pe, t, hsp)
                evacuated(pe, fz + 3)
                att.pe(pe)
                out_pe(pe)

            @block.scalar
            def _(act):
                nrm.act(act, meanwhile=fq)
                nrm.act_split(act)
                high(act, fq + 2)
                act.wait_ge(f_steps, 2)
                nc.scalar.activation(f_exp, f_abs, ACT.Exp).then_inc(f_steps_a, 1)
                act.wait_ge(f_steps_a, 1)
                nc.scalar.activation(f_log, f_exp, ACT.Ln, bias=ones[:, 0:1]).then_inc(f_steps_a, 1)
                for i in range(4):
                    act.wait_ge(tile_done, fq + i + 1)
                    nc.scalar.activation(qT[:, 2 * i:2 * i + 2, :], bank2(fq + i), ACT.Copy,
                                         scale=-(HD ** -0.5)).then_inc(freed(fq + i), 1)
                    high(act, fq + i + 3)
                act.wait_ge(kz_clear, 1)
                for i in range(4):
                    act.wait_ge(tile_done, fk + i + 1)
                    k4 = kz[:, 4 * i:4 * i + 4, :].rearrange("p (c e) t -> p c e t", e=2)
                    b = bank2(fk + i)
                    nc.scalar.activation(k4[0:HD, :, 0, :], b[0:HD], ACT.Copy)
                    nc.scalar.activation(k4[HD:P, :, 1, :], b[HD:P], ACT.Copy).then_inc(freed(fk + i), 1)
                    high(act, fk + i + 3)
                for i in range(4):
                    act.wait_ge(tile_done, fv + i + 1)
                    nc.scalar.activation(v[:, :, i * 256:(i + 1) * 256], bank2(fv + i), ACT.Copy)\
                        .then_inc(freed(fv + i), 1)
                    high(act, fv + i + 3)
                for i in range(4):
                    act.wait_ge(tile_done, fz + i + 1)
                    a = nc.scalar.activation(zT[:, 2 * i:2 * i + 2, :], bank2(fz + i), ACT.Silu)
                    a.then_inc(freed(fz + i), 1)
                    if i < 3:
                        high(act, fz + i + 3)
                high(act, fz + 6)
                att.act(act)
                high(act, fz + 7)

            @block.vector
            def _(dve):
                nrm.dve(dve, meanwhile=fq + 1)
                dve.wait_ge(fps, 1)
                step = Chain(dve, f_steps)
                fr = f_raw.rearrange("p (t n) -> p t n", t=TT)
                step(nc.vector.tensor_tensor(fr, B[6][:, 0:TT * FOX_H].rearrange("p (t n) -> p t n", t=TT),
                                             bcast(b_f, 1, TT), ALU.add))
                step(nc.vector.scalar_tensor_tensor(out=f_abs, in0=f_raw, scalar=-1.0, in1=f_raw, op0=ALU.mult,
                                                    op1=ALU.min))
                dve.wait_ge(f_steps_a, 2)
                nc.vector.scalar_tensor_tensor(out=logf.rearrange("p t n -> p (t n)"), in0=f_raw, scalar=0.0,
                                               in1=f_log, op0=ALU.min, op1=ALU.subtract).then_inc(logf_ready, 1)
                dve.wait_ge(cq_ps, 1)
                nc.vector.tensor_copy(c_q.rearrange("p t n -> p (t n)"), B[6][:, 0:TT * FOX_H]).then_inc(cq_ready, 1)
                dve.wait_ge(cq_ready, 1)
                for n in range(FOX_H):
                    dve.wait_ge(ck_ps, n + 1)
                    o = B[4 + n % 2]
                    nc.vector.scalar_tensor_tensor(out=cm0[:, n, :], in0=o[:, 0:P], scalar=c_q[:, 0, n:n + 1],
                                                   in1=masks(0), op0=ALU.subtract, op1=ALU.add)
                    nc.vector.scalar_tensor_tensor(out=cm1[:, n, :], in0=o[:, 0:S], scalar=c_q[:, 1, n:n + 1],
                                                   in1=masks(1), op0=ALU.subtract, op1=ALU.add).then_inc(ck_used, 1)
                dve.wait_ge(ck_used, FOX_H)
                evacuated(dve, fz + 3)
                att.dve(dve)
                out_dve(dve)

        memory.open(less=CLEN * P)
        b_hi, b_lo = [memory.float32r("blocks_" + n, CLEN // 2, P) for n in ("high", "low")]
        area = Area()
        raw_c = area(2, 2, S)
        xs2 = area(2, 2, 2, S)
        xb = area(CLEN // 2, P)
        att_area = area.same(4 * S + 8 * S + CLEN // 2 * P)
        raw_k = [area(2, S) for _ in range(2)]
        roped_k = [area(2, S) for _ in range(2)]
        t_cos, t_sin = area(2, S), area(2, S)
        kz2 = [area(2, 2, 2, S) for _ in range(2)]
        v2 = [area(TT, 256) for _ in range(2)]
        raw_q, qT = area(4, S), area(DC, S)
        zT = h
        w_gate = area(DC, 3 * FOX_H)
        gate, gatec = area(TT, 3 * FOX_H), area(TT, 3 * FOX_H)
        w2k, w2v = area(2, 2, HD), area(2, HD)
        hid_t, hid = area(HID), area(2, P)
        raw_kc, cos_kc, sin_kc = area(NG), area(NG), area(NG)
        kzc = area(G, 2, CMP)
        vcm = area(G, HD)
        pbc = [area(2, P) for _ in range(2)]
        nrm2 = Norm(pc("norm_g", DC, DC), split=hsp, sq=qT)
        t_in, t_q, t_z = T["nsa_in"], T["nsa_q"], T["nsa_z"]
        for t in list(range(t_in, t_in + 6)) + list(range(t_q, t_z + 4)):
            plan_tile(t)
        small2, moved_x = sem("nsa_small_loaded"), sem("nsa_blocks_moved")
        moved_k = [sem("nsa_sel_keys_moved"), sem("nsa_win_keys_moved")]
        clear2, xb_clear = sem("nsa_cleared"), sem("blocks_cleared")
        rotated, roped, rope_step = sem("nsa_rotated"), sem("nsa_roped"), sem("nsa_rope_step")
        gate_ps, gate_in, gate_out = sem("gate_product"), sem("gate_sigmoid"), sem("gate_masked")
        block_high, block_split = sem("blocks_high"), sem("blocks_split")
        hid_turned = sem("hidden_turned")
        blocked, hid_ps, hid_in = sem("blocks_ready"), sem("hidden_product"), sem("hidden_ready")
        cmp_ps, cmp_raw, cmp_rot = sem("cmp_product"), sem("cmp_raw"), sem("cmp_rotated")
        cmp_k, cmp_step = sem("cmp_keys_ready"), sem("cmp_step")
        ropes = [(raw_k[0], roped_k[0]), (raw_k[1], roped_k[1])] + \
            [(raw_q[:, 2 * (i % 2):2 * (i % 2) + 2, :], qT[:, 2 * i:2 * i + 2, :]) for i in range(4)]
        raw_tile = [t_in + 2, t_in + 4] + [t_q + i for i in range(4)]

        units = []
        for c in range(DC):
            g = c // 2
            for qt in range(TT):
                w = (qt + 1) * P
                q = qT[:, c, qt * P:(qt + 1) * P]
                for br in (1, 2):
                    kz_b, v_b = kz2[br - 1], v2[br - 1]
                    units.append(dict(
                        group=c, qt=qt, nh=2, w=w, nkt=qt + 1, first=(qt == 0 and br == 1), open=(br == 1),
                        close=False, qk=[(q, kz_b[:, g // 2, g % 2, :, 0:w])], bias=[masks(qt)] * 2,
                        gate=[gate[:, qt, 3 * (2 * c + e) + br:3 * (2 * c + e) + br + 1] for e in range(2)],
                        v=lambda e, kt, g=g, v_b=v_b: v_b[:, kt, g * HD:(g + 1) * HD]))
                units.append(dict(
                    group=c, qt=qt, nh=2, w=CMP, nkt=1, first=False, open=False, close=True,
                    qk=[(q, kzc[:, g, :, :])], bias=[C(f"cmask{qt}")] * 2,
                    gate=[gatec[:, qt, 3 * (2 * c + e):3 * (2 * c + e) + 1] for e in range(2)],
                    v=lambda e, kt, g=g: vcm[:, g, :], pb=pbc[(2 * c + qt) % 2]))
        att2 = Attention(att_area, units, DC,
                         lambda g, ps, zT=zT: nc.vector.tensor_tensor(zT[:, g, :], ps, zT[:, g, :], ALU.mult))
        out2_pe, out2_dve = project_out(T["nsa_out"])

        with nc.Block() as block:
            @block.sync
            def _(sp):
                sp.dma_start(w_gate, nw.rearrange("(c p) n -> p c n", p=P)[:, :, NSA_GATE:NSA_Z]).then_inc(small2, 16)
                for e in range(2):
                    sp.dma_start(w2k[:, :, e, :], A["nsa_w_ck2"][0].rearrange("(c p) n -> p c n", p=P))\
                        .then_inc(small2, 16)
                sp.dma_start(w2v, A["nsa_w_cv2"][0].rearrange("(c p) n -> p c n", p=P)).then_inc(small2, 16)
                for t in range(T["fox_out"] + 4 + NSLOT, T["nsa_out"] + 4 + NSLOT):
                    load(sp, t)
                    if t == t_in + 6:
                        evacuated(sp, t_in)
                        evacuated(sp, t_in + 1)
                        for par_g in range(2):
                            src = raw_c[par_g * HD:(par_g + 1) * HD]
                            for n in range(2):
                                sp.dma_start(xs2[0:HD, n, :, par_g, :], src[:, n]).then_inc(moved_x, 16)
                                sp.dma_start(xs2[HD:P, n, :, par_g, 0:S - 1], src[:, n, :, 1:S])\
                                    .then_inc(moved_x, 16)
                    if t in (t_in + 8, t_in + 10):
                        b = (t - t_in - 8) // 2
                        sp.wait_ge(clear2, 1)
                        sp.wait_ge(roped, b + 1)
                        for par_g in range(2):
                            for e in range(2):
                                sp.dma_start(kz2[b][e * HD:(e + 1) * HD, :, par_g, e, :],
                                             roped_k[b][par_g * HD:(par_g + 1) * HD]).then_inc(moved_k[b], 16)

            @block.gpsimd
            def _(pool):
                for t in range(t_in, t_in + 3):
                    low(pool, nc.gpsimd, t)
                nc.gpsimd.memset(xb, 0.0).then_inc(xb_clear, 1)
                for b in (*kz2, kzc, *pbc):
                    nc.gpsimd.memset(b, 0.0)
                nc.gpsimd.memset(vcm, 0.0).then_inc(clear2, 1)
                for t in range(t_in + 3, T["nsa_out"] + 3):
                    low(pool, nc.gpsimd, t)
                att2.split(pool, zT)
                low(pool, nc.gpsimd, T["nsa_out"] + 3)

            @block.tensor
            def _(pe):
                def rotate(r):
                    evacuated(pe, raw_tile[r])
                    if r >= 2:
                        pe.wait_ge(roped, r - 1)
                    nc.tensor.matmul(B[4 + r % 2][:, :], C("rot"), ropes[r][0], start=True,
                                     stop=True).then_inc(rotated, 1)

                def hidden(n):
                    pe.wait_ge(block_split, 1)
                    for i in range(CLEN // 2):
                        t = ck[n] + i // 8
                        if i % 8 == 0:
                            in_parts(pe, t)
                        mm = product3(B[2 + n][:, 0:HID], [v[:, i, :] for v in (b_hi, b_lo)],
                                      [v[:, i % 8, :] for v in parts(t, "p (i n) -> p i n", i=8, n=HID)],
                                      i == 0, i == CLEN // 2 - 1)
                        if i % 8 == 7:
                            mm.then_inc(tile_done, 1)

                nrm2.pe(pe)
                by_feature(pe, t_in, hsp, ready=nrm2.chunk(pe))
                by_feature(pe, t_in + 1, hsp)
                by_feature(pe, t_in + 2, hsp)
                by_token(pe, t_in + 3, hsp)
                rotate(0)
                by_feature(pe, t_in + 4, hsp)
                by_token(pe, t_in + 5, hsp)
                rotate(1)
                hidden(0)
                hidden(1)
                pe.wait_ge(small2, 64)
                for tt in range(TT):
                    for c in range(DC):
                        mm = nc.tensor.matmul(B[6][:, tt * 48:(tt + 1) * 48], h[:, c, tt * P:(tt + 1) * P],
                                              w_gate[:, c, :], start=(c == 0), stop=(c == DC - 1))
                mm.then_inc(gate_ps, 1)
                by_feature(pe, t_q, hsp)
                pe.wait_ge(hid_in, 2)
                for j in range(2):
                    mm = nc.tensor.transpose(B[2][:, j * P:(j + 1) * P], hid_t[:, j * P:(j + 1) * P], ident)
                mm.then_inc(hid_turned, 1)
                by_feature(pe, t_q + 1, hsp)
                pe.wait_ge(hid_in, 3)
                pe.wait_ge(gate_in, 1)
                for j in range(2):
                    nc.tensor.matmul(B[6][:, 0:NG], w2k[:, j].rearrange("p e d -> p (e d)"), hid[:, j, 0:NG],
                                     start=(j == 0), stop=(j == 1))
                for g in range(G):
                    for j in range(2):
                        mm = nc.tensor.matmul(B[7][0:CMP, g * HD:(g + 1) * HD],
                                              hid[:, j, HD + g * CMP:HD + (g + 1) * CMP],
                                              w2v[:, j, :], start=(j == 0), stop=(j == 1))
                mm.then_inc(cmp_ps, 1)
                rotate(2)
                pe.wait_ge(cmp_raw, 1)
                nc.tensor.matmul(B[2][:, 0:NG], C("rot"), raw_kc, start=True, stop=True).then_inc(cmp_rot, 1)
                by_feature(pe, t_q + 2, hsp)
                rotate(3)
                by_feature(pe, t_q + 3, hsp)
                rotate(4)
                by_feature(pe, t_z, hsp)
                rotate(5)
                for t in range(t_z + 1, t_z + 4):
                    by_feature(pe, t, hsp)
                pe.wait_ge(roped, 6)
                pe.wait_ge(cmp_k, 1)
                for b in range(2):
                    pe.wait_ge(moved_k[b], 64)
                evacuated(pe, t_z + 3)
                att2.pe(pe)
                out2_pe(pe)

            @block.scalar
            def _(act):
                def evac(t, dst, func=ACT.Copy, scale=1.0):
                    act.wait_ge(tile_done, t + 1)
                    nc.scalar.activation(dst, bank2(t), func, scale=scale).then_inc(freed(t), 1)
                    if t < t_z + 3:
                        high(act, t + 3)

                nrm2.act(act, meanwhile=t_in)
                nrm2.act_split(act)
                high(act, t_in + 2)
                evac(t_in, raw_c[:, 0])
                evac(t_in + 1, raw_c[:, 1])
                evac(t_in + 2, raw_k[0])
                evac(t_in + 3, v2[0])
                evac(t_in + 4, raw_k[1])
                evac(t_in + 5, v2[1])
                for n in range(2):
                    for k in range(2):
                        act.wait_ge(tile_done, ck[n] + k + 1)
                        if k:
                            rows = slice(n * HD, (n + 1) * HD)
                            nc.scalar.activation(hid_t[rows], B[2 + n][rows, 0:HID], ACT.Silu).then_inc(hid_in, 1)
                        high(act, ck[n] + k + 3)
                act.wait_ge(gate_ps, 1)
                nc.scalar.activation(gate, B[6][:, 0:96].rearrange("p (t n) -> p t n", t=TT),
                                     ACT.Sigmoid).then_inc(gate_in, 1)
                evac(t_q, raw_q[:, 0:2, :], scale=-(HD ** -0.5))
                act.wait_ge(hid_turned, 1)
                nc.scalar.activation(hid, B[2][:, 0:2 * P].rearrange("p (j c) -> p j c", j=2),
                                     ACT.Copy).then_inc(hid_in, 1)
                evac(t_q + 1, raw_q[:, 2:4, :], scale=-(HD ** -0.5))
                act.wait_ge(cmp_ps, 1)
                nc.scalar.activation(raw_kc, B[6][:, 0:NG], ACT.Copy).then_inc(cmp_raw, 1)
                act.wait_ge(clear2, 1)
                nc.scalar.activation(vcm[0:CMP], B[7][0:CMP, 0:G * HD].rearrange("p (g d) -> p g d", g=G),
                                     ACT.Copy)
                for i in range(2, 4):
                    act.wait_ge(roped, i + 1)
                    evac(t_q + i, raw_q[:, 2 * (i % 2):2 * (i % 2) + 2, :], scale=-(HD ** -0.5))
                for i in range(4):
                    evac(t_z + i, zT[:, 2 * i:2 * i + 2, :], ACT.Silu)
                high(act, T["nsa_out"] + 2)
                att2.act(act)
                high(act, T["nsa_out"] + 3)

            @block.vector
            def _(dve):
                step = Chain(dve, rope_step)

                def rope(r):
                    src, dst = ropes[r]
                    tc, ts = t_cos, t_sin
                    dve.wait_ge(rotated, r + 1)
                    if r:
                        dve.wait_ge(roped, r)
                    nc.vector.tensor_tensor(tc, src, bcast(C("cos_tok"), 1, 2), ALU.mult)
                    step(nc.vector.tensor_tensor(ts, B[4 + r % 2][:, :].rearrange("p (a b) -> p a b", a=2),
                                                 bcast(C("sin_tok"), 1, 2), ALU.mult))
                    nc.vector.tensor_tensor(dst, tc, ts, ALU.add).then_inc(roped, 1)

                nrm2.dve(dve, meanwhile=t_in + 1)
                rope(0)
                dve.wait_ge(moved_x, 128)
                dve.wait_ge(xb_clear, 1)
                for n in range(2):
                    src = xs2[:, n].rearrange("p a b (c i k) -> p i (a b) c k", c=16, k=2)
                    for half in range(2):
                        i8 = slice(8 * half, 8 * half + 8)
                        pe_n = pc("pe_" + "kv"[n], 8 * half, 8)
                        i = nc.vector.tensor_tensor(
                            xb[:, i8, n * HD:n * HD + NG].rearrange("p i (g c) -> p i g c", g=G),
                            src[:, :, :, half:half + CMP, 0],
                            pe_n.unsqueeze(2).unsqueeze(3).broadcast_to([P, 8, G, CMP]), ALU.add)
                    i.then_inc(blocked, 1)
                dve.wait_ge(blocked, 2)
                nc.vector.tensor_copy(b_hi[:, :, :], xb).then_inc(block_high, 1)
                dve.wait_ge(block_high, 1)
                nc.vector.tensor_tensor(b_lo[:, :, :], xb, b_hi[:, :, :].bitcast(F32),
                                        ALU.subtract).then_inc(block_split, 1)
                rope(1)
                dve.wait_ge(gate_in, 1)
                for tt in range(TT):
                    i = nc.vector.tensor_scalar(gatec[:, tt, :], gate[:, tt, :], C(f"cvalid{tt}"), None, ALU.mult)
                i.then_inc(gate_out, 1)
                rope(2)
                dve.wait_ge(cmp_rot, 1)
                nc.vector.tensor_tensor(cos_kc, raw_kc, C("cos_cmp"), ALU.mult)
                nc.vector.tensor_tensor(sin_kc, B[2][:, 0:NG], C("sin_cmp"), ALU.mult).then_inc(cmp_step, 1)
                dve.wait_ge(cmp_step, 1)
                dve.wait_ge(clear2, 1)
                for e in range(2):
                    r0 = slice(e * HD, (e + 1) * HD)
                    i = nc.vector.tensor_tensor(kzc[r0, :, e, :], cos_kc[r0].rearrange("p (g c) -> p g c", g=G),
                                                sin_kc[r0].rearrange("p (g c) -> p g c", g=G), ALU.add)
                i.then_inc(cmp_k, 1)
                rope(3)
                rope(4)
                rope(5)
                dve.wait_ge(gate_out, 1)
                evacuated(dve, t_z + 3)
                att2.dve(dve)
                out2_dve(dve)

        memory.open()
        area = Area()
        n_late = sum(at[n][1] for n in ("levels", "lmask"))
        late = area(n_late)
        lf = area(TT, D)
        fg = area(TT, D)
        fg_area = area.same(TT * D)
        sm, sc, scx = fg_area(8, P), fg_area(2, TT, P), fg_area(2, P)
        keyt = area(TT, D)
        decay = area.same(TT * D)(2, 8, P)
        qT, gT, keyT = area(DC, S), area(DC, S), area(DC, S)
        v = area(TT, D)
        sq3 = area.same(TT * D)(DC, S)
        oh = h
        qd, kd = area(3, 8, P), area(3, 8, P)
        row_area = area.same(6 * 8 * P)
        b_row, e_row, lb_row, om_row = [row_area(D) for _ in range(4)]
        sq8, rs8 = fg.rearrange("p t n -> p (t n)"), keyt.rearrange("p t n -> p (t n)")
        nrm_f = Norm(pc("final_g", 0, DC), dst=x, sq=sq3)
        nrm3 = Norm(pc("norm_mix", 0, DC), after=nrm_f, split=hsp, sq=sq3)
        t_f, t_q3, t_i, t_g = T["hgrn_f"], T["hgrn_q"], T["hgrn_i"], T["hgrn_g"]
        for t in range(t_f, t_g + 4):
            plan_tile(t)
        lb_in, lb_step, lb_exp = sem("bounds_loaded"), sem("bounds_step"), sem("bounds_exp")
        forget, clamped, logged = sem("forget_step"), sem("forget_clamped"), sem("log_forget")
        key_turned, key_placed = sem("key_turned"), sem("key_placed")
        summed, decayed = sem("exponents_summed"), sem("decays_ready")
        q_dec, k_dec = sem("q_decayed"), sem("k_decayed")
        scored, masked, scores_in = sem("hgrn_scored"), sem("hgrn_masked"), sem("hgrn_scores_ready")
        cross_in, o_ps, o_in = sem("cross_scores_ready"), sem("hgrn_output_product"), sem("hgrn_output_ready")
        sq_in, sq_ps, sq_root = sem("hgrn_squares"), sem("hgrn_squares_summed"), sem("hgrn_roots")
        o_step, o_ready = sem("hgrn_norm_step"), sem("hgrn_gated")
        late_in = sem("hgrn_constants_loaded")
        out3_pe, out3_dve = project_out(T["hgrn_out"])
        NU = 2 * HG_H
        n_high3 = steps_taken["n"]
        steps_taken["n"] += DC

        def lslot(l, tt):
            return l if l < 4 or tt else l + 1

        with nc.Block() as block:
            @block.sync
            def _(sp):
                sp.dma_start(b_row, A["hgrn_lower_bounds_2"].broadcast_to([P, D])).then_inc(lb_in, 16)
                sp.dma_start(late, cst_dram[:, ncst:ncst + n_late]).then_inc(late_in, 16)
                for t in range(T["nsa_out"] + 4 + NSLOT, T["hgrn_out"] + 4 + NSLOT):
                    load(sp, t)

            @block.gpsimd
            def _(pool):
                t_o = T["hgrn_out"]
                for t in range(t_f, t_o + 1):
                    low(pool, nc.gpsimd, t)
                for w in range(NU):
                    hh, tt = w // 2, w % 2
                    if w in (5, 9):
                        low(pool, nc.gpsimd, t_o + 1 + (w - 5) // 4)
                    pool.wait_ge(decayed, w + 1)
                    if w == 0:
                        pool.wait_ge(key_placed, 4)
                    if w >= 3:
                        pool.wait_ge(scored, w - 1)
                    nc.gpsimd.tensor_tensor(kd[:, w % 3], decay[:, w % 2],
                                            bcast(keyT[:, hh, tt * P:(tt + 1) * P], 1, 8), ALU.mult)\
                        .then_inc(k_dec, 1)
                for c in range(DC):
                    pool.wait_ge(high_step, n_high3 + c + 1)
                    nc.gpsimd.tensor_tensor(h_lo[:, c, :], oh[:, c, :], h_hi[:, c, :].bitcast(F32),
                                            ALU.subtract).then_inc(act_split, 1)
                low(pool, nc.gpsimd, t_o + 3)

            @block.tensor
            def _(pe):
                nrm_f.pe(pe)
                nrm3.pe(pe)
                for i in range(4):
                    by_token(pe, t_f + i, hsp, ready=nrm3.chunk(pe) if i == 0 else None)
                for i in range(4):
                    by_feature(pe, t_q3 + i, hsp)
                pe.wait_ge(forget, 3)
                for c in range(DC):
                    for tt in range(TT):
                        mm = nc.tensor.transpose(B[2 + c // 2][:, (c % 2) * S + tt * P:(c % 2) * S + (tt + 1) * P],
                                                 keyt[:, tt, c * P:(c + 1) * P], ident)
                    if c % 2:
                        mm.then_inc(key_turned, 1)
                for i in range(4):
                    by_token(pe, t_i + i, hsp)
                for i in range(4):
                    by_feature(pe, t_g + i, hsp)
                pe.wait_ge(logged, 1)
                pe.wait_ge(late_in, 16)
                pe.wait_ge(key_placed, 4)
                evacuated(pe, t_g + 2)
                evacuated(pe, t_g + 3)

                def exponents(w):
                    hh, tt = w // 2, w % 2
                    if w >= 2:
                        pe.wait_ge(decayed, w - 1)
                    for b in range(2):
                        c0 = b * (512 + P * tt)
                        mm = nc.tensor.matmul(B[2 * (w % 2) + b][:, :], lf[:, tt, hh * P:(hh + 1) * P],
                                              late[:, c0:c0 + 512], start=True, stop=True)
                    mm.then_inc(summed, 1)

                def scores(w):
                    hh, tt = w // 2, w % 2
                    pe.wait_ge(q_dec, w + 1)
                    pe.wait_ge(k_dec, w + 1)
                    if w >= 1:
                        pe.wait_ge(masked, w)
                    for l in range(LEVELS):
                        s_ = lslot(l, tt)
                        nc.tensor.matmul(B[4 + l // 4][:, (l % 4) * P:(l % 4 + 1) * P], kd[:, w % 3, s_, :],
                                         qd[:, w % 3, s_, :], start=True, stop=True)
                    tk = slice(tt * P, (tt + 1) * P)
                    mm = nc.tensor.matmul(B[5][:, 3 * P:4 * P], keyT[:, hh, tk], qT[:, hh, tk], start=True, stop=True)
                    if tt:
                        if hh:
                            pe.wait_ge(cross_in, hh)
                        mm = nc.tensor.matmul(B[6][:, 0:P], kd[:, (w - 1) % 3, 4, :], qd[:, w % 3, 7, :],
                                              start=True, stop=True)
                    mm.then_inc(scored, 1)

                def outputs(hh):
                    pe.wait_ge(scores_in, 2 * hh + 2)
                    pe.wait_ge(cross_in, hh + 1)
                    if hh:
                        pe.wait_ge(o_in, hh)
                    vh = [v[:, tt, hh * P:(hh + 1) * P] for tt in range(TT)]
                    nc.tensor.matmul(B[7][:, 0:P], vh[0], sc[:, hh % 2, 0, :], start=True, stop=True)
                    nc.tensor.matmul(B[7][:, P:S], vh[0], scx[:, hh % 2, :], start=True, stop=False)
                    nc.tensor.matmul(B[7][:, P:S], vh[1], sc[:, hh % 2, 1, :], start=False, stop=True)\
                        .then_inc(o_ps, 1)

                for w in range(NU + 2):
                    if w < NU:
                        exponents(w)
                    if 1 <= w <= NU:
                        scores(w - 1)
                    if w >= 3 and w % 2:
                        outputs((w - 3) // 2)
                for i in range(4):
                    pe.wait_ge(sq_in, i + 1)
                    nc.tensor.matmul(B[2 + i][:, :], ones, sq8[:, i * 512:(i + 1) * 512], start=True,
                                     stop=True).then_inc(sq_ps, 1)
                out3_pe(pe)

            @block.scalar
            def _(act):
                nrm_f.act(act, meanwhile=t_f)
                nrm3.act(act, meanwhile=t_f + 2)
                nrm3.act_split(act)
                act.wait_ge(lb_step, 1)
                nc.scalar.activation(e_row, e_row, ACT.Exp).then_inc(lb_exp, 1)
                for i in range(4):
                    act.wait_ge(tile_done, t_f + i + 1)
                    nc.scalar.activation(fg[:, :, i * 256:(i + 1) * 256], bank2(t_f + i), ACT.Sigmoid)\
                        .then_inc(freed(t_f + i), 1)
                    high(act, t_f + i + 3)
                for i in range(4):
                    act.wait_ge(tile_done, t_q3 + i + 1)
                    nc.scalar.activation(qT[:, 2 * i:2 * i + 2, :], bank2(t_q3 + i), ACT.Silu)\
                        .then_inc(freed(t_q3 + i), 1)
                    high(act, t_q3 + i + 3)
                act.wait_ge(clamped, 1)
                nc.scalar.activation(lf, lf, ACT.Ln).then_inc(logged, 1)
                for i in range(4):
                    act.wait_ge(tile_done, t_i + i + 1)
                    nc.scalar.activation(v[:, :, i * 256:(i + 1) * 256], bank2(t_i + i), ACT.Copy)\
                        .then_inc(freed(t_i + i), 1)
                    high(act, t_i + i + 3)
                for i in range(4):
                    act.wait_ge(tile_done, t_g + i + 1)
                    nc.scalar.activation(gT[:, 2 * i:2 * i + 2, :], bank2(t_g + i), ACT.Silu)\
                        .then_inc(freed(t_g + i), 1)
                    if i < 3:
                        high(act, t_g + i + 3)
                for w in range(NU + 3):
                    if w < NU:
                        act.wait_ge(summed, w + 1)
                        if w >= 2:
                            act.wait_ge(q_dec, w - 1)
                            act.wait_ge(k_dec, w - 1)
                        for b in range(2):
                            i = nc.scalar.activation(decay[:, w % 2, 4 * b:4 * b + 4, :],
                                                     B[2 * (w % 2) + b][:, :].rearrange("p (l t) -> p l t", l=4),
                                                     ACT.Exp)
                        i.then_inc(decayed, 1)
                    if w >= 2 and w % 2 == 0 and w <= NU:
                        hh = w // 2 - 1
                        act.wait_ge(scored, 2 * hh + 2)
                        if hh >= 2:
                            act.wait_ge(o_ps, hh - 1)
                        nc.scalar.activation(scx[:, hh % 2, :], B[6][:, 0:P], ACT.Copy).then_inc(cross_in, 1)
                    if w == 3:
                        high(act, T["hgrn_out"] + 2)
                    if w >= 4 and w % 2 == 0:
                        hh = (w - 4) // 2
                        act.wait_ge(o_ps, hh + 1)
                        nc.scalar.activation(oh[:, hh, :], B[7][:, 0:S], ACT.Copy).then_inc(o_in, 1)
                for i in range(4):
                    act.wait_ge(o_in, 2 * i + 2)
                    nc.scalar.activation(sq8[:, i * 512:(i + 1) * 512].rearrange("p (a b) -> p a b", a=2),
                                         oh[:, 2 * i:2 * i + 2, :], ACT.Square).then_inc(sq_in, 1)
                for i in range(4):
                    act.wait_ge(sq_ps, i + 1)
                    nc.scalar.activation(rs8[:, i * 512:(i + 1) * 512], B[2 + i][:, :], ACT.Sqrt,
                                         scale=1.0 / P, bias=eps[:, 0:1]).then_inc(sq_root, 1)
                for i in range(4):
                    act.wait_ge(o_ready, i + 1)
                    nc.scalar.activation(h_hi[:, 2 * i:2 * i + 2, :], oh[:, 2 * i:2 * i + 2, :], ACT.Copy)\
                        .then_inc(high_step, 2)
                high(act, T["hgrn_out"] + 3)

            @block.vector
            def _(dve):
                nrm_f.dve(dve, meanwhile=t_f + 1)
                nrm3.dve(dve)
                dve.wait_ge(lb_in, 16)
                nc.vector.tensor_tensor(e_row, b_row, b_row, ALU.subtract).then_inc(lb_step, 1)
                dve.wait_ge(lb_exp, 1)
                nc.vector.reciprocal(om_row, e_row).then_inc(lb_step, 1)
                dve.wait_ge(lb_step, 2)
                nc.vector.tensor_tensor(b_row, e_row, om_row, ALU.mult).then_inc(lb_step, 1)
                dve.wait_ge(lb_step, 3)
                nc.vector.tensor_tensor(lb_row, b_row, b_row, ALU.subtract).then_inc(lb_step, 1)
                dve.wait_ge(lb_step, 4)
                nc.vector.tensor_scalar(om_row, lb_row, -1.0, 1.0, ALU.mult, ALU.add).then_inc(lb_step, 1)
                dve.wait_ge(lb_step, 5)
                evacuated(dve, t_f + 2)
                evacuated(dve, t_f + 3)
                nc.vector.tensor_tensor(fg, fg, bcast(om_row, 1, TT), ALU.mult).then_inc(forget, 1)
                dve.wait_ge(forget, 1)
                nc.vector.tensor_tensor(fg, fg, bcast(lb_row, 1, TT), ALU.add).then_inc(forget, 1)
                dve.wait_ge(forget, 2)
                nc.vector.tensor_scalar(keyt, fg, -1.0, 1.0, ALU.mult, ALU.add).then_inc(forget, 1)
                nc.vector.tensor_scalar(lf, fg, LEAST, None, ALU.max).then_inc(clamped, 1)
                for i in range(4):
                    dve.wait_ge(key_turned, i + 1)
                    nc.vector.tensor_copy(keyT[:, 2 * i:2 * i + 2, :],
                                          B[2 + i][:, :].rearrange("p (a b) -> p a b", a=2)).then_inc(key_placed, 1)

                def decayed_queries(w):
                    hh, tt = w // 2, w % 2
                    dve.wait_ge(decayed, w + 1)
                    if w == 0:
                        evacuated(dve, t_q3 + 3)
                    if w >= 3:
                        dve.wait_ge(scored, w - 1)
                    nc.vector.tensor_tensor(qd[:, w % 3], decay[:, w % 2],
                                            bcast(qT[:, hh, tt * P:(tt + 1) * P], 1, 8), ALU.mult).then_inc(q_dec, 1)

                def mask_scores(w):
                    hh, tt = w // 2, w % 2
                    dve.wait_ge(scored, w + 1)
                    if w >= 1:
                        dve.wait_ge(scores_in, w)
                    if hh >= 2:
                        dve.wait_ge(o_ps, hh - 1)
                    for b in range(2):
                        i = nc.vector.tensor_tensor(sm[:, 4 * b:4 * b + 4, :],
                                                    B[4 + b][:, :].rearrange("p (l t) -> p l t", l=4),
                                                    late[:, 9 * P + 512 * b:9 * P + 512 * b + 512].rearrange("p (l t) -> p l t", l=4),
                                                    ALU.mult)
                    i.then_inc(masked, 1)
                    dve.wait_ge(masked, w + 1)
                    nc.vector.tensor_reduce(sc[:, hh % 2, tt, :], sm.rearrange("p l t -> p t l"), AX.X,
                                            ALU.add).then_inc(scores_in, 1)

                for w in range(NU + 1):
                    if w < NU:
                        decayed_queries(w)
                    if w >= 1:
                        mask_scores(w - 1)
                step = Chain(dve, o_step)
                for i in range(4):
                    r = rs8[:, i * 512:(i + 1) * 512]
                    o2 = oh[:, 2 * i:2 * i + 2, :]
                    dve.wait_ge(sq_root, i + 1)
                    step(nc.vector.reciprocal(r, r))
                    step(nc.vector.scalar_tensor_tensor(out=o2, in0=o2, scalar=pc("hgrn_norm"),
                                                        in1=r.rearrange("p (a b) -> p a b", a=2),
                                                        op0=ALU.mult, op1=ALU.mult))
                    nc.vector.tensor_tensor(o2, o2, gT[:, 2 * i:2 * i + 2, :], ALU.mult).then_inc(o_ready, 1)
                out3_dve(dve)

        ffn(0, pc("norm_ffn", 0, DC), T["ffn0"], T["ffn0"] + NSLOT, T["ffn0"] + 33 + NSLOT)

        memory.open(less=2 * 4 * S)
        c_hi, c_lo = [memory.float32r("lora_" + n, 4, S) for n in ("high", "low")]
        area = Area()
        pos_i = area(S).bitcast(I32)
        cosT, sinT = area(S), area(S)
        w_r = area(DC, ROPE)
        cq, ckv = area(2, S), area(2, S)
        lrs = area(2, S)
        gq = area(2)
        kr, krg, kr_sq, kr_t, kr_base = [area(S) for _ in range(5)]
        qn, qr, krh, kn = [area(ML_H, S) for _ in range(4)]
        early = area.same(ML_H * S)
        ang, turns, sin_h = early(S), early(S), early(S)
        lsq = [early(2, S) for _ in range(2)]
        v = area(TT, D)
        sq5 = area.same(TT * D)(DC, S)
        oT = h
        sqn, sqr, rs2, tcos, tsin = [area(2, 2, S) for _ in range(5)]
        att_area = area.same(5 * 4 * S)
        nrm5 = Norm(pc("norm_mix", DC, DC), split=hsp, sq=sq5)
        t_mi, t_mq, t_mkv = T["mla_in"], T["mla_q"], T["mla_kv"]
        for t in (t_mi, t_mi + 1):
            plan_tile(t)
        use0 = turn["n"]
        uses = [(kind, p) for p in range(4) for kind in ("qn", "qr")]
        for n in range(2):
            uses += [("kn", 4 + 2 * n), ("kn", 5 + 2 * n), ("v", 2 * n), ("v", 2 * n + 1)]
        use_no = {k: use0 + n for n, k in enumerate(uses)}
        turn["n"] += len(uses)
        small5, pos_in, kr_clear = sem("mla_small_loaded"), sem("positions_loaded"), sem("mla_cleared")
        ang_step, sins, cos_ready = sem("angle_step"), sem("sines_ready"), sem("cosines_ready")
        lora_ps, lora_sum = sem("rope_key_product"), sem("lora_summed")
        lora_root, lora_step, lora_ready = sem("lora_root"), sem("lora_step"), sem("lora_ready")
        kr_in, krg_in, kr_rot, kr_ready = sem("rope_key_raw"), sem("rope_key_gained"), sem("rope_key_rotated"), sem("rope_key_ready")
        up_done, sum5 = sem("mla_up_product"), sem("mla_squares_summed")
        root5, step5, gained = sem("mla_root"), sem("mla_step"), sem("mla_gained")
        rot5, ready5 = sem("mla_rotated"), sem("mla_pair_ready")

        units = []
        for hh in range(ML_H):
            for qt in range(TT):
                w = (qt + 1) * P
                tk = slice(qt * P, (qt + 1) * P)
                units.append(dict(
                    group=hh, qt=qt, nh=1, w=w, nkt=qt + 1, first=(qt == 0), open=True, close=True,
                    qk=[(qn[:, hh, tk], kn[:, hh:hh + 1, 0:w]), (qr[:, hh, tk], krh[:, hh:hh + 1, 0:w])],
                    bias=[masks(qt)], v=lambda e, kt, hh=hh, v=v: v[:, kt, hh * P:(hh + 1) * P]))
        att5 = Attention(att_area, units, ML_H,
                         lambda g, ps, oT=oT: nc.vector.tensor_copy(oT[:, g, :], ps))
        out5_pe, out5_dve = project_out(T["mla_out"])
        TWO_PI = (6.28125, 0.0019340515136718750, float(np.float32(2 * np.pi - 6.28125 - 0.0019340515136718750)))
        ROUND = 1.5 * 2 ** 23

        with nc.Block() as block:
            @block.sync
            def _(sp):
                sp.dma_start(pos_i, A["positions_2"].broadcast_to([P, S])).then_inc(pos_in, 16)
                sp.dma_start(w_r, mw.rearrange("(c p) n -> p c n", p=P)[:, :, 2 * LORA:]).then_inc(small5, 16)
                for t in range(T["ffn0"] + 33 + NSLOT, T["mla_out"] + 4 + NSLOT):
                    load(sp, t)

            @block.gpsimd
            def _(pool):
                low(pool, nc.gpsimd, t_mi)
                nc.gpsimd.memset(kr, 0.0)
                nc.gpsimd.memset(qr, 0.0)
                nc.gpsimd.memset(sqr, 0.0).then_inc(kr_clear, 1)
                for t in range(t_mi + 1, T["mla_out"] + 3):
                    low(pool, nc.gpsimd, t)
                att5.split(pool, oT)
                low(pool, nc.gpsimd, T["mla_out"] + 3)

            @block.tensor
            def _(pe):
                def use_bank(k):
                    u = use_no[k]
                    pe.wait_ge(bank_free[u % 2], u // 2)
                    return B[u % 2]

                def up(p):
                    t = (t_mq if p < 4 else t_mkv) + (p % 4) // 2
                    width = QK if p < 4 else 256
                    if p % 2 == 0:
                        in_parts(pe, t)
                    w = [r[:, t % NSLOT, :] for r in (w_hi, w_lo)]
                    k0, kinds = (0, (("qn", 0), ("qr", NOPE))) if p < 4 else (2, (("kn", 0),))
                    for kind, c0 in kinds:
                        b = use_bank((kind, p))
                        for e in range(2):
                            c = (2 * (p % 2) + e) * width + c0
                            for k in range(2):
                                at_k = 4 * width * k + c
                                mm = product3(b[:, e * S:(e + 1) * S], [v[:, at_k:at_k + P] for v in w],
                                              [v[:, k0 + k, :] for v in (c_hi, c_lo)], k == 0, k == 1)
                        if kind == "qr" and p % 2:
                            mm.then_inc(tile_done, 1)
                        else:
                            mm.then_inc(up_done, 1)

                def up_values(n):
                    t = t_mkv + n
                    w = parts(t, "p (k e n) -> p k e n", k=2, e=4, n=256)
                    for tt in range(TT):
                        b = use_bank(("v", 2 * n + tt))
                        for k in range(2):
                            mm = product3(b[:, :], [v[:, 2 + k, tt * P:(tt + 1) * P] for v in (c_hi, c_lo)],
                                          [v[:, k, :, NOPE:] for v in w], k == 0, k == 1)
                        mm.then_inc(tile_done if tt else up_done, 1)

                def sums(p):
                    u = use_no[("qr" if p < 4 else "kn", p)]
                    pe.wait_ge(bank_free[u % 2], u // 2 + 1)
                    if p >= 2:
                        pe.wait_ge(root5, p - 1)
                    b = B[2 + p % 2]
                    nc.tensor.matmul(b[:, :], ones, sqn[:, p % 2], start=True, stop=False)
                    r = sqr[:, p % 2] if p < 4 else bcast(kr_sq, 1, 2)
                    nc.tensor.matmul(b[:, :], ones, r, start=False, stop=True).then_inc(sum5, 1)

                def rotate(p):
                    pe.wait_ge(gained, p + 1)
                    if p >= 2:
                        pe.wait_ge(ready5, p - 1)
                    nc.tensor.matmul(B[4 + p % 2][:, :], C("rot2"), qr[:, 2 * p:2 * p + 2, :], start=True,
                                     stop=True).then_inc(rot5, 1)

                nrm5.pe(pe)
                by_feature(pe, t_mi, hsp, ready=nrm5.chunk(pe))
                by_feature(pe, t_mi + 1, hsp)
                pe.wait_ge(small5, 16)
                for c in range(DC):
                    mm = nc.tensor.matmul(B[6][0:ROPE, 0:S], w_r[:, c, :], h[:, c, :], start=(c == 0), stop=(c == DC - 1))
                mm.then_inc(lora_ps, 1)
                for n in range(2):
                    evacuated(pe, t_mi + n)
                    for k in range(2):
                        mm = nc.tensor.matmul(B[4 + n][:, 0:S], ones, lsq[n][:, k, :], start=(k == 0), stop=(k == 1))
                    mm.then_inc(lora_sum, 1)
                pe.wait_ge(krg_in, 1)
                nc.tensor.matmul(B[7][:, 0:S], C("rot2"), krg, start=True, stop=True).then_inc(kr_rot, 1)
                pe.wait_ge(lora_ready, 2)
                for p in range(10):
                    if p < 8:
                        up(p)
                    if 1 <= p <= 8:
                        sums(p - 1)
                    if 2 <= p < 6:
                        rotate(p - 2)
                    if p in (5, 7):
                        up_values((p - 5) // 2)
                pe.wait_ge(ready5, 8)
                for k in (("v", 2), ("v", 3)):
                    pe.wait_ge(bank_free[use_no[k] % 2], use_no[k] // 2 + 1)
                att5.pe(pe)
                out5_pe(pe)

            def product_done(eng, k):
                last = {("qr", 1): t_mq, ("qr", 3): t_mq + 1, ("v", 1): t_mkv, ("v", 3): t_mkv + 1}
                if k in last:
                    eng.wait_ge(tile_done, last[k] + 1)
                else:
                    eng.wait_ge(up_done, sum(1 for q in uses[:uses.index(k) + 1] if q not in last))

            @block.scalar
            def _(act):
                act.wait_ge(ang_step, 7)
                nc.scalar.activation(sinT, ang, ACT.Sin)
                nc.scalar.activation(sin_h, ang, ACT.Sin, scale=0.5).then_inc(sins, 1)
                nrm5.act(act, meanwhile=t_mi)
                nrm5.act_split(act)
                high(act, t_mi + 2)
                for n, dst in enumerate((cq, ckv)):
                    act.wait_ge(tile_done, t_mi + n + 1)
                    nc.scalar.activation(dst, bank2(t_mi + n), ACT.Copy)
                    nc.scalar.activation(lsq[n], bank2(t_mi + n), ACT.Square).then_inc(freed(t_mi + n), 1)
                    high(act, t_mi + n + 3)
                act.wait_ge(lora_ps, 1)
                act.wait_ge(kr_clear, 1)
                nc.scalar.activation(kr[0:ROPE], B[6][0:ROPE, 0:S], ACT.Copy).then_inc(kr_in, 1)
                act.wait_ge(kr_in, 1)
                nc.scalar.activation(kr_sq, kr, ACT.Square).then_inc(kr_in, 1)
                for n in range(2):
                    act.wait_ge(lora_sum, n + 1)
                    nc.scalar.activation(lrs[:, n, :], B[4 + n][:, 0:S], ACT.Sqrt, scale=1.0 / LORA,
                                         bias=eps[:, 0:1]).then_inc(lora_root, 1)

                def evac(p):
                    if p >= 2:
                        act.wait_ge(sum5, p - 1)
                    parts = (("qn", qn, P, sqn), ("qr", qr, ROPE, sqr)) if p < 4 else (("kn", kn, P, sqn),)
                    for kind, dst, m, sq in parts:
                        product_done(act, (kind, p))
                        u = use_no[(kind, p)]
                        b = B[u % 2][0:m, :].rearrange("p (a b) -> p a b", a=2)
                        pp = 2 * (p % 4)
                        nc.scalar.activation(dst[0:m, pp:pp + 2, :], b, ACT.Copy)
                        i = nc.scalar.activation(sq[0:m, p % 2], b, ACT.Square)
                        i.then_inc(bank_free[u % 2], 1)

                def root(p):
                    act.wait_ge(sum5, p + 1)
                    if p >= 2:
                        act.wait_ge(ready5, p - 1)
                    nc.scalar.activation(rs2[:, p % 2], B[2 + p % 2][:, :].rearrange("p (a b) -> p a b", a=2),
                                         ACT.Sqrt, scale=1.0 / QK, bias=eps[:, 0:1]).then_inc(root5, 1)

                for p in range(9):
                    if p < 8:
                        evac(p)
                    if p in (1, 3):
                        high(act, t_mq + p // 2 + 3)
                    if p >= 1:
                        root(p - 1)
                    if p in (5, 7):
                        n = (p - 5) // 2
                        for tt in range(TT):
                            k = ("v", 2 * n + tt)
                            product_done(act, k)
                            nc.scalar.activation(v[:, tt, n * 512:(n + 1) * 512], B[use_no[k] % 2][:, :],
                                                 ACT.Copy).then_inc(bank_free[use_no[k] % 2], 1)
                        high(act, t_mkv + n + 3)
                att5.act(act)
                high(act, T["mla_out"] + 3)

            @block.vector
            def _(dve):
                step = Chain(dve, ang_step)
                dve.wait_ge(pos_in, 16)
                step(nc.vector.tensor_copy(ang, pos_i))
                step(nc.vector.tensor_scalar(ang, ang, C("inv2"), None, ALU.mult))
                step(nc.vector.tensor_scalar(turns, ang, 1 / (2 * np.pi), ROUND, ALU.mult, ALU.add))
                step(nc.vector.tensor_scalar(turns, turns, ROUND, None, ALU.subtract))
                for part in TWO_PI:
                    step(nc.vector.scalar_tensor_tensor(out=ang, in0=turns, scalar=-part, in1=ang,
                                                        op0=ALU.mult, op1=ALU.add))
                dve.wait_ge(sins, 1)
                nc.vector.tensor_tensor(cosT, sin_h, sin_h, ALU.mult).then_inc(cos_ready, 1)
                dve.wait_ge(cos_ready, 1)
                nc.vector.tensor_scalar(cosT, cosT, -2.0, 1.0, ALU.mult, ALU.add).then_inc(cos_ready, 1)
                nrm5.dve(dve, meanwhile=t_mi + 1)
                nc.vector.tensor_scalar(gq, par[:, pcol["q_nope"]:pcol["q_nope"] + 2], -(QK ** -0.5), None, ALU.mult)
                dve.wait_ge(kr_in, 2)
                nc.vector.tensor_scalar(krg, kr, pc("k_rope"), None, ALU.mult).then_inc(krg_in, 1)
                lstep = Chain(dve, lora_step)
                for n, (c, g) in enumerate(((cq, "q_a"), (ckv, "kv_a"))):
                    dve.wait_ge(lora_root, n + 1)
                    lstep(nc.vector.reciprocal(lrs[:, n, :], lrs[:, n, :]))
                    for k in range(2):
                        i = nc.vector.scalar_tensor_tensor(out=c[:, k, :], in0=c[:, k, :], scalar=pc(g, k),
                                                           in1=lrs[:, n, :], op0=ALU.mult, op1=ALU.mult)
                    lstep(i)
                    part = slice(2 * n, 2 * n + 2)
                    lstep(nc.vector.tensor_copy(c_hi[:, part, :], c))
                    nc.vector.tensor_tensor(c_lo[:, part, :], c, c_hi[:, part, :].bitcast(F32),
                                            ALU.subtract).then_inc(lora_ready, 1)
                dve.wait_ge(kr_rot, 1)
                dve.wait_ge(cos_ready, 2)
                nc.vector.tensor_tensor(kr_t, B[7][:, 0:S], sinT, ALU.mult)
                lstep(nc.vector.tensor_tensor(kr_base, krg, cosT, ALU.mult))
                lstep(nc.vector.tensor_tensor(kr_base, kr_base, kr_t, ALU.add))
                step = Chain(dve, step5)

                def gain(p):
                    dve.wait_ge(root5, p + 1)
                    r = rs2[:, p % 2]
                    step(nc.vector.reciprocal(r, r))
                    pp = 2 * (p % 4)
                    src, g = (qn, gq[:, 0:1]) if p < 4 else (kn, pc("k_nope"))
                    o = src[:, pp:pp + 2, :]
                    i = nc.vector.scalar_tensor_tensor(out=o, in0=o, scalar=g, in1=r, op0=ALU.mult, op1=ALU.mult)
                    if p < 4:
                        o = qr[:, pp:pp + 2, :]
                        nc.vector.scalar_tensor_tensor(out=o, in0=o, scalar=gq[:, 1:2], in1=r, op0=ALU.mult,
                                                       op1=ALU.mult).then_inc(gained, 1)
                    else:
                        nc.vector.tensor_tensor(krh[:, pp:pp + 2, :], bcast(kr_base, 1, 2), r,
                                                ALU.mult).then_inc(ready5, 1)

                def rope(p):
                    dve.wait_ge(rot5, p + 1)
                    o = qr[:, 2 * p:2 * p + 2, :]
                    nc.vector.tensor_tensor(tcos[:, p % 2], o, bcast(cosT, 1, 2), ALU.mult)
                    step(nc.vector.tensor_tensor(tsin[:, p % 2], B[4 + p % 2][:, :].rearrange("p (a b) -> p a b", a=2),
                                                 bcast(sinT, 1, 2), ALU.mult))
                    nc.vector.tensor_tensor(o, tcos[:, p % 2], tsin[:, p % 2], ALU.add).then_inc(ready5, 1)

                for p in range(9):
                    if p < 8:
                        gain(p)
                    if 1 <= p <= 4:
                        rope(p - 1)
                att5.dve(dve)
                out5_dve(dve)

        ffn(1, pc("norm_ffn", DC, DC), T["ffn1"], T["ffn1"] + NSLOT, NT)

        memory.open()
        area = Area()
        res = area(TT, D)
        res_turned, res_in, stored = sem("result_turned"), sem("result_placed"), sem("result_stored")
        with nc.Block() as block:
            @block.tensor
            def _(pe):
                for i in range(4):
                    tt, half = i // 2, i % 2
                    for c in range(4):
                        mm = nc.tensor.transpose(B[i][:, c * P:(c + 1) * P],
                                                 x[:, 4 * half + c, tt * P:(tt + 1) * P], ident)
                    mm.then_inc(res_turned, 1)

            @block.vector
            def _(dve):
                for i in range(4):
                    dve.wait_ge(res_turned, i + 1)
                    nc.vector.tensor_copy(res[:, i // 2, (i % 2) * 512:(i % 2 + 1) * 512], B[i][:, :])\
                        .then_inc(res_in, 1)

            @block.sync
            def _(sp):
                for tt in range(TT):
                    sp.wait_ge(res_in, 2 * tt + 2)
                    sp.dma_start(out[0, tt * P:(tt + 1) * P, :], res[:, tt, :]).then_inc(stored, 16)
                sp.wait_ge(stored, 32)


_OUTS = [((1, 256, 1024), 'float32')]
_INS = ['x', 'norm_g', 'fox_w_in', 'fox_b_f', 'fox_w_out', 'nsa_w_in', 'nsa_pe_k', 'nsa_w_ck1', 'nsa_w_ck2',
        'nsa_pe_v', 'nsa_w_cv1', 'nsa_w_cv2', 'nsa_w_out', 'final_g', 'positions_2', 'norm_mix_2', 'norm_ffn_2',
        'hgrn_w_in_2', 'hgrn_lower_bounds_2', 'hgrn_out_norm_2', 'hgrn_w_out_2', 'mla_w_in_2', 'mla_q_a_norm_2',
        'mla_w_q_up_2', 'mla_kv_a_norm_2', 'mla_w_kv_up_2', 'mla_q_norm_2', 'mla_k_norm_2', 'mla_w_out_2',
        'ffn_w_up_2', 'ffn_conv_w_2', 'ffn_conv_b_2', 'ffn_w_down_2']


def kernel(**inputs):
    import numpy as _np
    import concourse.bacc as _bacc
    from concourse import mybir as _mybir
    from concourse.bass_utils import run_bass_kernel_spmd as _run

    nc = _bacc.Bacc("TRN2", target_bir_lowering=False, num_devices=1)
    arrays, args = {}, {}
    consts, at = shape_constants()
    for name, a in [(n, inputs[n]) for n in _INS] + [("consts", consts)]:
        a = _np.ascontiguousarray(a)
        arrays[f"in_{name}_dram"] = a
        args[name] = nc.dram_tensor(f"in_{name}_dram", a.shape, _mybir.dt.from_np(a.dtype), kind="ExternalInput").ap()
    outs = []
    for i, (shape, dtype) in enumerate(_OUTS):
        dt = _mybir.dt.from_np(_np.dtype(dtype))
        outs.append(nc.dram_tensor(f"out_{i}_dram", shape, dt, kind="ExternalOutput").ap())
    build(nc, args, args["consts"], outs[0], at)
    r = _run(nc, [arrays], core_ids=[0])
    return r.results[0]["out_0_dram"]
```

```python
from contextlib import ExitStack

import numpy as np

import concourse.bass as bass
from concourse import mybir

F32 = mybir.dt.float32
F32R = mybir.dt.float32r
BF16 = mybir.dt.bfloat16
I32 = mybir.dt.int32
ALU = mybir.AluOpType
ACT = mybir.ActivationFunctionType
AX = mybir.AxisListType

P = 128
D = 1024
S = 256
TT = S // P
DC = D // P
EPS = 1e-6
BIG = 1e30
LEAST = 1e-37

FOX_H, HD = 16, 64
FOX_F = 3 * D
G, CMP, STRIDE, CLEN, HID = 4, 15, 16, 32, 256
NG = G * CMP
NSA_KC, NSA_VC, NSA_KS, NSA_VS, NSA_KW, NSA_VW, NSA_GATE = [D + 256 * i for i in range(7)]
NSA_Z = NSA_GATE + 3 * FOX_H
HG_H, LEVELS = 8, 7
ML_H, NOPE, ROPE, QK, LORA = 8, 128, 64, 192, 256
FF = 2816
FC = FF // P
UNITS_PER_LOOP = 4

NSLOT = 3
SLOT = 2048
AB = 4
LAG = 3


def shape_constants():
    p = np.arange(P)
    f = np.float32
    cols, at = [], {}

    def put(name, a):
        at[name] = (sum(c.shape[1] for c in cols), a.shape[1])
        cols.append(np.asarray(a, f))

    put("ident", np.eye(P))
    put("tri", p[:, None] <= p[None, :])
    put("ones", np.ones((P, P)))
    put("zero", np.zeros((P, P)))
    put("mask", np.where(p[None, :] > p[:, None], f(BIG), f(0)))
    end = np.arange(CMP) * STRIDE + CLEN - 1
    for t in range(TT):
        put(f"cmask{t}", np.where(end[None, :] > (p + t * P)[:, None], f(BIG), f(0)))
        put(f"cvalid{t}", (end[0] <= p + t * P)[:, None])
    half = HD // 8
    rot = np.zeros((P, P))
    for b in (0, HD):
        for d in range(half):
            rot[b + d + half, b + d] = -1.0
            rot[b + d, b + d + half] = 1.0
    put("rot", rot)
    inv = np.power(f(500000.0), -np.arange(half, dtype=f) * f(2.0 / (2 * half)))
    for name, pos in (("tok", np.arange(S)), ("cmp", np.tile(end, G))):
        ang = pos.astype(f)[None, :] * inv[:, None]
        c, s = np.ones((P, len(pos)), f), np.zeros((P, len(pos)), f)
        for b in (0, half, HD, HD + half):
            c[b:b + half], s[b:b + half] = np.cos(ang), np.sin(ang)
        put("cos_" + name, c)
        put("sin_" + name, s)
    lev, msk = [], []
    for l in range(LEVELS):
        m = 1 << l
        mid = p // (2 * m) * (2 * m) + m - 1
        up = (p & m) > 0
        a = np.where(up[None, :], (p[:, None] > mid[None, :]) & (p[:, None] <= p[None, :]),
                     (p[:, None] > p[None, :]) & (p[:, None] <= mid[None, :]))
        lev.append(a)
        msk.append((~up)[:, None] & up[None, :] & (p[:, None] // (2 * m) == p[None, :] // (2 * m)))
    before = p[:, None] > p[None, :]
    upto = p[:, None] <= p[None, :]
    rot2 = np.zeros((P, P))
    for d in range(ROPE // 2):
        rot2[d + ROPE // 2, d] = -1.0
        rot2[d, d + ROPE // 2] = 1.0
    put("rot2", rot2)
    inv2 = f(10000.0) ** (-np.arange(0, ROPE, 2, dtype=f) / f(ROPE))
    put("inv2", np.where(p < ROPE, inv2[p % (ROPE // 2)], 0)[:, None])
    put("levels", np.concatenate(lev[:4] + [before] + lev[4:] + [upto], 1))
    put("lmask", np.concatenate(msk + [np.eye(P)], 1))
    return np.ascontiguousarray(np.concatenate(cols, 1)), at


def bcast(ap, axis, n):
    a = ap.unsqueeze(axis)
    shape = list(a.shape)
    shape[axis] = n
    return a.broadcast_to(shape)


class Chain:

    def __init__(self, eng, sem):
        self.eng, self.sem, self.n = eng, sem, 0

    def __call__(self, ins):
        self.n += 1
        ins.then_inc(self.sem, 1)
        self.eng.wait_ge(self.sem, self.n)


def build(nc, A, cst_dram, out, at):
    ctx = ExitStack()
    with ctx:
        def sb(name, shape, dt=F32):
            return ctx.enter_context(nc.sbuf_tensor(name, shape, dt))

        def sem(name):
            return ctx.enter_context(nc.semaphore(name))

        B = [ctx.enter_context(nc.psum_tensor(f"bank{i}", [P, 512], F32)) for i in range(8)]
        x = sb("x", [P, DC, S])
        h = sb("h", [P, DC, S])
        h_hi, h_lo = sb("h_high", [P, DC, S], F32R), sb("h_low", [P, DC, S], F32R)
        w_hi, w_lo = sb("w_high", [P, NSLOT, SLOT], F32R), sb("w_low", [P, NSLOT, SLOT], F32R)
        ring = sb("ring", [P, NSLOT, SLOT])
        ncst = at["levels"][0]
        cst = sb("cst", [P, ncst])
        zeros_bf = sb("zeros_bf", [P, 512], BF16)
        eps = sb("eps", [P, 1])
        rstd = sb("rstd", [P, TT])
        WORK = 23 * 1024 - 320
        class Memory:

            def __init__(self):
                self.ctx, self.times = ExitStack(), 0

            def open(self, less=0):
                self.ctx.close()
                self.times += 1
                self.work = self.ctx.enter_context(nc.sbuf_tensor(f"work{self.times}", [P, WORK - less], F32))

            def float32r(self, name, *dims):
                return self.ctx.enter_context(nc.sbuf_tensor(name, [P, *dims], F32R))

            def close(self):
                self.ctx.close()

        memory = Memory()

        def C(name, a=0, b=None):
            o, n = at[name]
            return cst[:, o + a:o + (n if b is None else b)]

        ident, ones = C("ident"), C("ones")

        class Area:

            def __init__(self):
                self.at = 0

            def same(self, n):
                other = Area()
                other.at = self.at - n
                return other

            def __call__(self, *dims):
                n = int(np.prod(dims))
                a = memory.work[:, self.at:self.at + n]
                self.at += n
                assert self.at <= WORK, self.at
                if len(dims) == 1:
                    return a
                names = "abcd"[:len(dims)]
                return a.rearrange(f"p ({' '.join(names)}) -> p {' '.join(names)}",
                                   **dict(zip(names, dims)))

        prows, pcol = [], {}

        def rows(name, ap, n, width=P):
            pcol[name] = len(prows)
            prows.extend((ap, i, n, width) for i in range(n))

        def vec(ap, n):
            return ap.rearrange("(r q) -> r q", q=n)

        rows("norm_g", A["norm_g"].rearrange("l (r q) -> (l r) q", q=P), 2 * DC)
        rows("final_g", vec(A["final_g"], P), DC)
        rows("norm_mix", A["norm_mix_2"].rearrange("l (r q) -> (l r) q", q=P), 2 * DC)
        rows("norm_ffn", A["norm_ffn_2"].rearrange("l (r q) -> (l r) q", q=P), 2 * DC)
        rows("hgrn_norm", A["hgrn_out_norm_2"], 1)
        rows("q_a", vec(A["mla_q_a_norm_2"][0], P), LORA // P)
        rows("kv_a", vec(A["mla_kv_a_norm_2"][0], P), LORA // P)
        for name in ("q", "k"):
            rows(name + "_nope", A[f"mla_{name}_norm_2"][:, 0:NOPE], 1)
            rows(name + "_rope", A[f"mla_{name}_norm_2"][:, NOPE:QK], 1, ROPE)
        for n in "kv":
            rows("pe_" + n, A[f"nsa_pe_{n}"][0].rearrange("(i a) d -> i (a d)", a=2), CLEN // 2)
        n_small = len(prows)
        conv_col = []
        for l in range(2):
            w = A["ffn_conv_w_2"][l].rearrange("j (r q) -> (j r) q", q=P)
            conv_col.append(n_small + 8 * FC * l)
            rows(f"conv_w{l}", w, 6 * FC)
            rows(f"conv_b{l}", vec(A["ffn_conv_b_2"][l], P), 2 * FC)
        NPAR = len(prows)
        par = sb("par", [P, NPAR])
        prow = sb("prow", [P, 6, P])
        groups = [(0, 2 * DC), (2 * DC, n_small - 2 * DC)] + [(n_small + 88 * i, 88) for i in range(4)]
        ctx.callback(memory.close)
        memory.open()

        def pc(name, i=0, n=1):
            return par[:, pcol[name] + i:pcol[name] + i + n]

        tiles = []

        def wtiles(w, c0, width, step=256, kc=DC):
            a = w.rearrange("(c p) n -> p c n", p=P)
            first = len(tiles)
            for c in range(c0, c0 + width, step):
                tiles.append((a[:, :, c:c + step], kc, step))
            return first

        T = {}
        fw = A["fox_w_in"][0]
        T["fox_q"] = wtiles(fw, 0, D)
        T["fox_k"] = wtiles(fw, D, D)
        T["fox_v"] = wtiles(fw, 2 * D, D)
        T["fox_z"] = wtiles(fw, FOX_F + FOX_H, D)
        T["fox_out"] = wtiles(A["fox_w_out"][0], 0, D)
        nw = A["nsa_w_in"][0]
        T["nsa_in"] = wtiles(nw, D, 6 * 256)
        ck = []
        for n, name in enumerate(("nsa_w_ck1", "nsa_w_cv1")):
            a = A[name][0].rearrange("(i p) n -> p i n", p=P)
            ck.append(len(tiles))
            for b in range(2):
                tiles.append((a[:, 8 * b:8 * b + 8, :], 8, HID))
        T["nsa_q"] = wtiles(nw, 0, D)
        T["nsa_z"] = wtiles(nw, NSA_Z, D)
        T["nsa_out"] = wtiles(A["nsa_w_out"][0], 0, D)
        hw = A["hgrn_w_in_2"][0]
        T["hgrn_f"] = wtiles(hw, D, D)
        T["hgrn_q"] = wtiles(hw, 0, D)
        T["hgrn_i"] = wtiles(hw, 2 * D, D)
        T["hgrn_g"] = wtiles(hw, 3 * D, D)
        T["hgrn_out"] = wtiles(A["hgrn_w_out_2"][0], 0, D)

        def ffn_tiles(l):
            up = A["ffn_w_up_2"][l].rearrange("(c p) (e n) -> p e c n", p=P, e=2)
            down = A["ffn_w_down_2"][l].rearrange("(c p) n -> p c n", p=P)
            first = len(tiles)
            for j in range(2):
                tiles.append(("up", up, j))
            for g in range(10):
                tiles.append(("up", up, 2 * g + 2))
                tiles.append(("up", up, 2 * g + 3))
                tiles.append(("down", down, g))
            tiles.append(("down", down, 10))
            return first

        T["ffn0"] = ffn_tiles(0)
        mw = A["mla_w_in_2"][0]
        T["mla_in"] = wtiles(mw, 0, 2 * LORA)
        T["mla_q"] = wtiles(A["mla_w_q_up_2"][0], 0, ML_H * QK, step=4 * QK, kc=2)
        T["mla_kv"] = wtiles(A["mla_w_kv_up_2"][0], 0, ML_H * 256, step=1024, kc=2)
        T["mla_out"] = wtiles(A["mla_w_out_2"][0], 0, D)
        T["ffn1"] = ffn_tiles(1)
        NT = len(tiles)

        def slot(t, kc, n):
            return ring[:, t % NSLOT, 0:kc * n].rearrange("p (k n) -> p k n", k=kc)

        w_loaded = [sem(f"w_loaded{i}") for i in range(NSLOT)]
        high_in = [sem(f"w_high_ready{i}") for i in range(NSLOT)]
        low_in = [sem(f"w_low_ready{i}") for i in range(NSLOT)]
        tile_done = sem("tile_done")
        bank_free = [sem(f"bank_free{i}") for i in range(2)]

        def load(sp, t):
            if t >= NT:
                return
            if t >= NSLOT:
                sp.wait_ge(low_in[t % NSLOT], t // NSLOT)
            src = tiles[t]
            s = w_loaded[t % NSLOT]
            if src[0] == "up":
                sp.dma_start(up_slot(t), src[1][:, :, :, src[2] * P:(src[2] + 1) * P]).then_inc(s, 16)
            elif src[0] == "down":
                sp.dma_start(slot(t, 2, D), src[1][:, 2 * src[2]:2 * src[2] + 2, :]).then_inc(s, 16)
            else:
                sp.dma_start(slot(t, src[1], src[2]), src[0]).then_inc(s, 16)

        def up_slot(t):
            return ring[:, t % NSLOT, :].rearrange("p (e c n) -> p e c n", e=2, c=DC)

        def landed(eng, t, later=0):
            eng.wait_ge(w_loaded[t % NSLOT], later * 32 + 16 * (t // NSLOT + 1))

        def high(act, t, later=0, ops=None):
            if t >= NT:
                return
            landed(act, t, later)
            if t >= NSLOT:
                act.wait_ge(tile_done, later * 6 + t - NSLOT + 1)
            dst, src = w_hi[:, t % NSLOT, :], ring[:, t % NSLOT, :]
            if ops is None:
                i = nc.scalar.activation(dst, src, ACT.Copy)
            else:
                i = ops.tensor_copy(dst, src)
            i.then_inc(high_in[t % NSLOT], 1)

        def low(eng, ops, t, later=0):
            if t >= NT:
                return
            eng.wait_ge(high_in[t % NSLOT], later * 2 + t // NSLOT + 1)
            ops.tensor_tensor(w_lo[:, t % NSLOT, :], ring[:, t % NSLOT, :], w_hi[:, t % NSLOT, :].bitcast(F32),
                              ALU.subtract).then_inc(low_in[t % NSLOT], 1)

        def in_parts(eng, t, later=0):
            eng.wait_ge(low_in[t % NSLOT], later * 2 + t // NSLOT + 1)

        def parts(t, pattern, **dims):
            n = int(np.prod(list(dims.values())))
            return [r[:, t % NSLOT, 0:n].rearrange(pattern, **dims) for r in (w_hi, w_lo)]

        def product3(o, a, b, start, stop, **kw):
            (ah, al), (bh, bl) = a, b
            nc.tensor.matmul(o, ah, bh, start=start, stop=False, **kw)
            nc.tensor.matmul(o, ah, bl, start=False, stop=False, **kw)
            return nc.tensor.matmul(o, al, bh, start=False, stop=stop, **kw)

        def next_high(act, t0):
            high(act, t0)
            high(act, t0 + 1)

        high_step, act_split = sem("high_step"), sem("activations_split")
        steps_taken = {"n": 0}

        def split_chunk(pool, c, src, wait):
            wait()
            steps_taken["n"] += 1
            nc.gpsimd.tensor_copy(h_hi[:, c, :], src[:, c, :]).then_inc(high_step, 1)
            pool.wait_ge(high_step, steps_taken["n"])
            nc.gpsimd.tensor_tensor(h_lo[:, c, :], src[:, c, :], h_hi[:, c, :].bitcast(F32),
                                    ALU.subtract).then_inc(act_split, 1)

        hsp = (h_hi, h_lo)

        turn = {"n": 0}
        bank_of = {}

        def plan_tile(t):
            bank_of[t] = turn["n"]
            turn["n"] += 1

        def pbank(t):
            return B[bank_of[t] % 2]

        def wait_bank(pe, t):
            u = bank_of[t]
            if u >= 2:
                pe.wait_ge(bank_free[u % 2], u // 2)

        def freed(t):
            return bank_free[bank_of[t] % 2]

        def evacuated(eng, t):
            eng.wait_ge(freed(t), bank_of[t] // 2 + 1)

        def by_feature(pe, t, act, ready=None):
            in_parts(pe, t)
            wait_bank(pe, t)
            w = parts(t, "p (c n) -> p c n", c=DC, n=256)
            for j in range(2):
                for c in range(DC):
                    if ready is not None and j == 0:
                        ready(c)
                    mm = product3(pbank(t)[:, j * S:(j + 1) * S], [v[:, c, j * P:(j + 1) * P] for v in w],
                                  [v[:, c, :] for v in act], c == 0, c == DC - 1)
            mm.then_inc(tile_done, 1)

        def by_token(pe, t, act, ready=None):
            in_parts(pe, t)
            wait_bank(pe, t)
            w = parts(t, "p (c n) -> p c n", c=DC, n=256)
            for tt in range(TT):
                for c in range(DC):
                    if ready is not None and tt == 0:
                        ready(c)
                    mm = product3(pbank(t)[:, tt * 256:(tt + 1) * 256], [v[:, c, tt * P:(tt + 1) * P] for v in act],
                                  [v[:, c, :] for v in w], c == 0, c == DC - 1)
            mm.then_inc(tile_done, 1)

        def bank2(t):
            return pbank(t)[:, :].rearrange("p (a b) -> p a b", a=2)

        norms = {"n": 0, "split": 0}
        squared, x_placed, x_added = sem("squared"), sem("x_placed"), sem("ffn_added_to_x")
        n_summed, n_root, n_inv = sem("norm_summed"), sem("norm_root"), sem("norm_inverse")
        n_spread = sem("norm_spread")
        n_ready = sem("norm_ready")
        n_high, n_split, n_split_pool = sem("norm_high_ready"), sem("norm_split"), sem("norm_split_pool")

        def keep_warm(n):
            for _ in range(n):
                nc.tensor.matmul(B[5][:, :], zeros_bf[:, 0:P], zeros_bf[:, :], start=True, stop=True)

        def spread(o, columns):
            for i, column in enumerate(columns):
                mm = nc.tensor.matmul(o[:, i * P:(i + 1) * P], column.broadcast_to([P, P]), ident, start=True,
                                      stop=True)
            return mm

        class Norm:

            def __init__(self, gain, x_ready, dst=None, split=hsp, bank=2):
                self.x_ready = x_ready
                self.row = B[bank][:, S:2 * S]
                self.split = split
                self.n = norms["n"]
                norms["n"] += 1
                self.gain, self.dst = gain, h if dst is None else dst
                if split is not None:
                    self.s = DC * norms["split"]
                    norms["split"] += 1

            def square(self, act, i):
                self.x_ready(act, i)
                nc.scalar.activation(h[:, 2 * i:2 * i + 2, :], x[:, 2 * i:2 * i + 2, :], ACT.Square).then_inc(squared, 1)

            def sums(self, pe, i):
                pe.wait_ge(squared, 4 * self.n + i + 1)
                for c in (2 * i, 2 * i + 1):
                    for tt in range(TT):
                        mm = nc.tensor.matmul(B[2 + tt][:, 0:1], h[:, c, tt * P:(tt + 1) * P], ones[:, 0:1],
                                              start=(c == 0), stop=(c == DC - 1))
                if i == 3:
                    mm.then_inc(n_summed, 1)

            def root(self, act):
                act.wait_ge(n_summed, self.n + 1)
                for tt in range(TT):
                    i = nc.scalar.activation(rstd[:, tt:tt + 1], B[2 + tt][:, 0:1], ACT.Sqrt, scale=1.0 / D,
                                             bias=eps[:, 0:1])
                i.then_inc(n_root, 1)

            def invert(self, dve):
                dve.wait_ge(n_root, self.n + 1)
                nc.vector.reciprocal(rstd[:, :], rstd[:, :]).then_inc(n_inv, 1)

            def spread(self, pe):
                keep_warm(6)
                pe.wait_ge(n_inv, self.n + 1)
                spread(self.row, [rstd[:, tt:tt + 1] for tt in range(TT)]).then_inc(n_spread, 1)

            def act_split(self, act):
                for c in range(DC):
                    self.wait(act, c + 1)
                    nc.scalar.activation(self.split[0][:, c, :], self.dst[:, c, :], ACT.Copy).then_inc(n_high, 1)

            def low(self, eng, ops, c, signal):
                eng.wait_ge(n_high, self.s + c + 1)
                ops.tensor_tensor(self.split[1][:, c, :], self.dst[:, c, :],
                                  self.split[0][:, c, :].bitcast(F32), ALU.subtract).then_inc(signal, 1)

            def pool_split(self, pool):
                for c in range(1, DC, 2):
                    self.low(pool, nc.gpsimd, c, n_split_pool)

            def dve(self, dve):
                dve.wait_ge(n_spread, self.n + 1)
                for c in range(DC):
                    nc.vector.scalar_tensor_tensor(out=self.dst[:, c, :], in0=x[:, c, :],
                                                   scalar=self.gain[:, c:c + 1], in1=self.row,
                                                   op0=ALU.mult, op1=ALU.mult).then_inc(n_ready, 1)
                    if self.split and c >= 2 and c % 2 == 0:
                        self.low(dve, nc.vector, c - 2, n_split)
                if self.split:
                    self.low(dve, nc.vector, DC - 2, n_split)

            def wait(self, eng, chunks):
                eng.wait_ge(n_ready, DC * self.n + chunks)

            def chunk(self, pe):
                if self.split:
                    return lambda c: pe.wait_ge((n_split, n_split_pool)[c % 2], self.s // 2 + c // 2 + 1)
                return lambda c: self.wait(pe, c + 1)

        def after_tiles(name):
            return lambda eng, i: evacuated(eng, T[name] + i)

        nrm = Norm(pc("norm_g", 0, DC), lambda eng, i: eng.wait_ge(x_placed, i + 1))
        nrm2 = Norm(pc("norm_g", DC, DC), after_tiles("fox_out"))
        nrm_f = Norm(pc("final_g", 0, DC), after_tiles("nsa_out"), dst=x, split=None, bank=4)
        nrm3 = Norm(pc("norm_mix", 0, DC), lambda eng, i: nrm_f.wait(eng, 2 * i + 2))
        nrm4 = Norm(pc("norm_ffn", 0, DC), after_tiles("hgrn_out"))
        nrm5 = Norm(pc("norm_mix", DC, DC), lambda eng, i: eng.wait_ge(x_added, i + 1))
        nrm6 = Norm(pc("norm_ffn", DC, DC), after_tiles("mla_out"))

        before = {"units": 0, "groups": 0}
        a_multiplied, a_biased, a_exped = sem("logits_ready"), sem("logits_biased"), sem("weights_exped")
        a_inv, a_scaled, a_turned = sem("sums_inverted"), sem("weights_scaled"), sem("weights_turned")
        a_copied, a_weighed, a_taken = sem("weights_copied"), sem("values_weighed"), sem("output_taken")

        class Attention:

            def __init__(self, area, units, groups, take):
                self.units, self.groups, self.take = units, groups, take
                self.u0, self.g0 = before["units"], before["groups"]
                before["units"] += len(units)
                before["groups"] += groups
                n = len(units)
                self.least, self.sum, self.rsum = area(n, 2), area(n, 2), area(n, 2)
                self.lb, self.pb, self.pt = [area(AB, 512) for _ in range(3)]
                self.last_unit = {}
                for u, unit in enumerate(units):
                    self.last_unit[unit["group"]] = u

            def view(self, buf, u):
                unit = self.units[u]
                if buf is None:
                    return B[2 + u % 2][:, 0:unit["nh"] * unit["w"]].rearrange("p (e k) -> p e k", e=unit["nh"])
                return buf[:, u % AB, 0:unit["nh"] * unit["w"]].rearrange("p (e k) -> p e k", e=unit["nh"])

            def pview(self, u):
                unit = self.units[u]
                if unit.get("pb") is not None:
                    return unit["pb"]
                return self.view(self.pb, u)

            def logits(self, pe, u):
                unit = self.units[u]
                if u >= 2:
                    pe.wait_ge(a_biased, self.u0 + u - 1)
                n = len(unit["qk"])
                o = self.view(None, u)
                for i, (q, k) in enumerate(unit["qk"]):
                    mm = nc.tensor.matmul(o, q, k, start=(i == 0), stop=(i == n - 1))
                mm.then_inc(a_multiplied, 1)

            def bias(self, dve, u):
                unit = self.units[u]
                dve.wait_ge(a_multiplied, self.u0 + u + 1)
                if u >= AB:
                    dve.wait_ge(a_exped, self.u0 + u - AB + 1)
                ps, lb = self.view(None, u), self.view(self.lb, u)
                for e in range(unit["nh"]):
                    i = nc.vector.tensor_tensor_reduce(out=lb[:, e, :], in0=ps[:, e, :], in1=unit["bias"][e],
                                                       scale=1.0, scalar=3e38, op0=ALU.add, op1=ALU.min,
                                                       accum_out=self.least[:, u, e:e + 1])
                i.then_inc(a_biased, 1)

            def exp(self, act, u):
                unit = self.units[u]
                act.wait_ge(a_biased, self.u0 + u + 1)
                if u >= AB:
                    act.wait_ge(a_turned, self.u0 + u - AB + 1)
                lb, pb = self.view(self.lb, u), self.pview(u)
                for e in range(unit["nh"]):
                    i = nc.scalar.activation(pb[:, e, 0:unit["w"]], lb[:, e, :], ACT.Exp, scale=-1.0,
                                             bias=self.least[:, u, e:e + 1],
                                             accum_out=self.sum[:, u, e:e + 1])
                i.then_inc(a_exped, 1)

            def scale(self, dve, u):
                unit = self.units[u]
                dve.wait_ge(a_exped, self.u0 + u + 1)
                nh = unit["nh"]
                nc.vector.reciprocal(self.rsum[:, u, 0:nh], self.sum[:, u, 0:nh]).then_inc(a_inv, 1)
                dve.wait_ge(a_inv, self.u0 + u + 1)
                pb = self.pview(u)
                for e in range(nh):
                    w = pb[:, e, 0:unit["w"]]
                    if unit.get("gate") is None:
                        i = nc.vector.tensor_scalar(w, w, self.rsum[:, u, e:e + 1], None, ALU.mult)
                    else:
                        i = nc.vector.tensor_scalar(w, w, self.rsum[:, u, e:e + 1], unit["gate"][e],
                                                    ALU.mult, ALU.mult)
                i.then_inc(a_scaled, 1)

            def turn(self, pe, u):
                unit = self.units[u]
                pe.wait_ge(a_scaled, self.u0 + u + 1)
                if u >= 2:
                    pe.wait_ge(a_copied, self.u0 + u - 1)
                pb = self.pview(u)
                for i in range(unit["nh"] * unit["nkt"]):
                    e, kt = i // unit["nkt"], i % unit["nkt"]
                    mm = nc.tensor.transpose(B[4 + u % 2][:, i * P:(i + 1) * P],
                                             pb[:, e, kt * P:(kt + 1) * P], ident)
                mm.then_inc(a_turned, 1)

            def copy(self, act, u):
                unit = self.units[u]
                act.wait_ge(a_turned, self.u0 + u + 1)
                if u >= AB:
                    act.wait_ge(a_weighed, self.u0 + u - AB + 1)
                n = unit["nh"] * unit["nkt"] * P
                nc.scalar.activation(self.pt[:, u % AB, 0:n], B[4 + u % 2][:, 0:n], ACT.Copy).then_inc(a_copied, 1)

            def weigh(self, pe, u):
                unit = self.units[u]
                pe.wait_ge(a_copied, self.u0 + u + 1)
                g = unit["group"]
                if unit["first"] and g >= 2:
                    pe.wait_ge(a_taken, self.g0 + g - 1)
                o = B[6 + g % 2]
                rows_e = P // unit["nh"]
                c0 = unit["qt"] * P
                for e in range(unit["nh"]):
                    for kt in range(unit["nkt"]):
                        i = e * unit["nkt"] + kt
                        mm = nc.tensor.matmul(o[e * rows_e:(e + 1) * rows_e, c0:c0 + P], unit["v"](e, kt),
                                              self.pt[:, u % AB, i * P:(i + 1) * P],
                                              start=(unit["open"] and kt == 0),
                                              stop=(unit["close"] and kt == unit["nkt"] - 1))
                mm.then_inc(a_weighed, 1)

            def out(self, dve, g):
                dve.wait_ge(a_weighed, self.u0 + self.last_unit[g] + 1)
                self.take(g, B[6 + g % 2][:, 0:S]).then_inc(a_taken, 1)

            def split(self, pool, src):
                for c in range(DC):
                    split_chunk(pool, c, src, lambda: pool.wait_ge(a_taken, self.g0 + c + 1))

            def pe(self, pe):
                n = len(self.units)
                for u in range(n + LAG + 1):
                    if u < n:
                        self.logits(pe, u)
                    if LAG <= u < n + LAG:
                        self.turn(pe, u - LAG)
                    if u > LAG:
                        self.weigh(pe, u - LAG - 1)

            def act(self, act):
                n = len(self.units)
                for u in range(n + LAG):
                    if u < n:
                        self.exp(act, u)
                    if u >= LAG:
                        self.copy(act, u - LAG)

            def dve(self, dve):
                n = len(self.units)
                ends = {u: g for g, u in self.last_unit.items()}
                for u in range(n + LAG + 2):
                    if u < n:
                        self.bias(dve, u)
                    if 1 <= u <= n:
                        self.scale(dve, u - 1)
                    if u - LAG - 2 in ends:
                        self.out(dve, ends[u - LAG - 2])

        projected = {"n": 0}

        def project_out(t0, nrm):
            for t in range(t0, t0 + 4):
                plan_tile(t)
            n0 = projected["n"]
            projected["n"] += DC

            def pe(pe):
                for t in range(t0, t0 + 4):
                    by_feature(pe, t, hsp, ready=(lambda c: pe.wait_ge(act_split, n0 + c + 1)) if t == t0 else None)
                    if t > t0:
                        nrm.sums(pe, t - t0 - 1)
                nrm.sums(pe, 3)
                nrm.spread(pe)

            def dve(dve):
                for i, t in enumerate(range(t0, t0 + 4)):
                    dve.wait_ge(tile_done, t + 1)
                    xs = x[:, 2 * i:2 * i + 2, :]
                    nc.vector.tensor_tensor(xs, bank2(t), xs, ALU.add).then_inc(freed(t), 1)
                nrm.invert(dve)

            def act(act):
                high(act, t0 + 3)
                nrm.square(act, 0)
                for i in range(2):
                    high(act, t0 + 4 + i)
                    nrm.square(act, 1 + i)
                nrm.square(act, 3)
                nrm.root(act)
            return pe, dve, act

        tapped, convolved, gated = sem("ffn_tapped"), sem("ffn_convolved"), sem("ffn_gated")
        hidden, conv_step = sem("ffn_hidden_ready"), sem("ffn_conv_step")
        product, hidden_high = sem("ffn_hidden_product"), sem("ffn_hidden_high")

        def ffn(l, nrm, following, t0, sp_from, sp_to):
            mem = ExitStack()

            def buf(name, *dims, dt=F32):
                return mem.enter_context(nc.sbuf_tensor(f"ffn{l}_{name}", [P, *dims], dt))

            memory.close()
            act_hi, act_lo = buf("hidden_high", FC, S, dt=F32R), buf("hidden_low", FC, S, dt=F32R)
            y, sg, hid32 = buf("conv", 2, 2, S), buf("gate", 2, S), buf("hidden", 2, S)
            NTILE = 33
            p0 = l * FC
            u0 = turn["n"]
            turn["n"] += FC
            cw, cb = pcol[f"conv_w{l}"], pcol[f"conv_b{l}"]
            NLOOP = 5

            def column(base, e, j, later):
                c = base + e * FC + j
                return par[:, c:c + 1] if isinstance(later, int) else par[:, bass.ds(later * 4 + c, 1)]

            def pair_tile(j):
                return t0 + (j if j < 2 else 2 + (j - 2) // 2 * 3 + (j - 2) % 2)

            def pair(pe, j, later=0, ready=None):
                t, u = pair_tile(j), u0 + j
                in_parts(pe, t, later)
                if u >= 2:
                    pe.wait_ge(bank_free[u % 2], later * 2 + u // 2)
                w = parts(t, "p (e c n) -> p e c n", e=2, c=DC, n=P)
                for e in range(2):
                    for c in range(DC):
                        if ready and e == 0:
                            ready(c)
                        mm = product3(B[u % 2][:, e * S:(e + 1) * S], [v[:, e, c, :] for v in w],
                                      [v[:, c, :] for v in (h_hi, h_lo)], c == 0, c == DC - 1)
                mm.then_inc(tile_done, 1)

            def step_down(pe, g, later=0, last=False):
                t = t0 + 4 + 3 * g if g < 10 else t0 + 32
                in_parts(pe, t, later)
                pe.wait_ge(hidden, p0 + later * 4 + 2 * g + 2)
                w = parts(t, "p (k n) -> p k n", k=2, n=D)
                for k in range(2):
                    c = 2 * g + k
                    a = [v[:, c, :] if isinstance(later, int) else v[:, bass.ds(later * 4 + c, 1), :]
                         for v in (act_hi, act_lo)]
                    for o in range(DC):
                        mm = product3(B[4 + o // 2][:, (o % 2) * S:(o % 2 + 1) * S],
                                      [v[:, k, o * P:(o + 1) * P] for v in w], a, False, last and k == 1,
                                      skip_group_check=True)
                mm.then_inc(tile_done, 1)

            def tap(act, j, later=0):
                t, u = pair_tile(j), u0 + j
                act.wait_ge(tile_done, later * 6 + t + 1)
                if not (isinstance(later, int) and j < 2):
                    act.wait_ge(hidden, p0 + later * 4 + j - 1)
                for e in range(2):
                    i = nc.scalar.activation(y[:, j % 2, e, :], B[u % 2][:, e * S:(e + 1) * S], ACT.Identity,
                                             scale=column(cw + 4 * FC, e, j, later),
                                             bias=column(cb, e, j, later))
                i.then_inc(tapped, 1)

            def gate(act, j, later=0):
                act.wait_ge(convolved, p0 + later * 4 + j + 1)
                nc.scalar.activation(sg[:, j % 2, :], y[:, j % 2, 0, :], ACT.Silu).then_inc(gated, 1)

            def convolve(dve, j, later=0):
                u = u0 + j
                dve.wait_ge(tapped, p0 + later * 4 + j + 1)
                for back in (1, 2):
                    for e in range(2):
                        dst = y[:, j % 2, e, back:S]
                        i = nc.vector.scalar_tensor_tensor(
                            out=dst, in0=B[u % 2][:, e * S:(e + 1) * S - back],
                            scalar=column(cw + (2 - back) * 2 * FC, e, j, later), in1=dst,
                            op0=ALU.mult, op1=ALU.add)
                        if back == 1:
                            i.then_inc(conv_step, 1)
                        elif e == 0:
                            i.then_inc(convolved, 1)
                        else:
                            i.then_inc(bank_free[u % 2], 1)
                    if back == 1:
                        dve.wait_ge(conv_step, 2 * p0 + later * 8 + 2 * j + 2)

            def multiply(dve, j, later=0):
                u = u0 + j
                dve.wait_ge(gated, p0 + later * 4 + j + 1)
                dve.wait_ge(bank_free[u % 2], later * 2 + u // 2 + 1)
                ah, al = [v[:, j, :] if isinstance(later, int) else v[:, bass.ds(later * 4 + j, 1), :].squeeze(1)
                          for v in (act_hi, act_lo)]
                a = hid32[:, j % 2, :]
                nc.vector.tensor_tensor(a, sg[:, j % 2, :], y[:, j % 2, 1, :], ALU.mult).then_inc(product, 1)
                dve.wait_ge(product, p0 + later * 4 + j + 1)
                nc.vector.tensor_copy(ah, a).then_inc(hidden_high, 1)
                dve.wait_ge(hidden_high, p0 + later * 4 + j + 1)
                nc.vector.tensor_tensor(al, a, ah.bitcast(F32), ALU.subtract).then_inc(hidden, 1)
                dve.wait_ge(hidden, p0 + later * 4 + j + 1)

            def load_ffn(sp, off, later=0):
                t = t0 + off
                sp.wait_ge(low_in[t % NSLOT], later * 2 + t // NSLOT)
                kind, src, n = tiles[t]
                s = w_loaded[t % NSLOT]
                if kind == "up":
                    sp.dma_start(up_slot(t), src[:, :, :, bass.ds(later * (4 * P) + n * P, P)]).then_inc(s, 16)
                else:
                    sp.dma_start(slot(t, 2, D), src[:, bass.ds(later * 4 + 2 * n, 2), :]).then_inc(s, 16)

            with nc.Block() as block:
                @block.sync
                def _(sp):
                    for t in range(sp_from, t0 + 5):
                        load(sp, t)
                    with sp.Fori(0, 4) as i:
                        for off in range(5, 11):
                            load_ffn(sp, off, i)
                    for t in range(t0 + 29, sp_to):
                        load(sp, t)

                @block.tensor
                def _(pe):
                    keep_warm(12)
                    for b in range(4, 8):
                        nc.tensor.matmul(B[b][:, :], zeros_bf[:, 0:P], zeros_bf[:, :], start=True, stop=False,
                                         skip_group_check=True)
                    pair(pe, 0, ready=nrm.chunk(pe))
                    pair(pe, 1)
                    with pe.Fori(0, NLOOP) as i:
                        for g in range(2):
                            pair(pe, 2 * g + 2, i)
                            pair(pe, 2 * g + 3, i)
                            step_down(pe, g, i)
                    step_down(pe, 10, last=True)
                    if following:
                        for i in range(4):
                            following.sums(pe, i)
                        following.spread(pe)

                @block.gpsimd
                def _(pool):
                    nrm.pool_split(pool)
                    for j in range(2, 4):
                        low(pool, nc.gpsimd, pair_tile(j))
                    with pool.Fori(0, 4) as i:
                        for r in range(4):
                            low(pool, nc.gpsimd, pair_tile(4 + r), i)
                    for j in (FC - 2, FC - 1):
                        low(pool, nc.gpsimd, pair_tile(j))
                    low(pool, nc.gpsimd, t0 + NTILE)
                    low(pool, nc.gpsimd, t0 + NTILE + 1)

                @block.scalar
                def _(act):
                    nrm.act_split(act)
                    high(act, t0 + 2)
                    tap(act, 0)
                    high(act, t0 + 3)
                    tap(act, 1)
                    high(act, t0 + 4)
                    gate(act, 0)

                    def high_ahead(act, off, later):
                        if off < NTILE:
                            high(act, t0 + off, later)

                    def two_pairs(r, off, later=0):
                        tap(act, r, later)
                        high_ahead(act, off, later)
                        gate(act, r - 1, later)
                        tap(act, r + 1, later)
                        high_ahead(act, off + 1, later)
                        gate(act, r, later)
                        high_ahead(act, off + 2, later)

                    with act.Fori(0, NLOOP - 1) as i:
                        for g in range(2):
                            two_pairs(2 + 2 * g, 5 + 3 * g, i)
                    for g in range(2):
                        two_pairs(18 + 2 * g, 29 + 3 * g)
                    gate(act, FC - 1)
                    next_high(act, t0 + NTILE)
                    if following:
                        for i in range(4):
                            following.square(act, i)
                        following.root(act)

                @block.vector
                def _(dve):
                    nrm.dve(dve)
                    convolve(dve, 0)
                    convolve(dve, 1)
                    low(dve, nc.vector, t0 + 4)
                    multiply(dve, 0)

                    def two_pairs(r, off, later=0):
                        for k in range(2):
                            convolve(dve, r + k, later)
                            multiply(dve, r + k - 1, later)
                        if off < NTILE:
                            low(dve, nc.vector, t0 + off, later)

                    with dve.Fori(0, NLOOP - 1) as i:
                        for g in range(2):
                            two_pairs(2 + 2 * g, 7 + 3 * g, i)
                    two_pairs(18, 31)
                    two_pairs(20, 32)
                    multiply(dve, FC - 1)
                    dve.wait_ge(tile_done, t0 + 33)
                    for o in range(4):
                        xs = x[:, 2 * o:2 * o + 2, :]
                        nc.vector.tensor_tensor(xs, B[4 + o][:, :].rearrange("p (a b) -> p a b", a=2), xs,
                                                ALU.add).then_inc(x_added, 1)
                    if following:
                        following.invert(dve)
            mem.close()

        area = Area()
        x_tok = area(TT, D)
        loaded_c, loaded_c2 = sem("constants_loaded"), sem("late_constants_loaded")
        loaded_x, loaded_p = sem("x_loaded"), sem("params_loaded")
        cleared, x_turned = sem("cleared"), sem("x_turned")
        p_turned, p_placed = sem("params_turned"), sem("params_placed")
        loaded_p2 = sem("late_params_loaded")
        n_late = []

        def load_params(eng, some, signal):
            n = 0
            for g in some:
                r0, count = groups[g]
                r = r0
                while r < r0 + count:
                    ap, i, total, width = prows[r]
                    m = min(total - i, r0 + count - r)
                    eng.dma_start(prow[r - r0:r - r0 + m, g, 0:width], ap[i:i + m, :]).then_inc(signal, 16)
                    r += m
                    n += 1
            return n

        def turn_params(o, some, first):
            for g in some:
                r0, count = groups[g]
                mm = nc.tensor.transpose(o[:, r0 - first:r0 - first + count], prow[0:count, g, :],
                                         ident[0:count, 0:count])
            return mm
        with nc.Block() as block:
            @block.sync
            def _(sp):
                sp.dma_start(x_tok, A["x"][0].rearrange("(t p) d -> p t d", p=P)).then_inc(loaded_x, 16)
                sp.dma_start(cst[:, 0:640], cst_dram[:, 0:640]).then_inc(loaded_c, 16)
                for t in range(NSLOT):
                    load(sp, t)
                sp.dma_start(cst[:, 640:], cst_dram[:, 640:ncst]).then_inc(loaded_c2, 16)

            @block.gpsimd
            def _(pool):
                nc.gpsimd.memset(prow[:, 1, :], 0.0).then_inc(cleared, 1)
                nc.gpsimd.memset(zeros_bf[:, :], 0.0)
                nc.gpsimd.memset(eps[:, :], EPS).then_inc(cleared, 1)
                low(pool, nc.gpsimd, 0)

            @block.scalar
            def _(act):
                load_params(act, (0,), loaded_p)
                act.wait_ge(cleared, 1)
                n_late.append(load_params(act, (1,), loaded_p2))
                for i in range(4):
                    nrm.square(act, i)
                high(act, 1)
                act.wait_ge(cleared, 2)
                nrm.root(act)

            @block.tensor
            def _(pe):
                pe.wait_ge(cleared, 2)
                keep_warm(12)
                pe.wait_ge(loaded_x, 16)
                pe.wait_ge(loaded_c, 16)
                for c in range(DC):
                    for tt in range(TT):
                        mm = nc.tensor.transpose(B[4 + c // 2][:, (c % 2) * S + tt * P:(c % 2) * S + (tt + 1) * P],
                                                 x_tok[:, tt, c * P:(c + 1) * P], ident)
                    if c % 2:
                        mm.then_inc(x_turned, 1)
                pe.wait_ge(loaded_p, 16)
                turn_params(B[0], (0,), 0).then_inc(p_turned, 1)
                pe.wait_ge(x_placed, 4)
                keep_warm(4)
                for i in range(4):
                    nrm.sums(pe, i)
                nrm.spread(pe)

            @block.vector
            def _(dve):
                for i in range(4):
                    dve.wait_ge(x_turned, i + 1)
                    nc.vector.tensor_copy(x[:, 2 * i:2 * i + 2, :],
                                          B[4 + i][:, :].rearrange("p (a b) -> p a b", a=2)).then_inc(x_placed, 1)
                high(dve, 0, ops=nc.vector)
                low(dve, nc.vector, 1)
                nrm.invert(dve)
                dve.wait_ge(p_turned, 1)
                nc.vector.tensor_copy(par[:, 0:2 * DC], B[0][:, 0:2 * DC])

        memory.open()
        area = Area()
        w_f = area(DC, FOX_H)
        b_f = area(FOX_H)
        f_raw, f_abs, f_exp, f_log = [area(TT * FOX_H) for _ in range(4)]
        logf = area(TT, FOX_H)
        c_q = area(TT, FOX_H)
        qT = area(DC, S)
        zT = h
        kz = area(FOX_H, S)
        v = area(TT, D)
        cm0, cm1 = area(FOX_H, P), area(FOX_H, S)
        fl, fps = sem("fox_f_loaded"), sem("fox_f_product")
        f_steps, f_steps_a = sem("fox_f_steps"), sem("fox_f_act")
        logf_ready, cq_ps, cq_ready = sem("logf_ready"), sem("c_q_product"), sem("c_q_ready")
        ck_ps, ck_used = sem("c_k_product"), sem("c_k_used")
        kz_clear = sem("fox_keys_clear")
        fq, fk, fv, fz = T["fox_q"], T["fox_k"], T["fox_v"], T["fox_z"]
        for t in range(fq, fz + 4):
            plan_tile(t)

        def masks(qt):
            o, n = at["zero"]
            return cst[:, o:o + S] if qt else C("mask")

        units = []
        for c in range(DC):
            for qt in range(TT):
                w = (qt + 1) * P
                cm = (cm0, cm1)[qt]
                units.append(dict(
                    group=c, qt=qt, nh=2, w=w, nkt=qt + 1, first=(qt == 0), open=True, close=True,
                    qk=[(qT[:, c, qt * P:(qt + 1) * P], kz[:, 2 * c:2 * c + 2, 0:w])],
                    bias=[cm[:, 2 * c + e, :] for e in range(2)],
                    v=lambda e, kt, c=c: v[:, kt, (2 * c + e) * HD:(2 * c + e + 1) * HD]))
        att = Attention(area, units, DC,
                        lambda g, ps: nc.vector.tensor_tensor(zT[:, g, :], ps, zT[:, g, :], ALU.mult))
        out_pe, out_dve, out_act = project_out(T["fox_out"], nrm2)

        with nc.Block() as block:
            @block.sync
            def _(sp):
                sp.dma_start(w_f, fw.rearrange("(c p) n -> p c n", p=P)[:, :, FOX_F:FOX_F + FOX_H]).then_inc(fl, 16)
                sp.dma_start(b_f, A["fox_b_f"].broadcast_to([P, FOX_H])).then_inc(fl, 16)
                n_late.append(load_params(sp, range(2, 6), loaded_p2))
                for t in range(NSLOT, T["fox_out"] + 4 + NSLOT):
                    load(sp, t)

            @block.gpsimd
            def _(pool):
                nrm.pool_split(pool)
                low(pool, nc.gpsimd, fq + 2)
                nc.gpsimd.memset(kz, 0.0).then_inc(kz_clear, 1)
                for t in range(fq + 3, T["fox_out"] + 3):
                    low(pool, nc.gpsimd, t)
                att.split(pool, zT)
                for t in range(T["fox_out"] + 3, T["fox_out"] + 6):
                    low(pool, nc.gpsimd, t)

            @block.tensor
            def _(pe):
                keep_warm(12)
                pe.wait_ge(fl, 32)
                for tt in range(TT):
                    for c in range(DC):
                        if tt == 0:
                            nrm.wait(pe, c + 1)
                        mm = nc.tensor.matmul(B[6][:, tt * FOX_H:(tt + 1) * FOX_H], h[:, c, tt * P:(tt + 1) * P],
                                              w_f[:, c, :], start=(c == 0), stop=(c == DC - 1))
                mm.then_inc(fps, 1)
                for t in range(fq, fq + 4):
                    by_feature(pe, t, hsp, ready=nrm.chunk(pe) if t == fq else None)
                pe.wait_ge(logf_ready, 1)
                nc.tensor.matmul(B[6][:, 0:FOX_H], C("tri"), logf[:, 0, :], start=True, stop=True)
                nc.tensor.matmul(B[6][:, FOX_H:2 * FOX_H], ones, logf[:, 0, :], start=True, stop=False)
                nc.tensor.matmul(B[6][:, FOX_H:2 * FOX_H], C("tri"), logf[:, 1, :], start=False,
                                 stop=True).then_inc(cq_ps, 1)
                tri_ones = cst[:, at["tri"][0]:at["tri"][0] + S]
                for n in range(FOX_H):
                    if n >= 2:
                        pe.wait_ge(ck_used, n - 1)
                    o = B[4 + n % 2]
                    nc.tensor.matmul(o[:, 0:S], logf[:, 0, n:n + 1].broadcast_to([P, P]), tri_ones,
                                     start=True, stop=False)
                    nc.tensor.matmul(o[:, P:S], logf[:, 1, n:n + 1].broadcast_to([P, P]), C("tri"),
                                     start=False, stop=True).then_inc(ck_ps, 1)
                    if n % 4 == 3:
                        by_feature(pe, fk + n // 4, hsp)
                for t in range(fv, fv + 4):
                    by_token(pe, t, hsp)
                for t in range(fz, fz + 4):
                    by_feature(pe, t, hsp)
                evacuated(pe, fz + 3)
                att.pe(pe)
                out_pe(pe)

            @block.scalar
            def _(act):
                nrm.act_split(act)
                high(act, fq + 2)
                act.wait_ge(f_steps, 2)
                nc.scalar.activation(f_exp, f_abs, ACT.Exp).then_inc(f_steps_a, 1)
                act.wait_ge(f_steps_a, 1)
                nc.scalar.activation(f_log, f_exp, ACT.Ln, bias=ones[:, 0:1]).then_inc(f_steps_a, 1)
                for i in range(4):
                    act.wait_ge(tile_done, fq + i + 1)
                    nc.scalar.activation(qT[:, 2 * i:2 * i + 2, :], bank2(fq + i), ACT.Copy,
                                         scale=-(HD ** -0.5)).then_inc(freed(fq + i), 1)
                    high(act, fq + i + 3)
                act.wait_ge(kz_clear, 1)
                for i in range(4):
                    act.wait_ge(tile_done, fk + i + 1)
                    k4 = kz[:, 4 * i:4 * i + 4, :].rearrange("p (c e) t -> p c e t", e=2)
                    b = bank2(fk + i)
                    nc.scalar.activation(k4[0:HD, :, 0, :], b[0:HD], ACT.Copy)
                    nc.scalar.activation(k4[HD:P, :, 1, :], b[HD:P], ACT.Copy).then_inc(freed(fk + i), 1)
                    high(act, fk + i + 3)
                for i in range(4):
                    act.wait_ge(tile_done, fv + i + 1)
                    nc.scalar.activation(v[:, :, i * 256:(i + 1) * 256], bank2(fv + i), ACT.Copy)\
                        .then_inc(freed(fv + i), 1)
                    high(act, fv + i + 3)
                for i in range(4):
                    act.wait_ge(tile_done, fz + i + 1)
                    a = nc.scalar.activation(zT[:, 2 * i:2 * i + 2, :], bank2(fz + i), ACT.Silu)
                    a.then_inc(freed(fz + i), 1)
                    if i < 3:
                        high(act, fz + i + 3)
                high(act, fz + 6)
                att.act(act)
                out_act(act)

            @block.vector
            def _(dve):
                nrm.dve(dve)
                dve.wait_ge(fps, 1)
                step = Chain(dve, f_steps)
                fr = f_raw.rearrange("p (t n) -> p t n", t=TT)
                step(nc.vector.tensor_tensor(fr, B[6][:, 0:TT * FOX_H].rearrange("p (t n) -> p t n", t=TT),
                                             bcast(b_f, 1, TT), ALU.add))
                step(nc.vector.scalar_tensor_tensor(out=f_abs, in0=f_raw, scalar=-1.0, in1=f_raw, op0=ALU.mult,
                                                    op1=ALU.min))
                dve.wait_ge(f_steps_a, 2)
                nc.vector.scalar_tensor_tensor(out=logf.rearrange("p t n -> p (t n)"), in0=f_raw, scalar=0.0,
                                               in1=f_log, op0=ALU.min, op1=ALU.subtract).then_inc(logf_ready, 1)
                dve.wait_ge(cq_ps, 1)
                nc.vector.tensor_copy(c_q.rearrange("p t n -> p (t n)"), B[6][:, 0:TT * FOX_H]).then_inc(cq_ready, 1)
                dve.wait_ge(cq_ready, 1)
                for n in range(FOX_H):
                    dve.wait_ge(ck_ps, n + 1)
                    o = B[4 + n % 2]
                    nc.vector.scalar_tensor_tensor(out=cm0[:, n, :], in0=o[:, 0:P], scalar=c_q[:, 0, n:n + 1],
                                                   in1=masks(0), op0=ALU.subtract, op1=ALU.add)
                    nc.vector.scalar_tensor_tensor(out=cm1[:, n, :], in0=o[:, 0:S], scalar=c_q[:, 1, n:n + 1],
                                                   in1=masks(1), op0=ALU.subtract, op1=ALU.add).then_inc(ck_used, 1)
                dve.wait_ge(ck_used, FOX_H)
                evacuated(dve, fz + 3)
                att.dve(dve)
                out_dve(dve)

        memory.open(less=CLEN * P)
        b_hi, b_lo = [memory.float32r("blocks_" + n, CLEN // 2, P) for n in ("high", "low")]
        area = Area()
        raw_c = area(2, 2, S)
        xs2 = area(2, 2, 2, S)
        xb = area(CLEN // 2, P)
        raw_k = [area(2, S) for _ in range(2)]
        roped_k = [area(2, S) for _ in range(2)]
        t_cos, t_sin = area(2, S), area(2, S)
        att_area = area.same((4 + 8 + 3 * 4) * S + CLEN // 2 * P)
        kz2 = [area(2, 2, 2, S) for _ in range(2)]
        v2 = [area(TT, 256) for _ in range(2)]
        raw_q, qT = area(4, S), area(DC, S)
        zT = h
        w_gate = area(DC, 3 * FOX_H)
        gate, gatec = area(TT, 3 * FOX_H), area(TT, 3 * FOX_H)
        w2k, w2v = area(2, 2, HD), area(2, HD)
        hid_t, hid = area(HID), area(2, P)
        raw_kc, cos_kc, sin_kc = area(NG), area(NG), area(NG)
        kzc = area(G, 2, CMP)
        vcm = area(G, HD)
        pbc = [area(2, P) for _ in range(2)]
        t_in, t_q, t_z = T["nsa_in"], T["nsa_q"], T["nsa_z"]
        for t in list(range(t_in, t_in + 6)) + list(range(t_q, t_z + 4)):
            plan_tile(t)
        small2, moved_x = sem("nsa_small_loaded"), sem("nsa_blocks_moved")
        moved_k = [sem("nsa_sel_keys_moved"), sem("nsa_win_keys_moved")]
        clear2, xb_clear = sem("nsa_cleared"), sem("blocks_cleared")
        rotated, roped, rope_step = sem("nsa_rotated"), sem("nsa_roped"), sem("nsa_rope_step")
        gate_ps, gate_in, gate_out = sem("gate_product"), sem("gate_sigmoid"), sem("gate_masked")
        block_high, block_split = sem("blocks_high"), sem("blocks_split")
        hid_turned = sem("hidden_turned")
        blocked, hid_in = sem("blocks_ready"), sem("hidden_ready")
        cmp_ps, cmp_raw, cmp_rot = sem("cmp_product"), sem("cmp_raw"), sem("cmp_rotated")
        cmp_k, cmp_step = sem("cmp_keys_ready"), sem("cmp_step")
        ropes = [(raw_k[0], roped_k[0]), (raw_k[1], roped_k[1])] + \
            [(raw_q[:, 2 * (i % 2):2 * (i % 2) + 2, :], qT[:, 2 * i:2 * i + 2, :]) for i in range(4)]
        raw_tile = [t_in + 2, t_in + 4] + [t_q + i for i in range(4)]

        units = []
        for c in range(DC):
            g = c // 2
            for qt in range(TT):
                w = (qt + 1) * P
                q = qT[:, c, qt * P:(qt + 1) * P]
                for br in (1, 2):
                    kz_b, v_b = kz2[br - 1], v2[br - 1]
                    units.append(dict(
                        group=c, qt=qt, nh=2, w=w, nkt=qt + 1, first=(qt == 0 and br == 1), open=(br == 1),
                        close=False, qk=[(q, kz_b[:, g // 2, g % 2, :, 0:w])], bias=[masks(qt)] * 2,
                        gate=[gate[:, qt, 3 * (2 * c + e) + br:3 * (2 * c + e) + br + 1] for e in range(2)],
                        v=lambda e, kt, g=g, v_b=v_b: v_b[:, kt, g * HD:(g + 1) * HD]))
                units.append(dict(
                    group=c, qt=qt, nh=2, w=CMP, nkt=1, first=False, open=False, close=True,
                    qk=[(q, kzc[:, g, :, :])], bias=[C(f"cmask{qt}")] * 2,
                    gate=[gatec[:, qt, 3 * (2 * c + e):3 * (2 * c + e) + 1] for e in range(2)],
                    v=lambda e, kt, g=g: vcm[:, g, :], pb=pbc[(2 * c + qt) % 2]))
        att2 = Attention(att_area, units, DC,
                         lambda g, ps, zT=zT: nc.vector.tensor_tensor(zT[:, g, :], ps, zT[:, g, :], ALU.mult))
        out2_pe, out2_dve, out2_act = project_out(T["nsa_out"], nrm_f)

        with nc.Block() as block:
            @block.sync
            def _(sp):
                sp.dma_start(w_gate, nw.rearrange("(c p) n -> p c n", p=P)[:, :, NSA_GATE:NSA_Z]).then_inc(small2, 16)
                for e in range(2):
                    sp.dma_start(w2k[:, :, e, :], A["nsa_w_ck2"][0].rearrange("(c p) n -> p c n", p=P))\
                        .then_inc(small2, 16)
                sp.dma_start(w2v, A["nsa_w_cv2"][0].rearrange("(c p) n -> p c n", p=P)).then_inc(small2, 16)
                for t in range(T["fox_out"] + 4 + NSLOT, T["nsa_out"] + 4 + NSLOT):
                    load(sp, t)
                    if t == t_in + 6:
                        evacuated(sp, t_in)
                        evacuated(sp, t_in + 1)
                        for par_g in range(2):
                            src = raw_c[par_g * HD:(par_g + 1) * HD]
                            for n in range(2):
                                sp.dma_start(xs2[0:HD, n, :, par_g, :], src[:, n]).then_inc(moved_x, 16)
                                sp.dma_start(xs2[HD:P, n, :, par_g, 0:S - 1], src[:, n, :, 1:S])\
                                    .then_inc(moved_x, 16)
                    if t in (t_in + 8, t_in + 10):
                        b = (t - t_in - 8) // 2
                        sp.wait_ge(clear2, 1)
                        sp.wait_ge(roped, b + 1)
                        for par_g in range(2):
                            for e in range(2):
                                sp.dma_start(kz2[b][e * HD:(e + 1) * HD, :, par_g, e, :],
                                             roped_k[b][par_g * HD:(par_g + 1) * HD]).then_inc(moved_k[b], 16)

            @block.gpsimd
            def _(pool):
                nrm2.pool_split(pool)
                low(pool, nc.gpsimd, t_in + 2)
                nc.gpsimd.memset(xb, 0.0).then_inc(xb_clear, 1)
                for b in (*kz2, kzc, *pbc):
                    nc.gpsimd.memset(b, 0.0)
                nc.gpsimd.memset(vcm, 0.0).then_inc(clear2, 1)
                for t in range(t_in + 3, T["nsa_out"] + 3):
                    low(pool, nc.gpsimd, t)
                att2.split(pool, zT)
                for t in range(T["nsa_out"] + 3, T["nsa_out"] + 6):
                    low(pool, nc.gpsimd, t)

            @block.tensor
            def _(pe):
                def rotate(r):
                    evacuated(pe, raw_tile[r])
                    if r >= 2:
                        pe.wait_ge(roped, r - 1)
                    nc.tensor.matmul(B[4 + r % 2][:, :], C("rot"), ropes[r][0], start=True,
                                     stop=True).then_inc(rotated, 1)

                def hidden(n):
                    pe.wait_ge(block_split, 1)
                    for i in range(CLEN // 2):
                        t = ck[n] + i // 8
                        if i % 8 == 0:
                            in_parts(pe, t)
                        mm = product3(B[2 + n][:, 0:HID], [v[:, i, :] for v in (b_hi, b_lo)],
                                      [v[:, i % 8, :] for v in parts(t, "p (i n) -> p i n", i=8, n=HID)],
                                      i == 0, i == CLEN // 2 - 1)
                        if i % 8 == 7:
                            mm.then_inc(tile_done, 1)

                keep_warm(12)
                pe.wait_ge(loaded_p2, 16 * sum(n_late))
                turn_params(B[6], range(1, 6), 2 * DC).then_inc(p_turned, 1)
                by_feature(pe, t_in, hsp, ready=nrm2.chunk(pe))
                by_feature(pe, t_in + 1, hsp)
                by_feature(pe, t_in + 2, hsp)
                by_token(pe, t_in + 3, hsp)
                rotate(0)
                by_feature(pe, t_in + 4, hsp)
                by_token(pe, t_in + 5, hsp)
                rotate(1)
                hidden(0)
                hidden(1)
                pe.wait_ge(small2, 64)
                for tt in range(TT):
                    for c in range(DC):
                        mm = nc.tensor.matmul(B[6][:, tt * 48:(tt + 1) * 48], h[:, c, tt * P:(tt + 1) * P],
                                              w_gate[:, c, :], start=(c == 0), stop=(c == DC - 1))
                mm.then_inc(gate_ps, 1)
                by_feature(pe, t_q, hsp)
                pe.wait_ge(hid_in, 2)
                for j in range(2):
                    mm = nc.tensor.transpose(B[2][:, j * P:(j + 1) * P], hid_t[:, j * P:(j + 1) * P], ident)
                mm.then_inc(hid_turned, 1)
                by_feature(pe, t_q + 1, hsp)
                pe.wait_ge(hid_in, 3)
                pe.wait_ge(gate_in, 1)
                for j in range(2):
                    nc.tensor.matmul(B[6][:, 0:NG], w2k[:, j].rearrange("p e d -> p (e d)"), hid[:, j, 0:NG],
                                     start=(j == 0), stop=(j == 1))
                for g in range(G):
                    for j in range(2):
                        mm = nc.tensor.matmul(B[7][0:CMP, g * HD:(g + 1) * HD],
                                              hid[:, j, HD + g * CMP:HD + (g + 1) * CMP],
                                              w2v[:, j, :], start=(j == 0), stop=(j == 1))
                mm.then_inc(cmp_ps, 1)
                rotate(2)
                pe.wait_ge(cmp_raw, 1)
                nc.tensor.matmul(B[2][:, 0:NG], C("rot"), raw_kc, start=True, stop=True).then_inc(cmp_rot, 1)
                by_feature(pe, t_q + 2, hsp)
                rotate(3)
                by_feature(pe, t_q + 3, hsp)
                rotate(4)
                by_feature(pe, t_z, hsp)
                rotate(5)
                for t in range(t_z + 1, t_z + 4):
                    by_feature(pe, t, hsp)
                pe.wait_ge(roped, 6)
                pe.wait_ge(cmp_k, 1)
                for b in range(2):
                    pe.wait_ge(moved_k[b], 64)
                evacuated(pe, t_z + 3)
                att2.pe(pe)
                out2_pe(pe)

            @block.scalar
            def _(act):
                def evac(t, dst, func=ACT.Copy, scale=1.0):
                    act.wait_ge(tile_done, t + 1)
                    nc.scalar.activation(dst, bank2(t), func, scale=scale).then_inc(freed(t), 1)
                    if t < t_z + 3:
                        high(act, t + 3)

                nrm2.act_split(act)
                high(act, t_in + 2)
                evac(t_in, raw_c[:, 0])
                evac(t_in + 1, raw_c[:, 1])
                evac(t_in + 2, raw_k[0])
                evac(t_in + 3, v2[0])
                evac(t_in + 4, raw_k[1])
                evac(t_in + 5, v2[1])
                for n in range(2):
                    for k in range(2):
                        act.wait_ge(tile_done, ck[n] + k + 1)
                        if k:
                            rows = slice(n * HD, (n + 1) * HD)
                            nc.scalar.activation(hid_t[rows], B[2 + n][rows, 0:HID], ACT.Silu).then_inc(hid_in, 1)
                        high(act, ck[n] + k + 3)
                act.wait_ge(gate_ps, 1)
                nc.scalar.activation(gate, B[6][:, 0:96].rearrange("p (t n) -> p t n", t=TT),
                                     ACT.Sigmoid).then_inc(gate_in, 1)
                evac(t_q, raw_q[:, 0:2, :], scale=-(HD ** -0.5))
                act.wait_ge(hid_turned, 1)
                nc.scalar.activation(hid, B[2][:, 0:2 * P].rearrange("p (j c) -> p j c", j=2),
                                     ACT.Copy).then_inc(hid_in, 1)
                evac(t_q + 1, raw_q[:, 2:4, :], scale=-(HD ** -0.5))
                act.wait_ge(cmp_ps, 1)
                nc.scalar.activation(raw_kc, B[6][:, 0:NG], ACT.Copy).then_inc(cmp_raw, 1)
                act.wait_ge(clear2, 1)
                nc.scalar.activation(vcm[0:CMP], B[7][0:CMP, 0:G * HD].rearrange("p (g d) -> p g d", g=G),
                                     ACT.Copy)
                for i in range(2, 4):
                    act.wait_ge(roped, i + 1)
                    evac(t_q + i, raw_q[:, 2 * (i % 2):2 * (i % 2) + 2, :], scale=-(HD ** -0.5))
                for i in range(4):
                    evac(t_z + i, zT[:, 2 * i:2 * i + 2, :], ACT.Silu)
                high(act, T["nsa_out"] + 2)
                att2.act(act)
                out2_act(act)

            @block.vector
            def _(dve):
                step = Chain(dve, rope_step)

                def rope(r):
                    src, dst = ropes[r]
                    tc, ts = t_cos, t_sin
                    dve.wait_ge(rotated, r + 1)
                    if r:
                        dve.wait_ge(roped, r)
                    nc.vector.tensor_tensor(tc, src, bcast(C("cos_tok"), 1, 2), ALU.mult)
                    step(nc.vector.tensor_tensor(ts, B[4 + r % 2][:, :].rearrange("p (a b) -> p a b", a=2),
                                                 bcast(C("sin_tok"), 1, 2), ALU.mult))
                    nc.vector.tensor_tensor(dst, tc, ts, ALU.add).then_inc(roped, 1)

                nrm2.dve(dve)
                dve.wait_ge(p_turned, 2)
                nc.vector.tensor_copy(par[:, 2 * DC:NPAR], B[6][:, 0:NPAR - 2 * DC]).then_inc(p_placed, 1)
                dve.wait_ge(p_placed, 1)
                rope(0)
                dve.wait_ge(moved_x, 128)
                dve.wait_ge(xb_clear, 1)
                for n in range(2):
                    src = xs2[:, n].rearrange("p a b (c i k) -> p i (a b) c k", c=16, k=2)
                    for half in range(2):
                        i8 = slice(8 * half, 8 * half + 8)
                        pe_n = pc("pe_" + "kv"[n], 8 * half, 8)
                        i = nc.vector.tensor_tensor(
                            xb[:, i8, n * HD:n * HD + NG].rearrange("p i (g c) -> p i g c", g=G),
                            src[:, :, :, half:half + CMP, 0],
                            pe_n.unsqueeze(2).unsqueeze(3).broadcast_to([P, 8, G, CMP]), ALU.add)
                    i.then_inc(blocked, 1)
                dve.wait_ge(blocked, 2)
                nc.vector.tensor_copy(b_hi[:, :, :], xb).then_inc(block_high, 1)
                dve.wait_ge(block_high, 1)
                nc.vector.tensor_tensor(b_lo[:, :, :], xb, b_hi[:, :, :].bitcast(F32),
                                        ALU.subtract).then_inc(block_split, 1)
                rope(1)
                dve.wait_ge(gate_in, 1)
                for tt in range(TT):
                    i = nc.vector.tensor_scalar(gatec[:, tt, :], gate[:, tt, :], C(f"cvalid{tt}"), None, ALU.mult)
                i.then_inc(gate_out, 1)
                rope(2)
                dve.wait_ge(cmp_rot, 1)
                nc.vector.tensor_tensor(cos_kc, raw_kc, C("cos_cmp"), ALU.mult)
                nc.vector.tensor_tensor(sin_kc, B[2][:, 0:NG], C("sin_cmp"), ALU.mult).then_inc(cmp_step, 1)
                dve.wait_ge(cmp_step, 1)
                dve.wait_ge(clear2, 1)
                for e in range(2):
                    r0 = slice(e * HD, (e + 1) * HD)
                    i = nc.vector.tensor_tensor(kzc[r0, :, e, :], cos_kc[r0].rearrange("p (g c) -> p g c", g=G),
                                                sin_kc[r0].rearrange("p (g c) -> p g c", g=G), ALU.add)
                i.then_inc(cmp_k, 1)
                rope(3)
                rope(4)
                rope(5)
                dve.wait_ge(gate_out, 1)
                evacuated(dve, t_z + 3)
                att2.dve(dve)
                out2_dve(dve)

        memory.open()
        area = Area()
        n_late_columns = sum(at[n][1] for n in ("levels", "lmask"))
        late = area(n_late_columns)
        lf = area(TT, D)
        fg = area(TT, D)
        fg_area = area.same(TT * D)
        sm, sc, scx = fg_area(8, P), fg_area(2, TT, P), fg_area(2, P)
        keyt = area(TT, D)
        decay = area.same(TT * D)(2, 8, P)
        qT, gT, keyT = area(DC, S), area(DC, S), area(DC, S)
        v = area(TT, D)
        oh = h
        qd, kd = area(3, 8, P), area(3, 8, P)
        row_area = area.same(6 * 8 * P)
        b_row, e_row, lb_row, om_row = [row_area(D) for _ in range(4)]
        sq8 = fg.rearrange("p t n -> p (t n)")
        roots = area(2 * HG_H)
        t_f, t_q3, t_i, t_g = T["hgrn_f"], T["hgrn_q"], T["hgrn_i"], T["hgrn_g"]
        for t in range(t_f, t_g + 4):
            plan_tile(t)
        lb_in, lb_step, lb_exp = sem("bounds_loaded"), sem("bounds_step"), sem("bounds_exp")
        forget, clamped, logged = sem("forget_step"), sem("forget_clamped"), sem("log_forget")
        key_turned, key_placed = sem("key_turned"), sem("key_placed")
        summed, decayed = sem("exponents_summed"), sem("decays_ready")
        q_dec, k_dec = sem("q_decayed"), sem("k_decayed")
        scored, masked, scores_in = sem("hgrn_scored"), sem("hgrn_masked"), sem("hgrn_scores_ready")
        cross_in, o_ps, o_in = sem("cross_scores_ready"), sem("hgrn_output_product"), sem("hgrn_output_ready")
        sq_in, sq_ps, sq_root = sem("hgrn_squares"), sem("hgrn_squares_summed"), sem("hgrn_roots")
        o_step, o_ready = sem("hgrn_norm_step"), sem("hgrn_gated")
        o_inv, o_spread = sem("hgrn_roots_inverted"), sem("hgrn_roots_spread")
        late_in = sem("hgrn_constants_loaded")
        out3_pe, out3_dve, out3_act = project_out(T["hgrn_out"], nrm4)
        NU = 2 * HG_H
        n_high3 = steps_taken["n"]
        steps_taken["n"] += DC

        def lslot(l, tt):
            return l if l < 4 or tt else l + 1

        with nc.Block() as block:
            @block.sync
            def _(sp):
                sp.dma_start(b_row, A["hgrn_lower_bounds_2"].broadcast_to([P, D])).then_inc(lb_in, 16)
                sp.dma_start(late, cst_dram[:, ncst:ncst + n_late_columns]).then_inc(late_in, 16)
                for t in range(T["nsa_out"] + 4 + NSLOT, T["hgrn_out"] + 4 + NSLOT):
                    load(sp, t)

            @block.gpsimd
            def _(pool):
                nrm3.pool_split(pool)
                t_o = T["hgrn_out"]
                for t in range(t_f + 2, t_o + 1):
                    low(pool, nc.gpsimd, t)
                for w in range(NU):
                    hh, tt = w // 2, w % 2
                    pool.wait_ge(decayed, w + 1)
                    if w == 0:
                        pool.wait_ge(key_placed, 4)
                    if w >= 3:
                        pool.wait_ge(scored, w - 1)
                    nc.gpsimd.tensor_tensor(kd[:, w % 3], decay[:, w % 2],
                                            bcast(keyT[:, hh, tt * P:(tt + 1) * P], 1, 8), ALU.mult)\
                        .then_inc(k_dec, 1)
                for c in range(DC):
                    pool.wait_ge(high_step, n_high3 + c + 1)
                    nc.gpsimd.tensor_tensor(h_lo[:, c, :], oh[:, c, :], h_hi[:, c, :].bitcast(F32),
                                            ALU.subtract).then_inc(act_split, 1)
                for t in range(t_o + 1, t_o + 6):
                    low(pool, nc.gpsimd, t)

            @block.tensor
            def _(pe):
                for i in range(4):
                    nrm3.sums(pe, i)
                nrm3.spread(pe)
                keep_warm(12)
                for i in range(4):
                    by_token(pe, t_f + i, hsp, ready=nrm3.chunk(pe) if i == 0 else None)
                for i in range(4):
                    by_feature(pe, t_q3 + i, hsp)
                pe.wait_ge(forget, 3)
                for c in range(DC):
                    for tt in range(TT):
                        mm = nc.tensor.transpose(B[2 + c // 2][:, (c % 2) * S + tt * P:(c % 2) * S + (tt + 1) * P],
                                                 keyt[:, tt, c * P:(c + 1) * P], ident)
                    if c % 2:
                        mm.then_inc(key_turned, 1)
                for i in range(4):
                    by_token(pe, t_i + i, hsp)
                for i in range(4):
                    by_feature(pe, t_g + i, hsp)
                pe.wait_ge(logged, 1)
                pe.wait_ge(late_in, 16)
                pe.wait_ge(key_placed, 4)
                evacuated(pe, t_g + 2)
                evacuated(pe, t_g + 3)

                def exponents(w):
                    hh, tt = w // 2, w % 2
                    if w >= 2:
                        pe.wait_ge(decayed, w - 1)
                    for b in range(2):
                        c0 = b * (512 + P * tt)
                        mm = nc.tensor.matmul(B[2 * (w % 2) + b][:, :], lf[:, tt, hh * P:(hh + 1) * P],
                                              late[:, c0:c0 + 512], start=True, stop=True)
                    mm.then_inc(summed, 1)

                def scores(w):
                    hh, tt = w // 2, w % 2
                    pe.wait_ge(q_dec, w + 1)
                    pe.wait_ge(k_dec, w + 1)
                    if w >= 1:
                        pe.wait_ge(masked, w)
                    for l in range(LEVELS):
                        s_ = lslot(l, tt)
                        nc.tensor.matmul(B[4 + l // 4][:, (l % 4) * P:(l % 4 + 1) * P], kd[:, w % 3, s_, :],
                                         qd[:, w % 3, s_, :], start=True, stop=True)
                    tk = slice(tt * P, (tt + 1) * P)
                    mm = nc.tensor.matmul(B[5][:, 3 * P:4 * P], keyT[:, hh, tk], qT[:, hh, tk], start=True, stop=True)
                    if tt:
                        if hh:
                            pe.wait_ge(cross_in, hh)
                        mm = nc.tensor.matmul(B[6][:, 0:P], kd[:, (w - 1) % 3, 4, :], qd[:, w % 3, 7, :],
                                              start=True, stop=True)
                    mm.then_inc(scored, 1)

                def outputs(hh):
                    pe.wait_ge(scores_in, 2 * hh + 2)
                    pe.wait_ge(cross_in, hh + 1)
                    if hh:
                        pe.wait_ge(o_in, hh)
                    vh = [v[:, tt, hh * P:(hh + 1) * P] for tt in range(TT)]
                    nc.tensor.matmul(B[7][:, 0:P], vh[0], sc[:, hh % 2, 0, :], start=True, stop=True)
                    nc.tensor.matmul(B[7][:, P:S], vh[0], scx[:, hh % 2, :], start=True, stop=False)
                    nc.tensor.matmul(B[7][:, P:S], vh[1], sc[:, hh % 2, 1, :], start=False, stop=True)\
                        .then_inc(o_ps, 1)

                for w in range(NU + 2):
                    if w < NU:
                        exponents(w)
                    if 1 <= w <= NU:
                        scores(w - 1)
                    if w >= 3 and w % 2:
                        outputs((w - 3) // 2)
                for i in range(4):
                    pe.wait_ge(sq_in, i + 1)
                    for k in range(4 * i, 4 * i + 4):
                        mm = nc.tensor.matmul(B[2][:, k:k + 1], sq8[:, k * P:(k + 1) * P], ones[:, 0:1],
                                              start=True, stop=True)
                    mm.then_inc(sq_ps, 1)
                pe.wait_ge(o_inv, 1)
                for i in range(4):
                    spread(B[3 + i], [roots[:, k:k + 1] for k in range(4 * i, 4 * i + 4)]).then_inc(o_spread, 1)
                out3_pe(pe)

            @block.scalar
            def _(act):
                for i in range(4):
                    nrm3.square(act, i)
                nrm3.root(act)
                nrm3.act_split(act)
                high(act, t_f + 2)
                act.wait_ge(lb_step, 1)
                nc.scalar.activation(e_row, e_row, ACT.Exp).then_inc(lb_exp, 1)
                for i in range(4):
                    act.wait_ge(tile_done, t_f + i + 1)
                    nc.scalar.activation(fg[:, :, i * 256:(i + 1) * 256], bank2(t_f + i), ACT.Sigmoid)\
                        .then_inc(freed(t_f + i), 1)
                    high(act, t_f + i + 3)
                for i in range(4):
                    act.wait_ge(tile_done, t_q3 + i + 1)
                    nc.scalar.activation(qT[:, 2 * i:2 * i + 2, :], bank2(t_q3 + i), ACT.Silu)\
                        .then_inc(freed(t_q3 + i), 1)
                    high(act, t_q3 + i + 3)
                act.wait_ge(clamped, 1)
                nc.scalar.activation(lf, lf, ACT.Ln).then_inc(logged, 1)
                for i in range(4):
                    act.wait_ge(tile_done, t_i + i + 1)
                    nc.scalar.activation(v[:, :, i * 256:(i + 1) * 256], bank2(t_i + i), ACT.Copy)\
                        .then_inc(freed(t_i + i), 1)
                    high(act, t_i + i + 3)
                for i in range(4):
                    act.wait_ge(tile_done, t_g + i + 1)
                    nc.scalar.activation(gT[:, 2 * i:2 * i + 2, :], bank2(t_g + i), ACT.Silu)\
                        .then_inc(freed(t_g + i), 1)
                    if i < 3:
                        high(act, t_g + i + 3)
                for w in range(NU + 3):
                    if w < NU:
                        act.wait_ge(summed, w + 1)
                        if w >= 2:
                            act.wait_ge(q_dec, w - 1)
                            act.wait_ge(k_dec, w - 1)
                        for b in range(2):
                            i = nc.scalar.activation(decay[:, w % 2, 4 * b:4 * b + 4, :],
                                                     B[2 * (w % 2) + b][:, :].rearrange("p (l t) -> p l t", l=4),
                                                     ACT.Exp)
                        i.then_inc(decayed, 1)
                    if w >= 2 and w % 2 == 0 and w <= NU:
                        hh = w // 2 - 1
                        act.wait_ge(scored, 2 * hh + 2)
                        if hh >= 2:
                            act.wait_ge(o_ps, hh - 1)
                        nc.scalar.activation(scx[:, hh % 2, :], B[6][:, 0:P], ACT.Copy).then_inc(cross_in, 1)
                    if w == 3:
                        high(act, T["hgrn_out"] + 2)
                    if w >= 4 and w % 2 == 0:
                        hh = (w - 4) // 2
                        act.wait_ge(o_ps, hh + 1)
                        nc.scalar.activation(oh[:, hh, :], B[7][:, 0:S], ACT.Copy).then_inc(o_in, 1)
                for i in range(4):
                    act.wait_ge(o_in, 2 * i + 2)
                    nc.scalar.activation(sq8[:, i * 512:(i + 1) * 512].rearrange("p (a b) -> p a b", a=2),
                                         oh[:, 2 * i:2 * i + 2, :], ACT.Square).then_inc(sq_in, 1)
                act.wait_ge(sq_ps, 4)
                nc.scalar.activation(roots, B[2][:, 0:NU], ACT.Sqrt, scale=1.0 / P,
                                     bias=eps[:, 0:1]).then_inc(sq_root, 1)
                for i in range(4):
                    act.wait_ge(o_ready, i + 1)
                    nc.scalar.activation(h_hi[:, 2 * i:2 * i + 2, :], oh[:, 2 * i:2 * i + 2, :], ACT.Copy)\
                        .then_inc(high_step, 2)
                out3_act(act)

            @block.vector
            def _(dve):
                nrm_f.dve(dve)
                nrm3.invert(dve)
                nrm3.dve(dve)
                dve.wait_ge(lb_in, 16)
                nc.vector.tensor_tensor(e_row, b_row, b_row, ALU.subtract).then_inc(lb_step, 1)
                dve.wait_ge(lb_exp, 1)
                nc.vector.reciprocal(om_row, e_row).then_inc(lb_step, 1)
                dve.wait_ge(lb_step, 2)
                nc.vector.tensor_tensor(b_row, e_row, om_row, ALU.mult).then_inc(lb_step, 1)
                dve.wait_ge(lb_step, 3)
                nc.vector.tensor_tensor(lb_row, b_row, b_row, ALU.subtract).then_inc(lb_step, 1)
                dve.wait_ge(lb_step, 4)
                nc.vector.tensor_scalar(om_row, lb_row, -1.0, 1.0, ALU.mult, ALU.add).then_inc(lb_step, 1)
                dve.wait_ge(lb_step, 5)
                evacuated(dve, t_f + 2)
                evacuated(dve, t_f + 3)
                nc.vector.tensor_tensor(fg, fg, bcast(om_row, 1, TT), ALU.mult).then_inc(forget, 1)
                dve.wait_ge(forget, 1)
                nc.vector.tensor_tensor(fg, fg, bcast(lb_row, 1, TT), ALU.add).then_inc(forget, 1)
                dve.wait_ge(forget, 2)
                nc.vector.tensor_scalar(keyt, fg, -1.0, 1.0, ALU.mult, ALU.add).then_inc(forget, 1)
                nc.vector.tensor_scalar(lf, fg, LEAST, None, ALU.max).then_inc(clamped, 1)
                for i in range(4):
                    dve.wait_ge(key_turned, i + 1)
                    nc.vector.tensor_copy(keyT[:, 2 * i:2 * i + 2, :],
                                          B[2 + i][:, :].rearrange("p (a b) -> p a b", a=2)).then_inc(key_placed, 1)

                def decayed_queries(w):
                    hh, tt = w // 2, w % 2
                    dve.wait_ge(decayed, w + 1)
                    if w == 0:
                        evacuated(dve, t_q3 + 3)
                    if w >= 3:
                        dve.wait_ge(scored, w - 1)
                    nc.vector.tensor_tensor(qd[:, w % 3], decay[:, w % 2],
                                            bcast(qT[:, hh, tt * P:(tt + 1) * P], 1, 8), ALU.mult).then_inc(q_dec, 1)

                def mask_scores(w):
                    hh, tt = w // 2, w % 2
                    dve.wait_ge(scored, w + 1)
                    if w >= 1:
                        dve.wait_ge(scores_in, w)
                    if hh >= 2:
                        dve.wait_ge(o_ps, hh - 1)
                    for b in range(2):
                        i = nc.vector.tensor_tensor(sm[:, 4 * b:4 * b + 4, :],
                                                    B[4 + b][:, :].rearrange("p (l t) -> p l t", l=4),
                                                    late[:, 9 * P + 512 * b:9 * P + 512 * b + 512].rearrange("p (l t) -> p l t", l=4),
                                                    ALU.mult)
                    i.then_inc(masked, 1)
                    dve.wait_ge(masked, w + 1)
                    nc.vector.tensor_reduce(sc[:, hh % 2, tt, :], sm.rearrange("p l t -> p t l"), AX.X,
                                            ALU.add).then_inc(scores_in, 1)

                for w in range(NU + 1):
                    if w < NU:
                        decayed_queries(w)
                    if w >= 1:
                        mask_scores(w - 1)
                step = Chain(dve, o_step)
                dve.wait_ge(sq_root, 1)
                nc.vector.reciprocal(roots, roots).then_inc(o_inv, 1)
                for i in range(4):
                    o2 = oh[:, 2 * i:2 * i + 2, :]
                    dve.wait_ge(o_spread, i + 1)
                    step(nc.vector.scalar_tensor_tensor(out=o2, in0=o2, scalar=pc("hgrn_norm"),
                                                        in1=B[3 + i][:, :].rearrange("p (a b) -> p a b", a=2),
                                                        op0=ALU.mult, op1=ALU.mult))
                    nc.vector.tensor_tensor(o2, o2, gT[:, 2 * i:2 * i + 2, :], ALU.mult).then_inc(o_ready, 1)
                out3_dve(dve)

        ffn(0, nrm4, nrm5, T["ffn0"], T["ffn0"] + NSLOT, T["ffn0"] + 33 + NSLOT)

        memory.open(less=2 * 4 * S)
        c_hi, c_lo = [memory.float32r("lora_" + n, 4, S) for n in ("high", "low")]
        area = Area()
        pos_i = area(S).bitcast(I32)
        cosT, sinT = area(S), area(S)
        w_r = area(DC, ROPE)
        cq, ckv = area(2, S), area(2, S)
        lrs = area(2, S)
        gq = area(2)
        kr, krg, kr_sq, kr_t, kr_base = [area(S) for _ in range(5)]
        qn, qr, krh, kn = [area(ML_H, S) for _ in range(4)]
        early = area.same(ML_H * S)
        ang, turns, sin_h = early(S), early(S), early(S)
        lsq = [early(2, S) for _ in range(2)]
        v = area(TT, D)
        oT = h
        sqn, sqr, tcos, tsin = [area(2, 2, S) for _ in range(4)]
        area(10 * S)
        att_area = area.same(26 * S)
        rs2 = area(8, 4)
        t_mi, t_mq, t_mkv = T["mla_in"], T["mla_q"], T["mla_kv"]
        for t in (t_mi, t_mi + 1):
            plan_tile(t)
        use0 = turn["n"]
        uses = [(kind, p) for p in range(4) for kind in ("qn", "qr")]
        for n in range(2):
            uses += [("kn", 4 + 2 * n), ("kn", 5 + 2 * n), ("v", 2 * n), ("v", 2 * n + 1)]
        use_no = {k: use0 + n for n, k in enumerate(uses)}
        turn["n"] += len(uses)
        small5, pos_in, kr_clear = sem("mla_small_loaded"), sem("positions_loaded"), sem("mla_cleared")
        ang_step, sins, cos_ready = sem("angle_step"), sem("sines_ready"), sem("cosines_ready")
        lora_ps, lora_sum = sem("rope_key_product"), sem("lora_summed")
        lora_root, lora_step, lora_ready = sem("lora_root"), sem("lora_step"), sem("lora_ready")
        kr_in, krg_in, kr_rot, kr_ready = sem("rope_key_raw"), sem("rope_key_gained"), sem("rope_key_rotated"), sem("rope_key_ready")
        up_done, sum5 = sem("mla_up_product"), sem("mla_squares_summed")
        root5, step5, gained = sem("mla_root"), sem("mla_step"), sem("mla_gained")
        rot5, ready5 = sem("mla_rotated"), sem("mla_pair_ready")
        inverted5, spread5 = sem("mla_roots_inverted"), sem("mla_roots_spread")

        units = []
        for hh in range(ML_H):
            for qt in range(TT):
                w = (qt + 1) * P
                tk = slice(qt * P, (qt + 1) * P)
                units.append(dict(
                    group=hh, qt=qt, nh=1, w=w, nkt=qt + 1, first=(qt == 0), open=True, close=True,
                    qk=[(qn[:, hh, tk], kn[:, hh:hh + 1, 0:w]), (qr[:, hh, tk], krh[:, hh:hh + 1, 0:w])],
                    bias=[masks(qt)], v=lambda e, kt, hh=hh, v=v: v[:, kt, hh * P:(hh + 1) * P]))
        att5 = Attention(att_area, units, ML_H,
                         lambda g, ps, oT=oT: nc.vector.tensor_copy(oT[:, g, :], ps))
        out5_pe, out5_dve, out5_act = project_out(T["mla_out"], nrm6)
        TWO_PI = (6.28125, 0.0019340515136718750, float(np.float32(2 * np.pi - 6.28125 - 0.0019340515136718750)))
        ROUND = 1.5 * 2 ** 23

        with nc.Block() as block:
            @block.sync
            def _(sp):
                sp.dma_start(pos_i, A["positions_2"].broadcast_to([P, S])).then_inc(pos_in, 16)
                sp.dma_start(w_r, mw.rearrange("(c p) n -> p c n", p=P)[:, :, 2 * LORA:]).then_inc(small5, 16)
                for t in range(T["ffn0"] + 33 + NSLOT, T["mla_out"] + 4 + NSLOT):
                    load(sp, t)

            @block.gpsimd
            def _(pool):
                nrm5.pool_split(pool)
                nc.gpsimd.memset(kr, 0.0)
                nc.gpsimd.memset(qr, 0.0)
                nc.gpsimd.memset(sqr, 0.0).then_inc(kr_clear, 1)
                for t in range(t_mi + 2, T["mla_out"] + 3):
                    low(pool, nc.gpsimd, t)
                att5.split(pool, oT)
                for t in range(T["mla_out"] + 3, T["mla_out"] + 6):
                    low(pool, nc.gpsimd, t)

            @block.tensor
            def _(pe):
                def use_bank(k):
                    u = use_no[k]
                    pe.wait_ge(bank_free[u % 2], u // 2)
                    return B[u % 2]

                def up(p):
                    t = (t_mq if p < 4 else t_mkv) + (p % 4) // 2
                    width = QK if p < 4 else 256
                    if p % 2 == 0:
                        in_parts(pe, t)
                    w = [r[:, t % NSLOT, :] for r in (w_hi, w_lo)]
                    k0, kinds = (0, (("qn", 0), ("qr", NOPE))) if p < 4 else (2, (("kn", 0),))
                    for kind, c0 in kinds:
                        b = use_bank((kind, p))
                        for e in range(2):
                            c = (2 * (p % 2) + e) * width + c0
                            for k in range(2):
                                at_k = 4 * width * k + c
                                mm = product3(b[:, e * S:(e + 1) * S], [v[:, at_k:at_k + P] for v in w],
                                              [v[:, k0 + k, :] for v in (c_hi, c_lo)], k == 0, k == 1)
                        if kind == "qr" and p % 2:
                            mm.then_inc(tile_done, 1)
                        else:
                            mm.then_inc(up_done, 1)

                def up_values(n):
                    t = t_mkv + n
                    w = parts(t, "p (k e n) -> p k e n", k=2, e=4, n=256)
                    for tt in range(TT):
                        b = use_bank(("v", 2 * n + tt))
                        for k in range(2):
                            mm = product3(b[:, :], [v[:, 2 + k, tt * P:(tt + 1) * P] for v in (c_hi, c_lo)],
                                          [v[:, k, :, NOPE:] for v in w], k == 0, k == 1)
                        mm.then_inc(tile_done if tt else up_done, 1)

                def sums(p):
                    u = use_no[("qr" if p < 4 else "kn", p)]
                    pe.wait_ge(bank_free[u % 2], u // 2 + 1)
                    if p >= 2:
                        pe.wait_ge(root5, p - 1)
                    for k in range(4):
                        e, tk = k // 2, slice(k % 2 * P, (k % 2 + 1) * P)
                        o = B[2 + p % 2][:, k:k + 1]
                        nc.tensor.matmul(o, sqn[:, p % 2, e, tk], ones[:, 0:1], start=True, stop=False)
                        r = sqr[:, p % 2, e, tk] if p < 4 else kr_sq[:, tk]
                        mm = nc.tensor.matmul(o, r, ones[:, 0:1], start=False, stop=True)
                    mm.then_inc(sum5, 1)

                def spread_roots(p):
                    pe.wait_ge(inverted5, p + 1)
                    if p >= 2:
                        pe.wait_ge(gained, p - 1)
                    spread(B[6 + p % 2], [rs2[:, p, k:k + 1] for k in range(4)]).then_inc(spread5, 1)

                def rotate(p):
                    pe.wait_ge(gained, p + 1)
                    if p >= 2:
                        pe.wait_ge(ready5, p - 1)
                    nc.tensor.matmul(B[4 + p % 2][:, :], C("rot2"), qr[:, 2 * p:2 * p + 2, :], start=True,
                                     stop=True).then_inc(rot5, 1)

                keep_warm(12)
                by_feature(pe, t_mi, hsp, ready=nrm5.chunk(pe))
                by_feature(pe, t_mi + 1, hsp)
                def lora_sums(n):
                    evacuated(pe, t_mi + n)
                    for k in range(2):
                        mm = nc.tensor.matmul(B[4 + n][:, 0:S], ones, lsq[n][:, k, :], start=(k == 0), stop=(k == 1))
                    mm.then_inc(lora_sum, 1)

                lora_sums(0)
                pe.wait_ge(small5, 16)
                for c in range(DC):
                    mm = nc.tensor.matmul(B[6][0:ROPE, 0:S], w_r[:, c, :], h[:, c, :], start=(c == 0), stop=(c == DC - 1))
                mm.then_inc(lora_ps, 1)
                lora_sums(1)
                pe.wait_ge(lora_ready, 1)
                for p in range(10):
                    if p < 8:
                        up(p)
                    if p == 0:
                        pe.wait_ge(krg_in, 1)
                        nc.tensor.matmul(B[7][:, 0:S], C("rot2"), krg, start=True, stop=True).then_inc(kr_rot, 1)
                    if p == 3:
                        pe.wait_ge(lora_ready, 2)
                    if 1 <= p <= 8:
                        sums(p - 1)
                    if p >= 2:
                        spread_roots(p - 2)
                    if 3 <= p < 7:
                        rotate(p - 3)
                    if p in (5, 7):
                        up_values((p - 5) // 2)
                pe.wait_ge(ready5, 8)
                pe.wait_ge(gained, 8)
                for k in (("v", 2), ("v", 3)):
                    pe.wait_ge(bank_free[use_no[k] % 2], use_no[k] // 2 + 1)
                att5.pe(pe)
                out5_pe(pe)

            def product_done(eng, k):
                last = {("qr", 1): t_mq, ("qr", 3): t_mq + 1, ("v", 1): t_mkv, ("v", 3): t_mkv + 1}
                if k in last:
                    eng.wait_ge(tile_done, last[k] + 1)
                else:
                    eng.wait_ge(up_done, sum(1 for q in uses[:uses.index(k) + 1] if q not in last))

            @block.scalar
            def _(act):
                nrm5.act_split(act)
                high(act, t_mi + 2)
                for n, dst in enumerate((cq, ckv)):
                    act.wait_ge(tile_done, t_mi + n + 1)
                    nc.scalar.activation(dst, bank2(t_mi + n), ACT.Copy)
                    nc.scalar.activation(lsq[n], bank2(t_mi + n), ACT.Square).then_inc(freed(t_mi + n), 1)
                    high(act, t_mi + n + 3)
                def lora_roots(n):
                    act.wait_ge(lora_sum, n + 1)
                    nc.scalar.activation(lrs[:, n, :], B[4 + n][:, 0:S], ACT.Sqrt, scale=1.0 / LORA,
                                         bias=eps[:, 0:1]).then_inc(lora_root, 1)

                lora_roots(0)
                act.wait_ge(lora_ps, 1)
                act.wait_ge(kr_clear, 1)
                nc.scalar.activation(kr[0:ROPE], B[6][0:ROPE, 0:S], ACT.Copy).then_inc(kr_in, 1)
                act.wait_ge(kr_in, 1)
                nc.scalar.activation(kr_sq, kr, ACT.Square).then_inc(kr_in, 1)
                lora_roots(1)
                act.wait_ge(ang_step, 7)
                nc.scalar.activation(sinT, ang, ACT.Sin)
                nc.scalar.activation(sin_h, ang, ACT.Sin, scale=0.5).then_inc(sins, 1)

                def evac(p):
                    if p >= 2:
                        act.wait_ge(sum5, p - 1)
                    parts = (("qn", qn, P, sqn), ("qr", qr, ROPE, sqr)) if p < 4 else (("kn", kn, P, sqn),)
                    for kind, dst, m, sq in parts:
                        product_done(act, (kind, p))
                        u = use_no[(kind, p)]
                        b = B[u % 2][0:m, :].rearrange("p (a b) -> p a b", a=2)
                        pp = 2 * (p % 4)
                        nc.scalar.activation(dst[0:m, pp:pp + 2, :], b, ACT.Copy)
                        i = nc.scalar.activation(sq[0:m, p % 2], b, ACT.Square)
                        i.then_inc(bank_free[u % 2], 1)

                def root(p):
                    act.wait_ge(sum5, p + 1)
                    nc.scalar.activation(rs2[:, p, :], B[2 + p % 2][:, 0:4], ACT.Sqrt, scale=1.0 / QK,
                                         bias=eps[:, 0:1]).then_inc(root5, 1)

                for p in range(9):
                    if p < 8:
                        evac(p)
                    if p in (1, 3):
                        high(act, t_mq + p // 2 + 3)
                    if p >= 1:
                        root(p - 1)
                    if p in (5, 7):
                        n = (p - 5) // 2
                        for tt in range(TT):
                            k = ("v", 2 * n + tt)
                            product_done(act, k)
                            nc.scalar.activation(v[:, tt, n * 512:(n + 1) * 512], B[use_no[k] % 2][:, :],
                                                 ACT.Copy).then_inc(bank_free[use_no[k] % 2], 1)
                        high(act, t_mkv + n + 3)
                att5.act(act)
                out5_act(act)

            @block.vector
            def _(dve):
                nrm5.dve(dve)
                step = Chain(dve, ang_step)
                dve.wait_ge(pos_in, 16)
                step(nc.vector.tensor_copy(ang, pos_i))
                step(nc.vector.tensor_scalar(ang, ang, C("inv2"), None, ALU.mult))
                step(nc.vector.tensor_scalar(turns, ang, 1 / (2 * np.pi), ROUND, ALU.mult, ALU.add))
                step(nc.vector.tensor_scalar(turns, turns, ROUND, None, ALU.subtract))
                for part in TWO_PI:
                    step(nc.vector.scalar_tensor_tensor(out=ang, in0=turns, scalar=-part, in1=ang,
                                                        op0=ALU.mult, op1=ALU.add))
                nc.vector.tensor_scalar(gq, par[:, pcol["q_nope"]:pcol["q_nope"] + 2], -(QK ** -0.5), None, ALU.mult)
                lstep = Chain(dve, lora_step)

                def lora(n):
                    c, g = ((cq, "q_a"), (ckv, "kv_a"))[n]
                    dve.wait_ge(lora_root, n + 1)
                    lstep(nc.vector.reciprocal(lrs[:, n, :], lrs[:, n, :]))
                    for k in range(2):
                        i = nc.vector.scalar_tensor_tensor(out=c[:, k, :], in0=c[:, k, :], scalar=pc(g, k),
                                                           in1=lrs[:, n, :], op0=ALU.mult, op1=ALU.mult)
                    lstep(i)
                    part = slice(2 * n, 2 * n + 2)
                    lstep(nc.vector.tensor_copy(c_hi[:, part, :], c))
                    nc.vector.tensor_tensor(c_lo[:, part, :], c, c_hi[:, part, :].bitcast(F32),
                                            ALU.subtract).then_inc(lora_ready, 1)

                lora(0)
                dve.wait_ge(kr_in, 2)
                nc.vector.tensor_scalar(krg, kr, pc("k_rope"), None, ALU.mult).then_inc(krg_in, 1)
                lora(1)
                dve.wait_ge(sins, 1)
                nc.vector.tensor_tensor(cosT, sin_h, sin_h, ALU.mult).then_inc(cos_ready, 1)
                dve.wait_ge(cos_ready, 1)
                nc.vector.tensor_scalar(cosT, cosT, -2.0, 1.0, ALU.mult, ALU.add).then_inc(cos_ready, 1)
                dve.wait_ge(kr_rot, 1)
                dve.wait_ge(cos_ready, 2)
                nc.vector.tensor_tensor(kr_t, B[7][:, 0:S], sinT, ALU.mult)
                lstep(nc.vector.tensor_tensor(kr_base, krg, cosT, ALU.mult))
                lstep(nc.vector.tensor_tensor(kr_base, kr_base, kr_t, ALU.add))
                step = Chain(dve, step5)

                def gain(p):
                    dve.wait_ge(spread5, p + 1)
                    r = B[6 + p % 2][:, :].rearrange("p (a b) -> p a b", a=2)
                    pp = 2 * (p % 4)
                    src, g = (qn, gq[:, 0:1]) if p < 4 else (kn, pc("k_nope"))
                    o = src[:, pp:pp + 2, :]
                    if p < 4:
                        nc.vector.scalar_tensor_tensor(out=o, in0=o, scalar=g, in1=r, op0=ALU.mult, op1=ALU.mult)
                        o, g = qr[:, pp:pp + 2, :], gq[:, 1:2]
                    else:
                        nc.vector.tensor_tensor(krh[:, pp:pp + 2, :], bcast(kr_base, 1, 2), r,
                                                ALU.mult).then_inc(ready5, 1)
                    nc.vector.scalar_tensor_tensor(out=o, in0=o, scalar=g, in1=r, op0=ALU.mult,
                                                   op1=ALU.mult).then_inc(gained, 1)

                def rope(p):
                    dve.wait_ge(rot5, p + 1)
                    o = qr[:, 2 * p:2 * p + 2, :]
                    nc.vector.tensor_tensor(tcos[:, p % 2], o, bcast(cosT, 1, 2), ALU.mult)
                    step(nc.vector.tensor_tensor(tsin[:, p % 2], B[4 + p % 2][:, :].rearrange("p (a b) -> p a b", a=2),
                                                 bcast(sinT, 1, 2), ALU.mult))
                    nc.vector.tensor_tensor(o, tcos[:, p % 2], tsin[:, p % 2], ALU.add).then_inc(ready5, 1)

                for p in range(9):
                    if p < 8:
                        dve.wait_ge(root5, p + 1)
                        nc.vector.reciprocal(rs2[:, p, :], rs2[:, p, :]).then_inc(inverted5, 1)
                    if p >= 1:
                        gain(p - 1)
                    if 2 <= p <= 5:
                        rope(p - 2)
                att5.dve(dve)
                out5_dve(dve)

        ffn(1, nrm6, None, T["ffn1"], T["ffn1"] + NSLOT, NT)

        memory.open()
        area = Area()
        res = area(TT, D)
        res_turned, res_in, stored = sem("result_turned"), sem("result_placed"), sem("result_stored")
        with nc.Block() as block:
            @block.tensor
            def _(pe):
                for i in range(4):
                    tt, half = i // 2, i % 2
                    for c in range(4):
                        mm = nc.tensor.transpose(B[i][:, c * P:(c + 1) * P],
                                                 x[:, 4 * half + c, tt * P:(tt + 1) * P], ident)
                    mm.then_inc(res_turned, 1)

            @block.vector
            def _(dve):
                for i in range(4):
                    dve.wait_ge(res_turned, i + 1)
                    nc.vector.tensor_copy(res[:, i // 2, (i % 2) * 512:(i % 2 + 1) * 512], B[i][:, :])\
                        .then_inc(res_in, 1)

            @block.sync
            def _(sp):
                for tt in range(TT):
                    sp.wait_ge(res_in, 2 * tt + 2)
                    sp.dma_start(out[0, tt * P:(tt + 1) * P, :], res[:, tt, :]).then_inc(stored, 16)
                sp.wait_ge(stored, 32)


_OUTS = [((1, 256, 1024), 'float32')]
_INS = ['x', 'norm_g', 'fox_w_in', 'fox_b_f', 'fox_w_out', 'nsa_w_in', 'nsa_pe_k', 'nsa_w_ck1', 'nsa_w_ck2',
        'nsa_pe_v', 'nsa_w_cv1', 'nsa_w_cv2', 'nsa_w_out', 'final_g', 'positions_2', 'norm_mix_2', 'norm_ffn_2',
        'hgrn_w_in_2', 'hgrn_lower_bounds_2', 'hgrn_out_norm_2', 'hgrn_w_out_2', 'mla_w_in_2', 'mla_q_a_norm_2',
        'mla_w_q_up_2', 'mla_kv_a_norm_2', 'mla_w_kv_up_2', 'mla_q_norm_2', 'mla_k_norm_2', 'mla_w_out_2',
        'ffn_w_up_2', 'ffn_conv_w_2', 'ffn_conv_b_2', 'ffn_w_down_2']


def kernel(**inputs):
    import numpy as _np
    import concourse.bacc as _bacc
    from concourse import mybir as _mybir
    from concourse.bass_utils import run_bass_kernel_spmd as _run

    nc = _bacc.Bacc("TRN2", target_bir_lowering=False, num_devices=1)
    arrays, args = {}, {}
    consts, at = shape_constants()
    for name, a in [(n, inputs[n]) for n in _INS] + [("consts", consts)]:
        a = _np.ascontiguousarray(a)
        arrays[f"in_{name}_dram"] = a
        args[name] = nc.dram_tensor(f"in_{name}_dram", a.shape, _mybir.dt.from_np(a.dtype), kind="ExternalInput").ap()
    outs = []
    for i, (shape, dtype) in enumerate(_OUTS):
        dt = _mybir.dt.from_np(_np.dtype(dtype))
        outs.append(nc.dram_tensor(f"out_{i}_dram", shape, dt, kind="ExternalOutput").ap())
    build(nc, args, args["consts"], outs[0], at)
    r = _run(nc, [arrays], core_ids=[0])
    return r.results[0]["out_0_dram"]
```
